# Optimizing a Trainium2 kernel written in Bass

```python
import jax, jax.numpy as jnp
from jax import lax
import numpy as np

D_MODEL = 1024
BATCH = 1
SEQ = 256
DEPTH = 1

GRID_W = 64
CTX_LEN = 256
N_MIXERS = 2
N_A_LAYERS = (DEPTH + N_MIXERS - 1) // N_MIXERS
N_B_LAYERS = DEPTH // N_MIXERS
EPS = 1e-6
HG_EXPAND = 128
HG_HEADS = D_MODEL // HG_EXPAND
HG_DK = HG_EXPAND
HG_DV = D_MODEL // HG_HEADS
HG_F = HG_HEADS * HG_DK
CHUNK = 64
D_RNN = D_MODEL
LRU_BLOCKS = 4
LRU_BW = D_RNN // LRU_BLOCKS
LRU_CONV_W = 4
LRU_C = 8.0
D_FF = 2816
FFN_CONV_W = 3


def rmsnorm(x, g):
    xf = x.astype(jnp.float32)
    y = xf * lax.rsqrt(jnp.mean(xf * xf, axis=-1, keepdims=True) + EPS)
    return (y * g).astype(x.dtype)

def modulate(h, shift, scale):
    return h * (1.0 + scale) + shift

def dwconv(x, w, b):
    K = w.shape[0]
    right = (K - 1) // 2
    left = K - 1 - right
    T = x.shape[1]
    xp = jnp.pad(x, ((0, 0), (left, right), (0, 0)))
    return sum(w[k] * xp[:, k:k + T] for k in range(K)) + b

def _flip(t, d, axis):
    return t if d == 0 else jnp.flip(t, axis=axis)

def hgrn2_chunk_scan(q, k, v, logf, s0):
    Bn, H, T, _ = q.shape
    n = T // CHUNK
    rs = lambda t: t.reshape(Bn, H, n, CHUNK, t.shape[-1])
    q, k, v, logf = rs(q), rs(k), rs(v), rs(logf)
    b = jnp.cumsum(logf, axis=3)
    b_ref = b[:, :, :, CHUNK // 2:CHUNK // 2 + 1]
    b_last = b[:, :, :, -1:]
    qe = q * jnp.exp(b - b_ref)
    ke = k * jnp.exp(b_ref - b)
    scores = jnp.einsum('bhnik,bhnjk->bhnij', qe, ke)
    mask = jnp.tril(jnp.ones((CHUNK, CHUNK), dtype=bool))
    scores = jnp.where(mask, scores, 0.0)
    o_intra = jnp.einsum('bhnij,bhnjv->bhniv', scores, v)
    kv = jnp.einsum('bhnjk,bhnjv->bhnkv', k * jnp.exp(b_last - b), v)
    decay = jnp.exp(b_last[:, :, :, 0])

    def step(s, inp):
        dcy, u = inp
        return dcy[..., None] * s + u, s

    s_final, s_start = lax.scan(step, s0, (jnp.moveaxis(decay, 2, 0), jnp.moveaxis(kv, 2, 0)))
    s_start = jnp.moveaxis(s_start, 0, 2)
    o_inter = jnp.einsum('bhnik,bhnkv->bhniv', q * jnp.exp(b), s_start)
    o = (o_intra + o_inter).reshape(Bn, H, T, v.shape[-1])
    return o, s_final

def hgrn2_mixer(h_ctx, h_lat, w_in, lb, g_gain, w_out, need_ctx):
    def prep(h):
        Bn, T, _ = h.shape
        heads = lambda t: t.reshape(Bn, T, HG_HEADS, -1).transpose(0, 2, 1, 3)
        q, zf_fwd, zf_bwd, v, g = jnp.split(h @ w_in, 5, axis=-1)
        q = heads(jax.nn.silu(q))
        v = heads(v)
        logf, k = [], []
        for d, zf in enumerate((zf_fwd, zf_bwd)):
            f = lb[d] + (1.0 - lb[d]) * jax.nn.sigmoid(zf.astype(jnp.float32))
            logf.append(heads(jnp.log(f)))
            k.append(heads(1.0 - f))
        return q, k, v, logf, g

    qc, kc, vc, lfc, gc = prep(h_ctx)
    ql, kl, vl, lfl, gl = prep(h_lat)
    s0 = jnp.zeros((h_lat.shape[0], HG_HEADS, HG_DK, HG_DV), jnp.float32)
    o_c, o_l = 0.0, 0.0
    for d in range(2):
        oc_d, s_ctx = hgrn2_chunk_scan(_flip(qc, d, 2), _flip(kc[d], d, 2), _flip(vc, d, 2),
                                       _flip(lfc[d], d, 2), s0)
        ol_d, _ = hgrn2_chunk_scan(_flip(ql, d, 2), _flip(kl[d], d, 2), _flip(vl, d, 2),
                                   _flip(lfl[d], d, 2), s_ctx)
        o_c = o_c + _flip(oc_d, d, 2)
        o_l = o_l + _flip(ol_d, d, 2)

    def readout(o, g):
        Bn, H, T, DV = o.shape
        o = rmsnorm(o, g_gain).transpose(0, 2, 1, 3).reshape(Bn, T, H * DV)
        return (o * jax.nn.silu(g)) @ w_out

    y_c = readout(o_c, gc) if need_ctx else None
    return y_c, readout(o_l, gl)

def lru_scan(log_a, u, h0):
    a = jnp.exp(log_a)
    u = u.at[:, 0].add(a[:, 0] * h0)

    def combine(l, r):
        al, ul = l
        ar, ur = r
        return al * ar, ar * ul + ur

    _, h = lax.associative_scan(combine, (a, u), axis=1)
    return h

def rglru_mixer(h_ctx, h_lat, w_in, conv_w, conv_b, wa, ba, wx, bx, lam, w_out, need_ctx):
    Bn, T, _ = h_lat.shape
    rows = T // GRID_W
    to_cm = lambda t: t.reshape(Bn, rows, GRID_W, -1).transpose(0, 2, 1, 3).reshape(Bn, T, -1)
    from_cm = lambda t: t.reshape(Bn, GRID_W, rows, -1).transpose(0, 2, 1, 3).reshape(Bn, T, -1)

    def branch(h):
        gate, xr = jnp.split(h @ w_in, 2, axis=-1)
        return gate, dwconv(xr, conv_w, conv_b)

    def gates(xr, d):
        xb = xr.reshape(*xr.shape[:-1], LRU_BLOCKS, LRU_BW)
        r = jax.nn.sigmoid(jnp.einsum('btnk,nkj->btnj', xb, wa[d]).reshape(xr.shape) + ba[d])
        i = jax.nn.sigmoid(jnp.einsum('btnk,nkj->btnj', xb, wx[d]).reshape(xr.shape) + bx[d])
        log_a = -LRU_C * r.astype(jnp.float32) * jax.nn.softplus(-lam[d].astype(jnp.float32))
        mult = jnp.sqrt(-jnp.expm1(2.0 * log_a))
        return log_a, mult * (i * xr)

    gate_c, xc = branch(h_ctx)
    gate_l, xl = branch(to_cm(h_lat))
    h0 = jnp.zeros((Bn, D_RNN), jnp.float32)
    y_c, y_l = 0.0, 0.0
    for d in range(2):
        la_c, u_c = gates(_flip(xc, d, 1), d)
        hc = lru_scan(la_c, u_c, h0)
        la_l, u_l = gates(_flip(xl, d, 1), d)
        hl = lru_scan(la_l, u_l, hc[:, -1])
        y_c = y_c + _flip(hc, d, 1)
        y_l = y_l + _flip(hl, d, 1)
    out_l = from_cm(y_l * jax.nn.gelu(gate_l)) @ w_out
    out_c = (y_c * jax.nn.gelu(gate_c)) @ w_out if need_ctx else None
    return out_c, out_l

def conv_ffn(h, w_up, conv_w, conv_b, w_down):
    u = dwconv(h @ w_up, conv_w, conv_b)
    gate, val = jnp.split(u, 2, axis=-1)
    return (jax.nn.silu(gate) * val) @ w_down

def first_inputs(seed: int = 0) -> dict:
    key = jax.random.key(seed)
    ks = iter(jax.random.split(key, 32))
    nrm = lambda shape, s: jax.random.normal(next(ks), shape, jnp.float32) * s
    D = D_MODEL
    a0 = jax.random.uniform(next(ks), (N_B_LAYERS, 2, D_RNN), jnp.float32, 0.9, 0.999)
    sig = a0 ** (1.0 / LRU_C)
    lam = jnp.log(sig) - jnp.log1p(-sig)
    return {
        "x": nrm((BATCH, SEQ, D), 1.0),
        "c": nrm((BATCH, D), 1.0),
        "ctx": nrm((BATCH, CTX_LEN, D), 1.0),
        "c_ctx": nrm((D,), 1.0),
        "w_ada": nrm((DEPTH, D, 6 * D), D ** -0.5),
        "b_ada": nrm((DEPTH, 6 * D), 0.02),
        "norm_g": 1.0 + nrm((DEPTH, 2, D), 0.02),
        "hg_w_in": nrm((N_A_LAYERS, D, 5 * D), D ** -0.5),
        "hg_lb_logits": nrm((N_A_LAYERS + 1, 2, HG_F), 0.1),
        "hg_gnorm": 1.0 + nrm((N_A_LAYERS, HG_DV), 0.02),
        "hg_w_out": nrm((N_A_LAYERS, D, D), D ** -0.5),
        "lru_w_in": nrm((N_B_LAYERS, D, 2 * D_RNN), D ** -0.5),
        "lru_conv_w": nrm((N_B_LAYERS, LRU_CONV_W, D_RNN), LRU_CONV_W ** -0.5),
        "lru_conv_b": nrm((N_B_LAYERS, D_RNN), 0.02),
        "lru_wa": nrm((N_B_LAYERS, 2, LRU_BLOCKS, LRU_BW, LRU_BW), LRU_BW ** -0.5),
        "lru_ba": nrm((N_B_LAYERS, 2, D_RNN), 0.02),
        "lru_wx": nrm((N_B_LAYERS, 2, LRU_BLOCKS, LRU_BW, LRU_BW), LRU_BW ** -0.5),
        "lru_bx": nrm((N_B_LAYERS, 2, D_RNN), 0.02),
        "lru_lambda": lam,
        "lru_w_out": nrm((N_B_LAYERS, D_RNN, D), D_RNN ** -0.5),
        "ffn_w_up": nrm((DEPTH, D, 2 * D_FF), D ** -0.5),
        "ffn_conv_w": nrm((DEPTH, FFN_CONV_W, 2 * D_FF), FFN_CONV_W ** -0.5),
        "ffn_conv_b": nrm((DEPTH, 2 * D_FF), 0.02),
        "ffn_w_down": nrm((DEPTH, D_FF, D), D_FF ** -0.5),
        "final_g": 1.0 + nrm((D,), 0.02),
    }

def first_block(x, c, ctx, c_ctx, w_ada, b_ada, norm_g, hg_w_in, hg_lb_logits, hg_gnorm, hg_w_out,
              lru_w_in, lru_conv_w, lru_conv_b, lru_wa, lru_ba, lru_wx, lru_bx, lru_lambda, lru_w_out,
              ffn_w_up, ffn_conv_w, ffn_conv_b, ffn_w_down, final_g):
    lower_bounds = jnp.cumsum(jax.nn.softmax(hg_lb_logits.astype(jnp.float32), axis=0), axis=0)
    lat, cx = x, ctx
    sc_lat, sc_ctx = jax.nn.silu(c), jax.nn.silu(c_ctx)
    for l in range(DEPTH):
        last = l == DEPTH - 1
        m_l = (sc_lat @ w_ada[l] + b_ada[l])[:, None, :]
        m_c = sc_ctx @ w_ada[l] + b_ada[l]
        sh1, sc1, g1, sh2, sc2, g2 = jnp.split(m_l, 6, axis=-1)
        csh1, csc1, cg1, csh2, csc2, cg2 = jnp.split(m_c, 6, axis=-1)
        hl = modulate(rmsnorm(lat, norm_g[l, 0]), sh1, sc1)
        hc = modulate(rmsnorm(cx, norm_g[l, 0]), csh1, csc1)
        j = l // N_MIXERS
        if l % N_MIXERS == 0:
            yc, yl = hgrn2_mixer(hc, hl, hg_w_in[j], lower_bounds[j], hg_gnorm[j], hg_w_out[j],
                                 not last)
        else:
            yc, yl = rglru_mixer(hc, hl, lru_w_in[j], lru_conv_w[j], lru_conv_b[j], lru_wa[j],
                                 lru_ba[j], lru_wx[j], lru_bx[j], lru_lambda[j], lru_w_out[j],
                                 not last)
        lat = lat + g1 * yl
        hl = modulate(rmsnorm(lat, norm_g[l, 1]), sh2, sc2)
        lat = lat + g2 * conv_ffn(hl, ffn_w_up[l], ffn_conv_w[l], ffn_conv_b[l], ffn_w_down[l])
        if not last:
            cx = cx + cg1 * yc
            hc = modulate(rmsnorm(cx, norm_g[l, 1]), csh2, csc2)
            cx = cx + cg2 * conv_ffn(hc, ffn_w_up[l], ffn_conv_w[l], ffn_conv_b[l], ffn_w_down[l])
    return rmsnorm(lat, final_g)


RET_HEADS = 4
RET_DK = 128
RET_DV = 256
RET_CHUNK = 128
SWA_HEADS = 8
SWA_KV_HEADS = 2
SWA_DH = 64
WINDOW = 128
D_FF_2 = 4 * D_MODEL

RET_QK = RET_HEADS * RET_DK
RET_V = RET_HEADS * RET_DV
SWA_Q = SWA_HEADS * SWA_DH
SWA_KV = SWA_KV_HEADS * SWA_DH
IN_SPLITS = (RET_QK, RET_QK, RET_V, RET_V, SWA_Q, SWA_KV, SWA_KV, D_MODEL, D_MODEL)
D_IN = sum(IN_SPLITS)
SPLIT_IDX = tuple(int(i) for i in np.cumsum(IN_SPLITS)[:-1])


def rmsnorm_2(x, g):
    xf = x.astype(jnp.float32)
    y = xf * lax.rsqrt(jnp.mean(xf * xf, axis=-1, keepdims=True) + EPS)
    return (y * g.astype(jnp.float32)).astype(x.dtype)

def retention_chunkwise(q, k, v):
    B, T, H, dk = q.shape
    dv = v.shape[-1]
    C = RET_CHUNK
    N = T // C
    f32 = jnp.float32
    log_gamma = jnp.log(1.0 - jnp.exp2(-5.0 - jnp.arange(H, dtype=f32)))
    q = q.astype(f32).reshape(B, N, C, H, dk)
    k = k.astype(f32).reshape(B, N, C, H, dk) * (dk ** -0.5)
    v = v.astype(f32).reshape(B, N, C, H, dv)
    pos = jnp.arange(C, dtype=f32)
    diff = pos[:, None] - pos[None, :]
    causal = diff >= 0
    decay = jnp.where(causal[None], jnp.exp(log_gamma[:, None, None] * jnp.where(causal, diff, 0.0)[None]), 0.0)
    qk = jnp.einsum('bnihd,bnjhd->bnhij', q, k) * decay[None, None]
    o_inner = jnp.einsum('bnhij,bnjhe->bnihe', qk, v)
    k_dec = k * jnp.exp(log_gamma[None, :] * (C - 1.0 - pos)[:, None])[None, None, :, :, None]
    kv = jnp.einsum('bnjhd,bnjhe->nbhde', k_dec, v)
    chunk_decay = jnp.exp(log_gamma * C)[None, :, None, None]

    def step(s, kv_n):
        return chunk_decay * s + kv_n, s

    _, s_prev = lax.scan(step, jnp.zeros((B, H, dk, dv), f32), kv)
    q_dec = q * jnp.exp(log_gamma[None, :] * (pos + 1.0)[:, None])[None, None, :, :, None]
    o_cross = jnp.einsum('bnihd,nbhde->bnihe', q_dec, s_prev)
    o = (o_inner + o_cross).reshape(B, T, H, dv)
    mu = jnp.mean(o, axis=-1, keepdims=True)
    var = jnp.mean(jnp.square(o - mu), axis=-1, keepdims=True)
    return (o - mu) * lax.rsqrt(var + EPS)

def swa_gqa_sinks(q, k, v, sinks):
    B, T, Hq, dh = q.shape
    G = k.shape[2]
    R = Hq // G
    W = WINDOW
    N = T // W
    f32 = jnp.float32
    qb = q.reshape(B, N, W, G, R, dh)
    kb = k.reshape(B, N, W, G, dh)
    vb = v.reshape(B, N, W, G, dh)
    pad = ((0, 0), (1, 0), (0, 0), (0, 0), (0, 0))
    kk = jnp.concatenate([jnp.pad(kb, pad)[:, :-1], kb], axis=2)
    vv = jnp.concatenate([jnp.pad(vb, pad)[:, :-1], vb], axis=2)
    s = jnp.einsum('bnigrd,bnjgd->bgrnij', qb, kk).astype(f32) * (dh ** -0.5)
    qpos = jnp.arange(W)[:, None] + W
    kpos = jnp.arange(2 * W)[None, :]
    dist = qpos - kpos
    valid = (dist >= 0) & (dist < W)
    blk_valid = valid[None] & ((jnp.arange(N)[:, None, None] > 0) | (kpos >= W)[None])
    slopes = jnp.exp2(-8.0 / Hq * jnp.arange(1, Hq + 1, dtype=f32)).reshape(G, R)
    s = s - slopes[None, :, :, None, None, None] * dist.astype(f32)[None, None, None, None]
    s = jnp.where(blk_valid[None, None, None], s, -jnp.inf)
    sink = sinks.astype(f32).reshape(G, R)[None, :, :, None, None, None]
    m = jnp.maximum(jnp.max(s, axis=-1, keepdims=True), sink)
    p = jnp.exp(s - m)
    p = p / (jnp.sum(p, axis=-1, keepdims=True) + jnp.exp(sink - m))
    out = jnp.einsum('bgrnij,bnjgd->bnigrd', p, vv.astype(f32))
    return out.reshape(B, T, Hq * dh)

def second_inputs(seed: int = 0) -> dict:
    key = jax.random.key(seed)
    ks = jax.random.split(key, 13)
    f32 = jnp.float32

    def dense(k, fan_in, fan_out):
        return jax.random.normal(k, (DEPTH, fan_in, fan_out), f32) * (fan_in ** -0.5)

    def gain(k):
        return 1.0 + 0.02 * jax.random.normal(k, (DEPTH, D_MODEL), f32)

    return {
        "x": jax.random.normal(ks[0], (BATCH, SEQ, D_MODEL), f32),
        "pre_mix_norm": gain(ks[1]),
        "w_in": dense(ks[2], D_MODEL, D_IN),
        "w_ret_out": dense(ks[3], RET_V, D_MODEL),
        "w_swa_out": dense(ks[4], SWA_Q, D_MODEL),
        "w_out": dense(ks[5], D_MODEL, D_MODEL),
        "sinks": 0.5 * jax.random.normal(ks[6], (DEPTH, SWA_HEADS), f32),
        "post_mix_norm": gain(ks[7]),
        "pre_mlp_norm": gain(ks[8]),
        "w_up": dense(ks[9], D_MODEL, D_FF_2),
        "w_down": dense(ks[10], D_FF_2, D_MODEL),
        "post_mlp_norm": gain(ks[11]),
    }

def second_block(x, pre_mix_norm, w_in, w_ret_out, w_swa_out, w_out, sinks, post_mix_norm, pre_mlp_norm, w_up, w_down, post_mlp_norm):
    B, T, _ = x.shape
    dt = x.dtype
    for l in range(DEPTH):
        h = rmsnorm_2(x, pre_mix_norm[l])
        proj = h @ w_in[l]
        q_r, k_r, v_r, g_r, q_s, k_s, v_s, gate_r, gate_s = jnp.split(proj, SPLIT_IDX, axis=-1)
        ret = retention_chunkwise(q_r.reshape(B, T, RET_HEADS, RET_DK),
                                  k_r.reshape(B, T, RET_HEADS, RET_DK),
                                  v_r.reshape(B, T, RET_HEADS, RET_DV)).reshape(B, T, RET_V)
        ret = (jax.nn.silu(g_r.astype(jnp.float32)) * ret).astype(dt)
        y_r = ret @ w_ret_out[l]
        swa = swa_gqa_sinks(q_s.reshape(B, T, SWA_HEADS, SWA_DH),
                            k_s.reshape(B, T, SWA_KV_HEADS, SWA_DH),
                            v_s.reshape(B, T, SWA_KV_HEADS, SWA_DH),
                            sinks[l]).astype(dt)
        y_s = swa @ w_swa_out[l]
        merged = jax.nn.sigmoid(gate_r) * y_r + jax.nn.sigmoid(gate_s) * y_s
        x = x + rmsnorm_2(merged @ w_out[l], post_mix_norm[l])
        h = rmsnorm_2(x, pre_mlp_norm[l])
        u = jnp.square(jax.nn.relu(h @ w_up[l]))
        x = x + rmsnorm_2(u @ w_down[l], post_mlp_norm[l])
    return x


def setup_inputs(seed=0):
    out = dict(first_inputs(seed))
    for name, value in second_inputs(seed + 1).items():
        if name != "x":
            out[name + "_2"] = value
    return out


def reference(
    x, c, ctx, c_ctx, w_ada, b_ada, norm_g, hg_w_in, hg_lb_logits, hg_gnorm, hg_w_out, lru_w_in,
    lru_conv_w, lru_conv_b, lru_wa, lru_ba, lru_wx, lru_bx, lru_lambda, lru_w_out, ffn_w_up,
    ffn_conv_w, ffn_conv_b, ffn_w_down, final_g, pre_mix_norm_2, w_in_2, w_ret_out_2,
    w_swa_out_2, w_out_2, sinks_2, post_mix_norm_2, pre_mlp_norm_2, w_up_2, w_down_2,
    post_mlp_norm_2,
):
    x = first_block(
        x, c, ctx, c_ctx, w_ada, b_ada, norm_g, hg_w_in, hg_lb_logits, hg_gnorm, hg_w_out,
        lru_w_in, lru_conv_w, lru_conv_b, lru_wa, lru_ba, lru_wx, lru_bx, lru_lambda, lru_w_out,
        ffn_w_up, ffn_conv_w, ffn_conv_b, ffn_w_down, final_g,
    )
    return second_block(
        x, pre_mix_norm_2, w_in_2, w_ret_out_2, w_swa_out_2, w_out_2, sinks_2, post_mix_norm_2,
        pre_mlp_norm_2, w_up_2, w_down_2, post_mlp_norm_2,
    )


_drawn_inputs = setup_inputs


def setup_inputs(seed=0):
    import zlib

    import numpy as np

    out = dict(_drawn_inputs(seed))
    spreads = {}
    factors = {'hg_lb_logits': 8.0,
     'hg_gnorm': 2.758,
     'ffn_conv_b': 2.94,
     'sinks_2': 3.299,
     'post_mix_norm_2': 3.718,
     'pre_mlp_norm_2': 12.264,
     'post_mlp_norm_2': 15.99}
    for name, (base, spread) in spreads.items():
        noise = np.random.default_rng([zlib.crc32(name.encode()), seed]).standard_normal(out[name].shape)
        drawn = base * np.exp(spread * noise) if base else spread * noise
        out[name] = __import__('jax').numpy.asarray(drawn.astype(out[name].dtype))
    for name, factor in factors.items():
        out[name] = (out[name] * factor).astype(out[name].dtype)
    return out
```

```python
from contextlib import ExitStack

import numpy as np

import concourse.bass as bass
from concourse import mybir

F32 = mybir.dt.float32
F32R = mybir.dt.float32r
I32 = mybir.dt.int32
ACT = mybir.ActivationFunctionType
ALU = mybir.AluOpType
AX = mybir.AxisListType.X

P = 128
D = 1024
KT = D // P
T = 256
TC = 2 * T
EPS = 1e-6
RING = 4
AHEAD = 2
ADA = 6 * KT
ADA_FIRST = 2 * KT
HEADS = 8
CH = 64
HALF = CH // 2
NCH = T // CH
D_FF = 2816
JF = D_FF // P
R_HEADS = 4
R_DV = 256
S_HEADS = 8
S_DH = 64
D_FF2 = 4096
JM = D_FF2 // P

N_V = 0
N_HEAD = N_V + HEADS
N_HOUT = N_HEAD + 4 * HEADS
N_FFN = N_HOUT + KT
N_IN2 = N_FFN + 3 * JF
TILES_IN2 = 46
N_SOUT = N_IN2 + TILES_IN2
N_ROUT = N_SOUT + 4
N_MOUT = N_ROUT + KT
N_MLP = N_MOUT + KT
N_ALL = N_MLP + 2 * JM

T_QS, T_KS, T_VS, T_QR, T_KR, T_VR, T_GR, T_GS, T_GT = 0, 4, 5, 6, 10, 14, 22, 30, 38

PAR = {}
_at = 0
for _name, _n in (("norm1", 8), ("norm2", 8), ("b_ada", 48), ("lb0", 16), ("lb1", 16), ("gnorm", 1),
                  ("conv_w", 3 * 2 * JF), ("conv_b", 2 * JF), ("final", 8), ("pre_mix", 8),
                  ("post_mix", 8), ("pre_mlp", 8), ("post_mlp", 8)):
    PAR[_name] = _at
    _at += _n
N_PAR = _at

CON = {"ident": 0, "ones": P, "scan": 2 * P, "decay": 2 * P + 2 * TC, "dist": 2 * P + 2 * TC + 3 * P * R_HEADS}
N_CON = CON["dist"] + 3 * P
ARENA = 14080
FAR = 1e30


def constants():
    c = np.zeros((P, N_CON), np.float32)
    c[:, 0:P] = np.eye(P)
    c[:, P:2 * P] = 1.0
    scan = np.ones(TC, np.float32)
    scan[0:T:CH] = 0.0
    scan[T] = 0.0
    c[:, CON["scan"]:CON["scan"] + TC] = scan
    c[:, CON["scan"] + TC:CON["scan"] + 2 * TC] = np.roll(scan, T)
    j = np.arange(P)[:, None]
    i = np.arange(T)[None, :]
    for h in range(R_HEADS):
        lg = np.log(np.float32(1.0) - np.exp2(np.float32(-5.0 - h)))
        d0 = np.where(i >= j, np.exp(lg * np.maximum(i - j, 0)), 0.0)
        at = CON["decay"] + 3 * P * h
        c[:, at:at + T] = d0 * P ** -0.5
        c[:, at + T:at + 3 * P] = d0[:, :P] * P ** -0.5
    q = np.arange(P)[:, None]
    k = np.arange(P)[None, :]
    own = np.where(k <= q, q - k, FAR)
    prev = np.where(k > q, q + P - k, FAR)
    c[:, CON["dist"]:] = np.concatenate([own, prev, own], axis=1)
    j, i = np.arange(CH)[:, None], np.arange(CH)[None, :]
    m = np.zeros((2, CH, 2, 2, CH), np.int32)
    m[:, :, 0] = (j <= i).astype(np.int32)[None, :, None, :]
    m[:, :, 1] = (j >= i).astype(np.int32)[None, :, None, :]
    return c, m.reshape(P, 4 * CH)


HOUT_BANKS = (0, 1, 2, 4)
LOW_BANKS = (0, 1, 2, 3)
HIGH_BANKS = (4, 5, 6, 7)
FFN_PEEL = 6
MLP_PEEL = 4
RET_FIRST = T_GS + 1


def ffn_first(j):
    return N_FFN + (2 * j if j < 2 else 3 * j - 2)


def mlp_first(j):
    return N_MLP + (j if j < 2 else 2 * j - 2)


def v_index(t):
    return 0 if t == T_VS else t - T_VR + 1 if T_VR <= t < T_GR else None


class Chunk:

    def __init__(self, base, m=0, i=0, per=0):
        assert per % RING == 0
        self.n = i * per + (base + m)
        self.slot = (base + m) % RING
        self.round = i * (per // RING) + (base + m) // RING
        self.least = base + m


def build(nc, tok_in, cc_in, ada_in, stream_in, par_in, con_in, msk_in, sink_in, out):
    ctx = ExitStack()
    with ctx:
        def sb(name, cols, dt=F32):
            return ctx.enter_context(nc.sbuf_tensor(name, [P, cols], dt))

        sems = {}

        def S(name):
            if name not in sems:
                sems[name] = ctx.enter_context(nc.semaphore(name))
            return sems[name]

        raw = [sb(f"raw{i}", D) for i in range(RING)]
        w_hi = [sb(f"w_hi{i}", D, F32R) for i in range(RING)]
        w_lo = [sb(f"w_lo{i}", D, F32R) for i in range(RING)]
        con = sb("con", N_CON)
        msk = sb("msk", 4 * CH, I32)
        par = sb("par", N_PAR)
        sink = sb("sink", S_HEADS)
        cc = sb("cc", 2 * KT)
        xres = sb("xres", KT * T)
        tok = sb("tok", KT * TC)
        wide = sb("wide", KT * TC)
        h_hi = sb("h_hi", KT * TC, F32R)
        h_lo = sb("h_lo", KT * TC, F32R)
        y_hi = sb("y_hi", KT * T, F32R)
        y_lo = sb("y_lo", KT * T, F32R)
        small = sb("small", 512)
        arena = sb("arena", ARENA)
        psum = [ctx.enter_context(nc.psum_tensor(f"bank{i}", [P, 512], F32)) for i in range(8)]

        ident = con[:, 0:P]
        ones = con[:, P:2 * P]
        scan_mask = [con[:, CON["scan"] + d * TC:CON["scan"] + (d + 1) * TC] for d in range(2)]
        dist = con[:, CON["dist"]:CON["dist"] + 3 * P]

        used = [0]

        def part(cols):
            used[0] += cols
            assert used[0] <= ARENA
            return arena[:, used[0] - cols:used[0]]

        def p1(name, k=0, n=1):
            return par[:, bass.ds(k + PAR[name], n)]

        used_small = [0]

        def tiny(cols):
            used_small[0] += cols
            assert used_small[0] <= 512
            return small[:, used_small[0] - cols:used_small[0]]

        cs = tiny(2 * KT)
        cs_e = tiny(2 * KT)
        lb = tiny(16)
        lb_om = tiny(16)
        lb_m = tiny(16)
        lb_d = tiny(32)
        mod = tiny(ADA)
        mod_c = tiny(ADA_FIRST)
        gain_l = tiny(KT)
        gain_c = tiny(KT)
        gain_2 = tiny(KT)
        sink_neg = tiny(S_HEADS)
        s_max = [tiny(2) for _ in range(2)]
        s_neg = [tiny(2) for _ in range(2)]
        s_sum = [tiny(2) for _ in range(2)]
        s_sink = [tiny(2) for _ in range(2)]
        s_den = [tiny(2) for _ in range(2)]
        v_mean = tiny(8)

        rstd = part(TC)
        f_buf = part(2 * TC)
        b_buf = part(2 * TC)
        k_buf = part(2 * TC)
        q_e = [part(2 * T) for _ in range(2)]
        q_d = [part(2 * T) for _ in range(2)]
        k_e = [part(2 * T) for _ in range(2)]
        k_d = [part(2 * TC) for _ in range(2)]
        qg = [part(2 * T) for _ in range(2)]
        k_dT = part(8 * P)
        state = part(8 * P)
        sc_T = part(8 * CH)
        v_cur = part(4 * P)
        o_sq = part(T)
        o_rs = part(T)
        o_n = part(T)
        y_f = part(T)
        used[0] = TC
        conv = [[part(T) for _ in range(2)] for _ in range(2)]
        f_silu = [part(T) for _ in range(2)]
        u_f = [part(T) for _ in range(2)]
        m_relu = [part(T) for _ in range(2)]
        used[0] = TC
        s_q = part(4 * T)
        s_k = part(T)
        s_v = part(T)
        r_q = part(4 * T)
        r_k = part(4 * T)
        r_v = part(8 * T)
        gate_r = part(8 * T)
        s_b = [part(3 * P) for _ in range(2)]
        s_p = [part(3 * P) for _ in range(2)]
        s_pT = [part(3 * P) for _ in range(2)]
        swa = part(4 * T)
        r_sc = [part(3 * P) for _ in range(2)]
        r_t = part(2 * T)
        r_sq = part(2 * T)
        r_rs = part(T)
        v_tmp = [part(T) for _ in range(2)]
        silu_g = tok[:, 0:KT * T]
        gate_s = tok[:, KT * T:2 * KT * T]

        def in2_dst(t):
            for first, n, dst in ((T_QS, 4, s_q), (T_KS, 1, s_k), (T_QR, 4, r_q), (T_KR, 4, r_k)):
                if first <= t < first + n:
                    return dst[:, (t - first) * T:(t - first + 1) * T]
            return None

        def gate_dst(t):
            dst, k = (silu_g, t - T_GR) if t < T_GS else (gate_s, t - T_GS) if t < T_GT else (gate_r, t - T_GT)
            return dst[:, k * T:(k + 1) * T]

        d1 = wide[:, 0:2 * T]
        qg_e = wide[:, 3072:3584]
        e_qe = wide[:, 512:1024]
        e_ke = wide[:, 1024:1536]
        e_qd = wide[:, 1536:2048]
        e_kd = wide[:, 2048:3072]
        v_T = [wide[:, 3072:3584], wide[:, 3584:4096]]

        def kv_at(d, s):
            c = s - 1 if d == 0 else NCH - s
            col = 0 if s == 0 else {(0, 1): 1, (0, 3): 2, (1, 2): 3, (0, 2): 1, (1, 1): 2, (1, 3): 3}[d, s]
            return psum[6 + (d if s == 0 else c % 2)][:, col * P:(col + 1) * P]

        v_all = tok

        def hi(act, c):
            if c.least >= N_ALL:
                return
            act.wait_ge(S(f"loaded{c.slot}"), c.round * 16 + 16 * (ADA // RING + 1))
            if c.least >= RING:
                act.wait_ge(S("multiplied"), c.n - (RING - 1))
            act.activation(w_hi[c.slot][:, :], raw[c.slot][:, :], ACT.Copy).then_inc(S("split_hi"), 1)

        def lo(dve, c):
            if c.least >= N_ALL:
                return
            dve.wait_ge(S("split_hi"), c.n + 1)
            dve.tensor_tensor(w_lo[c.slot][:, :], raw[c.slot][:, :], w_hi[c.slot][:, :].bitcast(F32),
                              ALU.subtract).then_inc(S("split_lo"), 1)

        def three(pe, dst, w, cols, a_hi, a_lo, start, stop):
            hi_w, lo_w = w_hi[w][:, cols], w_lo[w][:, cols]
            pe.matmul(dst, hi_w, a_hi, start=start, stop=False, skip_group_check=True)
            pe.matmul(dst, hi_w, a_lo, start=False, stop=False, skip_group_check=True)
            return pe.matmul(dst, lo_w, a_hi, start=False, stop=stop, skip_group_check=True)

        def column_tile(pe, c, dst, width, n_tok):
            pe.wait_ge(S("split_lo"), c.n + 1)
            for k in range(KT):
                last = three(pe, dst, c.slot, slice(k * P, k * P + P), h_hi[:, k * width:k * width + n_tok],
                             h_lo[:, k * width:k * width + n_tok], k == 0, k == KT - 1)
            last.then_inc(S("multiplied"), 1)

        def row_tile(pe, c, banks, a_hi, a_lo, first, stop):
            pe.wait_ge(S("split_lo"), c.n + 1)
            for m in range(KT):
                last = three(pe, psum[banks[m // 2]][:, (m % 2) * T:(m % 2) * T + T], c.slot,
                             slice(m * P, m * P + P), a_hi, a_lo, first and m % 2 == 0, stop)
            last.then_inc(S("multiplied"), 1)

        def by_tile(x, n=KT):
            return x.rearrange("p (k t) -> p k t", k=n)

        def over_tiles(x, n=KT):
            return x.rearrange("p (o t) -> p o t", o=1).broadcast_to([P, n, x.shape[1]])

        def norm_sum(pe, k, bank=7):
            pe.wait_ge(S("norm_squares"), k + 1)
            for m in range(KT):
                last = pe.matmul(psum[bank][:, 0:T], ones, wide[:, m * T:m * T + T], start=m == 0, stop=m == KT - 1)
            last.then_inc(S("norm_summed"), 1)

        def norm_mean(dve, k, bank=7):
            dve.wait_ge(S("norm_summed"), k + 1)
            dve.tensor_scalar(rstd[:, 0:T], psum[bank][:, 0:T], 1.0 / D, EPS, ALU.mult, ALU.add).then_inc(S("norm_mean"), 1)

        def norm_rstd(act, k):
            act.wait_ge(S("norm_mean"), k + 1)
            act.activation(rstd[:, 0:T], rstd[:, 0:T], ACT.Ln).then_inc(S("norm_log"), 1)
            act.wait_ge(S("norm_log"), k + 1)
            act.activation(rstd[:, 0:T], rstd[:, 0:T], ACT.Exp, scale=-0.5).then_inc(S("norm_rstd"), 1)

        def square_residual(act, k, updates):
            act.wait_ge(S("residual"), updates)
            act.activation(wide[:, 0:KT * T], xres[:, :], ACT.Square).then_inc(S("norm_squares"), 1)

        def square_banks(act, n_done, banks):
            act.wait_ge(S("multiplied"), n_done)
            for b in range(4):
                last = act.activation(wide[:, b * 512:b * 512 + 512], psum[banks[b]][:, :], ACT.Square)
            last.then_inc(S("norm_squares"), 1)

        normed = wide[:, KT * T:2 * KT * T]

        def scale_residual(dve, k, gain, dst):
            dve.wait_ge(S("norm_rstd"), k + 1)
            for m in range(KT):
                last = dve.scalar_tensor_tensor(dst[:, m * T:m * T + T], xres[:, m * T:m * T + T], gain(m),
                                                rstd[:, 0:T], ALU.mult, ALU.mult)
            return last

        def split_h_hi(act, q):
            act.wait_ge(S("h_full"), q)
            act.activation(h_hi[:, 0:KT * T], normed, ACT.Copy).then_inc(S("h_hi"), 1)

        def split_h_lo(dve, q):
            dve.wait_ge(S("h_hi"), q + 1)
            dve.tensor_tensor(h_lo[:, 0:KT * T], normed, h_hi[:, 0:KT * T].bitcast(F32),
                              ALU.subtract).then_inc(S("h_lo"), 1)

        def add_product(dve, gain, n_done, banks):
            dve.wait_ge(S("multiplied"), n_done)
            for m in range(KT):
                last = dve.scalar_tensor_tensor(xres[:, m * T:m * T + T], psum[banks[m // 2]][:, (m % 2) * T:(m % 2) * T + T],
                                                gain(m), xres[:, m * T:m * T + T], ALU.mult, ALU.add)
            last.then_inc(S("residual"), 1)

        def add_normed_product(dve, k, gain, count, banks):
            dve.wait_ge(S("norm_rstd"), k + 1)
            for m in range(KT):
                last = dve.scalar_tensor_tensor(normed[:, m * T:m * T + T], psum[banks[m // 2]][:, (m % 2) * T:(m % 2) * T + T],
                                                gain(m), rstd[:, 0:T], ALU.mult, ALU.mult)
            last.then_inc(S("product_normed"), 1)
            dve.wait_ge(S("product_normed"), count)
            dve.tensor_tensor(xres[:, :], xres[:, :], normed, ALU.add).then_inc(S("residual"), 1)

        block = ctx.enter_context(nc.Block())

        @block.sync
        def _(sp):
            def load(src, row, slot):
                sp.dma_start(raw[slot][:, :], src[bass.ds(row, P), :]).then_inc(S(f"loaded{slot}"), 16)

            for a in range(RING):
                load(ada_in, a * P, a)
            with sp.Fori(1, ADA // RING) as i:
                for u in range(RING):
                    sp.wait_ge(S("ada_done"), i * RING + (u + 1 - RING))
                    load(ada_in, i * (RING * P) + u * P, u)
            for n in range(RING):
                sp.wait_ge(S("ada_done"), ADA - RING + 1 + n)
                load(stream_in, n * P, n)
            with sp.Fori(1, N_ALL // RING) as i:
                for u in range(RING):
                    sp.wait_ge(S("split_lo"), i * RING + (u + 1 - RING))
                    load(stream_in, i * (RING * P) + u * P, u)
            sp.wait_ge(S("residual"), 5)
            sp.dma_start(out, xres[:, :]).then_inc(S("stored"), 16)
            sp.wait_ge(S("stored"), 16)

        @block.scalar
        def _(act):
            act.dma_start(cc[:, :], cc_in).then_inc(S("small_in"), 16)
            act.dma_start(par[:, :], par_in).then_inc(S("small_in"), 16)
            act.dma_start(con[:, :], con_in).then_inc(S("con_in"), 16)
            act.dma_start(tok[:, :], tok_in).then_inc(S("tok_in"), 16)
            act.dma_start(by_tile(xres[:, :]), by_tile(tok_in)[:, :, 0:T]).then_inc(S("xres_in"), 16)
            act.dma_start(msk[:, :], msk_in).then_inc(S("late_in"), 16)
            act.dma_start(sink[:, :], sink_in.partition_broadcast(P)).then_inc(S("late_in"), 16)

            act.wait_ge(S("small_in"), 32)
            act.activation(cs_e, cc[:, :], ACT.Exp, scale=-1.0).then_inc(S("cs_exp"), 1)
            act.wait_ge(S("lb_diff"), 1)
            act.activation(lb_d, lb_d, ACT.Exp).then_inc(S("lb_exp"), 1)
            act.wait_ge(S("tok_in"), 16)
            act.activation(wide[:, :], tok[:, :], ACT.Square).then_inc(S("tok_squares"), 1)
            act.wait_ge(S("tok_mean"), 1)
            act.activation(rstd, rstd, ACT.Ln).then_inc(S("tok_log"), 1)
            act.wait_ge(S("tok_log"), 1)
            act.activation(rstd, rstd, ACT.Exp, scale=-0.5).then_inc(S("tok_rstd"), 1)
            act.wait_ge(S("gains"), 1)
            for k in range(KT):
                x = tok[:, k * TC + T:(k + 1) * TC]
                last = act.activation(x, x, ACT.Identity, scale=gain_c[:, k:k + 1], bias=mod_c[:, k:k + 1])
            last.then_inc(S("ctx_modulated"), 1)
            act.wait_ge(S("lat_modulated"), 1)
            act.wait_ge(S("ctx_modulated"), 1)
            act.activation(h_hi[:, :], tok[:, :], ACT.Copy).then_inc(S("h_hi"), 1)
            for n in range(AHEAD):
                hi(act, Chunk(n))

            for h in range(HEADS + 1):
                if h < HEADS:
                    hi(act, Chunk(N_V, h + AHEAD))
                if h >= 1:
                    act.wait_ge(S("multiplied"), h)
                    if h >= 3:
                        act.wait_ge(S("v_turned"), h - 2)
                    act.activation(v_T[(h - 1) % 2], psum[(h - 1) % 2][:, :], ACT.Copy).then_inc(S("v_T"), 1)

            def exps(h, p):
                act.wait_ge(S("scanned"), h * 2 + 2)
                if p is not None:
                    act.wait_ge(S("k_d"), h)
                    act.wait_ge(S("state"), h * 8)
                act.activation(e_qd.rearrange("p (d t) -> p d t", d=2),
                               b_buf.rearrange("p (d t) -> p d t", d=2)[:, :, 0:T], ACT.Exp).then_inc(S("e_qd"), 1)
                for d in range(2):
                    total = d * TC + (TC - 1 if d == 0 else T)
                    act.activation(e_kd[:, d * TC + T:(d + 1) * TC], b_buf[:, d * TC + T:(d + 1) * TC], ACT.Exp,
                                   scale=-1.0, bias=b_buf[:, total:total + 1]).then_inc(S("e_kc"), 1)
                act.wait_ge(S("d1"), h * 2 + 2)
                act.activation(e_qe, d1, ACT.Exp).then_inc(S("e_qe"), 1)
                act.activation(e_ke, d1, ACT.Exp, scale=-1.0).then_inc(S("e_ke"), 1)
                act.wait_ge(S("d3"), h * 2 + 2)
                x = e_kd.rearrange("p (d t) -> p d t", d=2)[:, :, 0:T]
                act.activation(x, x, ACT.Exp).then_inc(S("e_kd"), 1)

            def out_rstd(h):
                act.wait_ge(S("o_mean"), h + 1)
                act.activation(o_rs, o_rs, ACT.Ln).then_inc(S("o_log"), 1)
                act.wait_ge(S("o_log"), h + 1)
                act.activation(o_rs, o_rs, ACT.Exp, scale=-0.5).then_inc(S("o_rstd"), 1)

            def out_hi(h):
                act.wait_ge(S("y_full"), h + 1)
                act.activation(y_hi[:, bass.ds(h * T, T)], y_f, ACT.Copy).then_inc(S("y_hi"), 1)

            def head(h, at, new, prev, prev2):
                if new:
                    hi(act, at(AHEAD))
                if prev:
                    exps(h - 1, prev2 or None)
                if prev2:
                    out_rstd(h - 2)
                if new:
                    hi(act, at(1 + AHEAD))
                if prev2:
                    out_hi(h - 2)
                if new:
                    if prev:
                        act.wait_ge(S("scanned"), h * 2)
                    for d in range(2):
                        act.wait_ge(S("multiplied"), at(d).n + 1)
                        act.activation(f_buf[:, d * TC:(d + 1) * TC], psum[d][:, :], ACT.Exp, scale=-1.0).then_inc(S("f_exp"), 1)
                        hi(act, at(2 + d + AHEAD))
                if prev:
                    act.wait_ge(S("k_turned"), h)
                    if prev2:
                        act.wait_ge(S("kv"), h - 1)
                    act.activation(k_dT[:, 0:512], psum[3][:, :], ACT.Copy).then_inc(S("k_dT"), 1)
                    act.activation(k_dT[:, 512:1024], psum[4][:, :], ACT.Copy).then_inc(S("k_dT"), 1)
                if new:
                    act.wait_ge(S("f"), h * 2 + 2)
                    if prev:
                        act.wait_ge(S("k_d"), h)
                    act.activation(k_buf, f_buf, ACT.Copy, scale=-1.0, bias=1.0).then_inc(S("k"), 1)
                    act.activation(f_buf, f_buf, ACT.Ln).then_inc(S("log_f"), 1)
                    act.wait_ge(S("multiplied"), at(3).n + 1)
                    act.activation(qg_e, psum[2][:, :], ACT.Exp, scale=-1.0).then_inc(S("qg_exp"), 1)
                if prev:
                    act.wait_ge(S("o"), h)
                    act.activation(o_sq, psum[5][:, T:2 * T], ACT.Square).then_inc(S("o_squares"), 1)

            def head_at(h):
                return lambda m: Chunk(N_HEAD, 4 * h + m)

            for h in range(2):
                head(h, head_at(h), True, h >= 1, False)
            with act.Fori(0, (HEADS - 2) // 2) as i:
                for u in range(2):
                    head(i * 2 + (2 + u), lambda m: Chunk(N_HEAD + 8, 4 * u + m, i, 8), True, True, True)
            head(HEADS, None, False, True, True)
            for k in range(KT - AHEAD):
                hi(act, Chunk(N_HOUT, k + AHEAD))
            out_rstd(HEADS - 1)
            out_hi(HEADS - 1)
            hi(act, Chunk(N_HOUT, KT))
            hi(act, Chunk(N_HOUT, KT + 1))
            square_residual(act, 0, 1)
            norm_rstd(act, 0)
            split_h_hi(act, 1)

            def ffn_tile(t, p, s, n_done, has_old):
                act.wait_ge(S("multiplied"), n_done)
                if has_old:
                    act.wait_ge(S("u_full"), t - 1)
                for half in range(2):
                    act.activation(conv[p][half], psum[4 + 2 * half + p][:, 0:T], ACT.Identity,
                                   scale=p1("conv_w", t + (2 * JF + half * JF)),
                                   bias=p1("conv_b", t + half * JF)).then_inc(S("conv_mid"), 1)
                act.wait_ge(S("conv"), t * 2 + 2)
                act.activation(f_silu[p], conv[p][0], ACT.Silu).then_inc(S("f_silu"), 1)
                act.wait_ge(S("u_full"), t + 1)
                act.activation(y_hi[:, s * T:s * T + T], u_f[p], ACT.Copy).then_inc(S("u_hi"), 1)

            for j in range(FFN_PEEL):
                c = ffn_first(j)
                hi(act, Chunk(c, AHEAD))
                hi(act, Chunk(c, 1 + AHEAD))
                if j >= 1:
                    ffn_tile(j - 1, (j - 1) % 2, (j - 1) % 4, ffn_first(j - 1) + 2, j >= 3)
                if j >= 2:
                    hi(act, Chunk(c, 2 + AHEAD))
            with act.Fori(0, (JF - FFN_PEEL) // 4) as i:
                for u in range(4):
                    hi(act, Chunk(ffn_first(FFN_PEEL), 3 * u + AHEAD, i, 12))
                    hi(act, Chunk(ffn_first(FFN_PEEL), 3 * u + 1 + AHEAD, i, 12))
                    t = FFN_PEEL + u - 1
                    ffn_tile(i * 4 + t, t % 2, t % 4, i * 12 + (ffn_first(t) + 2), True)
                    hi(act, Chunk(ffn_first(FFN_PEEL), 3 * u + 2 + AHEAD, i, 12))
            hi(act, Chunk(N_IN2 - 2, AHEAD))
            ffn_tile(JF - 1, (JF - 1) % 2, (JF - 1) % 4, ffn_first(JF - 1) + 2, True)
            hi(act, Chunk(N_IN2 - 1, AHEAD))
            square_residual(act, 1, 2)
            norm_rstd(act, 1)
            square_residual(act, 2, 3)
            norm_rstd(act, 2)
            split_h_hi(act, 2)

            def evacuate(t):
                act.wait_ge(S("multiplied"), N_IN2 + t + 1)
                z = psum[t % 4][:, 0:T]
                dst = in2_dst(t)
                if dst is not None:
                    act.activation(dst, z, ACT.Copy).then_inc(S("in2_copied"), 1)
                elif t < T_GR:
                    v = v_index(t)
                    if v >= 2:
                        act.wait_ge(S("v2_turned"), v - 1)
                    act.activation(v_tmp[v % 2], z, ACT.Copy).then_inc(S("in2_copied"), 1)
                else:
                    act.activation(gate_dst(t), z, ACT.Exp, scale=-1.0).then_inc(S("gate_exp"), 1)

            def softmax_exp(e):
                p = e % 2
                act.wait_ge(S("s_neg"), e + 1)
                if e >= 2:
                    act.wait_ge(S("p_turned"), e - 1)
                act.activation(s_p[p][:, 0:P], s_b[p][:, 0:P], ACT.Exp, scale=S_DH ** -0.5, bias=s_neg[p][:, 0:1],
                               accum_out=s_sum[p][:, 0:1]).then_inc(S("s_exp"), 1)
                act.activation(s_p[p][:, P:3 * P], s_b[p][:, P:3 * P], ACT.Exp, scale=S_DH ** -0.5,
                               bias=s_neg[p][:, 1:2], accum_out=s_sum[p][:, 1:2]).then_inc(S("s_exp"), 1)
                act.activation(s_sink[p], s_neg[p], ACT.Exp, bias=sink[:, e:e + 1]).then_inc(S("s_exp"), 1)

            def probs_copy(e):
                act.wait_ge(S("p_turned"), e + 1)
                if e >= 2:
                    act.wait_ge(S("pv"), e - 1)
                act.activation(s_pT[e % 2], psum[7][:, 0:3 * P], ACT.Copy).then_inc(S("p_T"), 1)

            def ret_squares(r):
                act.wait_ge(S("r_o"), r + 1)
                act.activation(r_sq, psum[4][:, :], ACT.Square).then_inc(S("r_squares"), 1)

            def ret_rstd(r):
                act.wait_ge(S("r_mean"), r + 1)
                act.activation(r_rs, r_rs, ACT.Ln).then_inc(S("r_log"), 1)
                act.wait_ge(S("r_log"), r + 1)
                act.activation(r_rs, r_rs, ACT.Exp, scale=-0.5).then_inc(S("r_rstd"), 1)

            def ret_hi(r):
                act.wait_ge(S("r_full"), r + 1)
                act.activation(y_hi[:, 2 * r * T:2 * (r + 1) * T], r_t, ACT.Copy).then_inc(S("r_hi"), 1)

            act.wait_ge(S("late_in"), 32)
            for t in range(TILES_IN2 + 1):
                if t < TILES_IN2:
                    hi(act, Chunk(N_IN2, t + AHEAD))
                if t >= 1:
                    evacuate(t - 1)
                e = t - T_GR
                if 1 <= e <= S_HEADS:
                    softmax_exp(e - 1)
                    probs_copy(e - 1)
                if e == S_HEADS + 3:
                    act.wait_ge(S("swa"), S_HEADS)
                    act.activation(h_hi[:, 8 * T:12 * T], swa, ACT.Copy).then_inc(S("swa_hi"), 1)
                r = t - RET_FIRST
                if r >= 3 and r % 2 == 1 and (r - 3) // 2 < R_HEADS:
                    ret_rstd((r - 3) // 2)
                    ret_hi((r - 3) // 2)
                if r >= 1 and r % 2 == 1 and (r - 1) // 2 < R_HEADS:
                    ret_squares((r - 1) // 2)
            for n in range(N_SOUT, N_MOUT):
                hi(act, Chunk(n, AHEAD))
            for b in range(4):
                act.wait_ge(S("mg_full"), b + 1)
                act.activation(h_hi[:, b * 512:b * 512 + 512], gate_r[:, b * 512:b * 512 + 512], ACT.Copy).then_inc(S("mg_hi"), 1)
                hi(act, Chunk(N_MOUT, b + AHEAD))
            for n in range(N_MOUT + 4, N_MLP):
                hi(act, Chunk(n, AHEAD))
            square_banks(act, N_MLP, HIGH_BANKS)
            norm_rstd(act, 3)
            square_residual(act, 4, 4)
            norm_rstd(act, 4)
            split_h_hi(act, 3)

            def mlp_tile(t, p, s, n_done, has_old):
                act.wait_ge(S("multiplied"), n_done)
                if has_old:
                    act.wait_ge(S("m_full"), t - 1)
                act.activation(m_relu[p], psum[4 + p][:, 0:T], ACT.Relu).then_inc(S("m_relu"), 1)
                act.wait_ge(S("m_full"), t + 1)
                act.activation(y_hi[:, s * T:s * T + T], u_f[p], ACT.Copy).then_inc(S("m_hi"), 1)

            for j in range(MLP_PEEL):
                hi(act, Chunk(mlp_first(j), AHEAD))
                if j >= 1:
                    mlp_tile(j - 1, (j - 1) % 2, (j - 1) % 4, mlp_first(j - 1) + 1, j >= 3)
                if j >= 2:
                    hi(act, Chunk(mlp_first(j), 1 + AHEAD))
            with act.Fori(0, (JM - MLP_PEEL) // 4 - 1) as i:
                for u in range(4):
                    hi(act, Chunk(mlp_first(MLP_PEEL), 2 * u + AHEAD, i, 8))
                    t = MLP_PEEL + u - 1
                    mlp_tile(i * 4 + t, t % 2, t % 4, i * 8 + (mlp_first(t) + 1), True)
                    hi(act, Chunk(mlp_first(MLP_PEEL), 2 * u + 1 + AHEAD, i, 8))
            for j in range(JM - 4, JM):
                hi(act, Chunk(mlp_first(j), AHEAD))
                mlp_tile(j - 1, (j - 1) % 2, (j - 1) % 4, mlp_first(j - 1) + 1, True)
                hi(act, Chunk(mlp_first(j), 1 + AHEAD))
            mlp_tile(JM - 1, (JM - 1) % 2, (JM - 1) % 4, mlp_first(JM - 1) + 1, True)
            square_banks(act, N_ALL, LOW_BANKS)
            norm_rstd(act, 5)

        @block.tensor
        def _(pe):
            pe.wait_ge(S("con_in"), 16)
            pe.wait_ge(S("tok_squares"), 1)
            for k in range(KT):
                last = pe.matmul(psum[1][:, :], ones, wide[:, k * TC:(k + 1) * TC], start=k == 0, stop=k == KT - 1)
            last.then_inc(S("tok_summed"), 1)
            pe.wait_ge(S("cs"), 1)

            def ada(bank, col, slot, rounds):
                pe.wait_ge(S(f"loaded{slot}"), rounds * 16 + 16)
                for k in range(KT):
                    last = pe.matmul(psum[bank][:, bass.ds(col, 2)], raw[slot][:, k * P:k * P + P],
                                     cs[:, 2 * k:2 * k + 2], start=k == 0, stop=k == KT - 1, skip_group_check=True)
                last.then_inc(S("ada_done"), 1)

            with pe.Fori(0, ADA_FIRST // RING) as i:
                for u in range(RING):
                    ada(0, i * (2 * RING) + 2 * u, u, i)
            with pe.Fori(ADA_FIRST // RING, ADA // RING) as i:
                for u in range(RING):
                    ada(2, i * (2 * RING) + (2 * u - 2 * ADA_FIRST), u, i)

            pe.wait_ge(S("h_lo"), 1)
            for h in range(HEADS + 1):
                if h < HEADS:
                    if h >= 2:
                        pe.wait_ge(S("v_T"), h - 1)
                    column_tile(pe, Chunk(N_V, h), psum[h % 2][:, :], TC, TC)
                if h >= 1:
                    pe.wait_ge(S("v_T"), h)
                    if h >= 3:
                        pe.wait_ge(S("v"), h - 2)
                    for b in range(4):
                        last = pe.transpose(psum[3 + (h - 1) % 2][:, b * P:b * P + P],
                                            v_T[(h - 1) % 2][:, b * P:b * P + P], ident)
                    last.then_inc(S("v_turned"), 1)

            def out_sum(h):
                pe.wait_ge(S("o_squares"), h + 1)
                pe.matmul(psum[3][:, 0:T], ones, o_sq, start=True, stop=True).then_inc(S("o_summed"), 1)

            def turn_and_score(h, p, old):
                pe.wait_ge(S("k_d"), h + 1)
                if old:
                    pe.wait_ge(S("o_mean"), h)
                    pe.wait_ge(S("o_n"), h)
                for part_ in range(2):
                    for d in range(2):
                        for b in range(2):
                            at = d * TC + part_ * T + b * P
                            last = pe.transpose(psum[3 + part_][:, (2 * d + b) * P:(2 * d + b + 1) * P],
                                                k_d[p][:, at:at + P], ident)
                last.then_inc(S("k_turned"), 1)
                for d in range(2):
                    behind, ahead = (HALF, 0) if d == 0 else (0, HALF)
                    for c in range(NCH):
                        x = d * T + c * CH
                        y = (2 * d + c // 2) * CH
                        row = CH * (c % 2)
                        pe.matmul(psum[5][row:row + CH, y + behind:y + behind + HALF], k_e[p][:, x:x + CH],
                                  q_e[p][:, x + behind:x + behind + HALF], start=True, stop=True, skip_group_check=True)
                        last = pe.matmul(psum[5][row + ahead:row + ahead + HALF, y + ahead:y + ahead + HALF],
                                         k_e[p][:, x + ahead:x + ahead + HALF], q_e[p][:, x + ahead:x + ahead + HALF],
                                         start=True, stop=True, skip_group_check=True)
                last.then_inc(S("scores"), 1)

            def key_values(h):
                pe.wait_ge(S("k_dT"), h * 2 + 2)
                pe.wait_ge(S("v_cur"), h + 1)
                for d in range(2):
                    for b in range(2):
                        x = 512 + (2 * d + b) * P
                        pe.matmul(psum[6 + d][:, 0:P], k_dT[:, x:x + P], v_cur[:, (2 + b) * P:(3 + b) * P],
                                  start=b == 0, stop=b == 1)
                    for s in range(1, NCH):
                        c = s - 1 if d == 0 else NCH - s
                        rows = slice(CH * (c % 2), CH * (c % 2) + CH)
                        x = (2 * d + c // 2) * P
                        last = pe.matmul(kv_at(d, s), k_dT[rows, x:x + P], v_cur[rows, (c // 2) * P:(c // 2 + 1) * P],
                                         start=True, stop=True, skip_group_check=True)
                last.then_inc(S("kv"), 1)

            def outputs(h, p):
                pe.wait_ge(S("masked"), h * 2 + 2)
                pe.wait_ge(S("state"), h * 8 + 8)
                for c in range(NCH):
                    dst = psum[5][:, T + c * CH:T + (c + 1) * CH]
                    for d in range(2):
                        pos = c if d == 0 else NCH - 1 - c
                        pe.matmul(dst, v_cur[:, (c // 2) * P:(c // 2 + 1) * P],
                                  sc_T[:, (NCH * d + c) * CH:(NCH * d + c + 1) * CH],
                                  start=d == 0, stop=False, skip_group_check=True)
                        last = pe.matmul(dst, state[:, (4 * d + pos) * P:(4 * d + pos + 1) * P],
                                         q_d[p][:, d * T + c * CH:d * T + (c + 1) * CH],
                                         start=False, stop=d == 1, skip_group_check=True)
                last.then_inc(S("o"), 1)

            def head(h, u, at, new, prev, prev2):
                if new:
                    if prev:
                        pe.wait_ge(S("f_exp"), h * 2)
                    else:
                        pe.wait_ge(S("v_T"), HEADS)
                    column_tile(pe, at(0), psum[0][:, :], TC, TC)
                if prev2:
                    out_sum(h - 2)
                if new:
                    column_tile(pe, at(1), psum[1][:, :], TC, TC)
                if prev:
                    if not prev2:
                        pe.wait_ge(S("scores_cleared"), 1)
                        pe.wait_ge(S("v"), HEADS)
                    turn_and_score(h - 1, 1 - u, prev2)
                if new:
                    if prev:
                        pe.wait_ge(S("qg"), h)
                    else:
                        pe.wait_ge(S("mod_late"), 1)
                    column_tile(pe, at(2), psum[2][:, 0:T], TC, T)
                if prev:
                    key_values(h - 1)
                if new:
                    column_tile(pe, at(3), psum[2][:, T:2 * T], TC, T)
                if prev:
                    outputs(h - 1, 1 - u)

            for h in range(2):
                head(h, h, lambda m: Chunk(N_HEAD, 4 * h + m), True, h >= 1, False)
            with pe.Fori(0, (HEADS - 2) // 2) as i:
                for u in range(2):
                    head(i * 2 + (2 + u), u, lambda m: Chunk(N_HEAD + 8, 4 * u + m, i, 8), True, True, True)
            head(HEADS, 0, None, False, True, True)
            for k in range(KT):
                if k == KT - 2:
                    out_sum(HEADS - 1)
                pe.wait_ge(S("y_lo"), k + 1)
                if k == 0:
                    pe.wait_ge(S("k_dT"), 2 * HEADS)
                    pe.wait_ge(S("qg"), HEADS)
                    pe.wait_ge(S("f_exp"), 2 * HEADS)
                row_tile(pe, Chunk(N_HOUT, k), HOUT_BANKS, y_hi[:, k * T:k * T + T], y_lo[:, k * T:k * T + T],
                         k == 0, k == KT - 1)
            norm_sum(pe, 0)

            def ffn_up(j, p, c, has_old):
                if has_old:
                    pe.wait_ge(S("conv"), j * 2 - 2)
                column_tile(pe, c[0], psum[4 + p][:, 0:T], T, T)
                column_tile(pe, c[1], psum[6 + p][:, 0:T], T, T)

            def ffn_down(t, s, c, first, last):
                pe.wait_ge(S("u_lo"), t + 1)
                row_tile(pe, c, LOW_BANKS, y_hi[:, s * T:s * T + T], y_lo[:, s * T:s * T + T], first, last)

            pe.wait_ge(S("h_lo"), 2)
            for j in range(FFN_PEEL):
                c = ffn_first(j)
                ffn_up(j, j % 2, [Chunk(c), Chunk(c, 1)], j >= 2)
                if j >= 2:
                    ffn_down(j - 2, (j - 2) % 4, Chunk(c, 2), j == 2, False)
            with pe.Fori(0, (JF - FFN_PEEL) // 4) as i:
                for u in range(4):
                    j = FFN_PEEL + u
                    c = [Chunk(ffn_first(FFN_PEEL), 3 * u + m, i, 12) for m in range(3)]
                    ffn_up(i * 4 + j, j % 2, c, True)
                    ffn_down(i * 4 + (j - 2), (j - 2) % 4, c[2], False, False)
            for t in range(JF - 2, JF):
                ffn_down(t, t % 4, Chunk(N_IN2 - JF + t), False, t == JF - 1)
            norm_sum(pe, 1)
            norm_sum(pe, 2)

            def turn_values(t):
                v = v_index(t)
                pe.wait_ge(S("in2_copied"), t + 1)
                if v >= 2:
                    pe.wait_ge(S("v2"), v - 1)
                for b in range(2):
                    last = pe.transpose(psum[4 + v % 2][:, b * P:b * P + P], v_tmp[v % 2][:, b * P:b * P + P], ident)
                last.then_inc(S("v2_turned"), 1)

            def swa_scores(e):
                g, x = e // 4, (e % 4) * T
                rows = slice(S_DH * g, S_DH * g + S_DH)
                if e == 0:
                    pe.wait_ge(S("v2"), 8)
                if e >= 2:
                    pe.wait_ge(S("s_biased"), e - 1)
                dst = psum[5 + e % 2]
                pe.matmul(dst[:, 0:P], s_q[rows, x:x + P], s_k[rows, 0:P], start=True, stop=True, skip_group_check=True)
                pe.matmul(dst[:, P:3 * P], s_q[rows, x + P:x + T], s_k[rows, 0:T], start=True, stop=True,
                          skip_group_check=True).then_inc(S("s_scores"), 1)

            def turn_probs(e):
                pe.wait_ge(S("p_norm"), 2 * e + 2)
                if e >= 1:
                    pe.wait_ge(S("p_T"), e)
                for b in range(3):
                    last = pe.transpose(psum[7][:, b * P:b * P + P], s_p[e % 2][:, b * P:b * P + P], ident)
                last.then_inc(S("p_turned"), 1)

            def swa_values(e):
                g, q = e // 4, S_DH * (e % 2)
                pe.wait_ge(S("p_T"), e + 1)
                if e == 0:
                    pe.wait_ge(S("v2"), 9)
                if e >= 2:
                    pe.wait_ge(S("swa"), e - 1)
                pe.matmul(psum[4][q:q + S_DH, 0:T], s_v[:, S_DH * g:S_DH * g + S_DH], s_pT[e % 2][:, 0:T],
                          start=True, stop=False, skip_group_check=True)
                pe.matmul(psum[4][q:q + S_DH, P:T], s_v[:, P + S_DH * g:P + S_DH * g + S_DH], s_pT[e % 2][:, T:3 * P],
                          start=False, stop=True, skip_group_check=True).then_inc(S("pv"), 1)

            def ret_scores(r):
                dst = psum[5 + r % 2]
                if r == 0:
                    pe.wait_ge(S("s_biased"), S_HEADS)
                if r >= 2:
                    pe.wait_ge(S("r_sc"), r - 1)
                pe.matmul(dst[:, 0:T], r_k[:, r * T:r * T + P], r_q[:, r * T:(r + 1) * T], start=True, stop=True,
                          skip_group_check=True)
                pe.matmul(dst[:, T:3 * P], r_k[:, r * T + P:(r + 1) * T], r_q[:, r * T + P:(r + 1) * T], start=True,
                          stop=True, skip_group_check=True).then_inc(S("r_scores"), 1)

            def ret_values(r):
                pe.wait_ge(S("r_sc"), r + 1)
                if r == 0:
                    pe.wait_ge(S("swa"), S_HEADS)
                    pe.wait_ge(S("v_centred"), 1)
                else:
                    pe.wait_ge(S("r_normed"), r)
                for m in range(2):
                    x = r * R_DV + m * P
                    pe.matmul(psum[4][:, m * T:m * T + T], r_v[:, x:x + P], r_sc[r % 2][:, 0:T], start=True, stop=False,
                              skip_group_check=True)
                    last = pe.matmul(psum[4][:, m * T + P:m * T + T], r_v[:, 4 * T + x:4 * T + x + P],
                                     r_sc[r % 2][:, T:3 * P], start=False, stop=True, skip_group_check=True)
                last.then_inc(S("r_o"), 1)

            def ret_sum(r):
                pe.wait_ge(S("r_squares"), r + 1)
                if r == 0:
                    pe.wait_ge(S("p_T"), S_HEADS)
                else:
                    pe.wait_ge(S("r_mean"), r)
                for m in range(2):
                    last = pe.matmul(psum[7][:, 0:T], ones, r_sq[:, m * T:m * T + T], start=m == 0, stop=m == 1)
                last.then_inc(S("r_summed"), 1)

            pe.wait_ge(S("h_lo"), 3)
            for t in range(TILES_IN2):
                if 4 <= t < T_GR + 4:
                    pe.wait_ge(S("in2_copied"), t - 3)
                elif t >= T_GR + 4:
                    pe.wait_ge(S("gate"), t - T_GR - 3)
                column_tile(pe, Chunk(N_IN2, t), psum[t % 4][:, 0:T], T, T)
                if t >= 1 and v_index(t - 1) is not None:
                    turn_values(t - 1)
                e = t - T_GR
                if 0 <= e < S_HEADS:
                    swa_scores(e)
                if 1 <= e <= S_HEADS:
                    turn_probs(e - 1)
                if 2 <= e <= S_HEADS + 1:
                    swa_values(e - 2)
                r = t - RET_FIRST
                if 0 <= r < 2 * R_HEADS and r % 2 == 0:
                    ret_scores(r // 2)
                if r >= 1 and r % 2 == 1 and (r - 1) // 2 < R_HEADS:
                    ret_values((r - 1) // 2)
                if r >= 2 and r % 2 == 0 and (r - 2) // 2 < R_HEADS:
                    ret_sum((r - 2) // 2)

            pe.wait_ge(S("swa_lo"), 1)
            pe.wait_ge(S("r_lo"), R_HEADS)
            for k in range(4):
                x = slice((8 + k) * T, (9 + k) * T)
                row_tile(pe, Chunk(N_SOUT, k), HIGH_BANKS, h_hi[:, x], h_lo[:, x], k == 0, k == 3)
            pe.wait_ge(S("gate"), TILES_IN2 - T_GR)
            for k in range(KT):
                x = slice(k * T, (k + 1) * T)
                row_tile(pe, Chunk(N_ROUT, k), LOW_BANKS, y_hi[:, x], y_lo[:, x], k == 0, k == KT - 1)
            for k in range(KT):
                x = slice(k * T, (k + 1) * T)
                pe.wait_ge(S("mg_lo"), k // 2 + 1)
                row_tile(pe, Chunk(N_MOUT, k), HIGH_BANKS, h_hi[:, x], h_lo[:, x], k == 0, k == KT - 1)
            norm_sum(pe, 3, bank=0)
            norm_sum(pe, 4)

            def mlp_up(j, p, c, has_old):
                if has_old:
                    pe.wait_ge(S("m_relu"), j - 1)
                column_tile(pe, c, psum[4 + p][:, 0:T], T, T)

            def mlp_down(t, s, c, first, last):
                pe.wait_ge(S("m_lo"), t + 1)
                row_tile(pe, c, LOW_BANKS, y_hi[:, s * T:s * T + T], y_lo[:, s * T:s * T + T], first, last)

            pe.wait_ge(S("h_lo"), 4)
            for j in range(MLP_PEEL):
                mlp_up(j, j % 2, Chunk(mlp_first(j)), j >= 2)
                if j >= 2:
                    mlp_down(j - 2, (j - 2) % 4, Chunk(mlp_first(j), 1), j == 2, False)
            with pe.Fori(0, (JM - MLP_PEEL) // 4) as i:
                for u in range(4):
                    j = MLP_PEEL + u
                    mlp_up(i * 4 + j, j % 2, Chunk(mlp_first(MLP_PEEL), 2 * u, i, 8), True)
                    mlp_down(i * 4 + (j - 2), (j - 2) % 4, Chunk(mlp_first(MLP_PEEL), 2 * u + 1, i, 8), False, False)
            for t in range(JM - 2, JM):
                mlp_down(t, t % 4, Chunk(N_ALL - JM + t), False, t == JM - 1)
            norm_sum(pe, 5)

        @block.vector
        def _(dve):
            dve.wait_ge(S("small_in"), 32)
            dve.tensor_tensor(lb_m, p1("lb0", 0, 16), p1("lb1", 0, 16), ALU.max).then_inc(S("lb_max"), 1)
            dve.wait_ge(S("cs_exp"), 1)
            dve.tensor_scalar(cs_e, cs_e, 1.0, None, ALU.add).then_inc(S("cs_1"), 1)
            dve.wait_ge(S("cs_1"), 1)
            dve.reciprocal(cs_e, cs_e).then_inc(S("cs_r"), 1)
            dve.wait_ge(S("cs_r"), 1)
            dve.tensor_tensor(cs, cc[:, :], cs_e, ALU.mult).then_inc(S("cs"), 1)
            dve.wait_ge(S("lb_max"), 1)
            dve.tensor_tensor(lb_d[:, 0:16], p1("lb0", 0, 16), lb_m, ALU.subtract)
            dve.tensor_tensor(lb_d[:, 16:32], p1("lb1", 0, 16), lb_m, ALU.subtract).then_inc(S("lb_diff"), 1)
            dve.wait_ge(S("lb_exp"), 1)
            dve.tensor_tensor(lb_m, lb_d[:, 0:16], lb_d[:, 16:32], ALU.add).then_inc(S("lb_sum"), 1)
            dve.wait_ge(S("lb_sum"), 1)
            dve.reciprocal(lb_m, lb_m).then_inc(S("lb_r"), 1)
            dve.wait_ge(S("lb_r"), 1)
            dve.tensor_tensor(lb, lb_d[:, 0:16], lb_m, ALU.mult).then_inc(S("lb"), 1)
            dve.wait_ge(S("lb"), 1)
            dve.tensor_scalar(lb_om, lb, -1.0, 1.0, ALU.mult, ALU.add).then_inc(S("lb_om"), 1)
            dve.memset(sc_T, 0.0)
            dve.memset(psum[5][:, 0:T], 0.0).then_inc(S("scores_cleared"), 1)
            dve.wait_ge(S("tok_summed"), 1)
            dve.tensor_scalar(rstd, psum[1][:, :], 1.0 / D, EPS, ALU.mult, ALU.add).then_inc(S("tok_mean"), 1)
            dve.wait_ge(S("tok_rstd"), 1)
            dve.tensor_tensor(by_tile(tok[:, :]), by_tile(tok[:, :]), over_tiles(rstd), ALU.mult).then_inc(S("tok_normed"), 1)
            dve.wait_ge(S("ada_done"), ADA_FIRST)
            ps0 = psum[0][:, 0:2 * ADA_FIRST].rearrange("p (a w) -> p a w", w=2)
            dve.tensor_tensor(mod[:, 0:ADA_FIRST], ps0[:, :, 0], p1("b_ada", 0, ADA_FIRST), ALU.add)
            dve.tensor_tensor(mod_c, ps0[:, :, 1], p1("b_ada", 0, ADA_FIRST), ALU.add).then_inc(S("mod_first"), 1)
            dve.wait_ge(S("mod_first"), 1)
            dve.scalar_tensor_tensor(gain_l, mod[:, KT:2 * KT], 1.0, p1("norm1", 0, KT), ALU.add, ALU.mult)
            dve.scalar_tensor_tensor(gain_c, mod_c[:, KT:2 * KT], 1.0, p1("norm1", 0, KT), ALU.add,
                                     ALU.mult).then_inc(S("gains"), 1)
            dve.wait_ge(S("gains"), 1)
            dve.wait_ge(S("tok_normed"), 1)
            for k in range(KT):
                x = tok[:, k * TC:k * TC + T]
                last = dve.tensor_scalar(x, x, gain_l[:, k:k + 1], mod[:, k:k + 1], ALU.mult, ALU.add)
            last.then_inc(S("lat_modulated"), 1)
            dve.wait_ge(S("h_hi"), 1)
            dve.tensor_tensor(h_lo[:, :], tok[:, :], h_hi[:, :].bitcast(F32), ALU.subtract).then_inc(S("h_lo"), 1)
            dve.wait_ge(S("ada_done"), ADA)
            ps2 = psum[2][:, 0:2 * (ADA - ADA_FIRST)].rearrange("p (a w) -> p a w", w=2)
            dve.tensor_tensor(mod[:, ADA_FIRST:ADA], ps2[:, :, 0], p1("b_ada", ADA_FIRST, ADA - ADA_FIRST),
                              ALU.add).then_inc(S("mod_late"), 1)
            dve.wait_ge(S("mod_late"), 1)
            dve.scalar_tensor_tensor(gain_2, mod[:, 4 * KT:5 * KT], 1.0, p1("norm2", 0, KT), ALU.add,
                                     ALU.mult).then_inc(S("gain_2"), 1)
            for n in range(AHEAD):
                lo(dve, Chunk(n))

            for h in range(HEADS + 1):
                if h < HEADS:
                    lo(dve, Chunk(N_V, h + AHEAD))
                if h >= 1:
                    dve.wait_ge(S("v_turned"), h)
                    dve.tensor_copy(v_all[:, (h - 1) * 512:h * 512], psum[3 + (h - 1) % 2][:, :]).then_inc(S("v"), 1)

            def split2(x):
                return x.rearrange("p (d t) -> p d t", d=2)

            def chunks(x):
                return x.rearrange("p (c t) -> p c t", c=NCH)

            def distances(h, old):
                dve.wait_ge(S("scanned"), h * 2 + 2)
                if old:
                    dve.wait_ge(S("e_ke"), h)
                for d in range(2):
                    b = chunks(b_buf[:, d * TC:d * TC + T])
                    at = CH // 2 if d == 0 else CH - 1 - CH // 2
                    dve.tensor_tensor(chunks(d1[:, d * T:(d + 1) * T]), b, b[:, :, at:at + 1].broadcast_to([P, NCH, CH]),
                                      ALU.subtract).then_inc(S("d1"), 1)
                for d in range(2):
                    b = chunks(b_buf[:, d * TC:d * TC + T])
                    at = CH - 1 if d == 0 else 0
                    dve.tensor_tensor(chunks(e_kd[:, d * TC:d * TC + T]), b[:, :, at:at + 1].broadcast_to([P, NCH, CH]), b,
                                      ALU.subtract).then_inc(S("d3"), 1)

            def silu_qg(h, p):
                dve.wait_ge(S("qg_exp"), h + 1)
                dve.tensor_scalar(qg_e, qg_e, 1.0, None, ALU.add).then_inc(S("qg_1"), 1)
                dve.wait_ge(S("qg_1"), h + 1)
                dve.reciprocal(qg_e, qg_e).then_inc(S("qg_r"), 1)
                dve.wait_ge(S("qg_r"), h + 1)
                dve.tensor_tensor(qg[p], psum[2][:, :], qg_e, ALU.mult).then_inc(S("qg"), 1)

            def scale_qk(h, p, old2):
                if old2:
                    dve.wait_ge(S("o"), h - 1)
                dve.wait_ge(S("qg"), h + 1)
                q = over_tiles(qg[p][:, 0:T], 2)
                dve.wait_ge(S("e_qd"), h + 1)
                dve.tensor_tensor(split2(q_d[p]), split2(e_qd), q, ALU.mult)
                dve.wait_ge(S("e_qe"), h + 1)
                dve.tensor_tensor(split2(q_e[p]), split2(e_qe), q, ALU.mult)
                dve.wait_ge(S("e_ke"), h + 1)
                dve.wait_ge(S("k"), h + 1)
                dve.tensor_tensor(split2(k_e[p]), split2(e_ke), split2(k_buf)[:, :, 0:T], ALU.mult)
                dve.wait_ge(S("e_kd"), h + 1)
                dve.tensor_tensor(k_d[p], e_kd, k_buf, ALU.mult).then_inc(S("k_d"), 1)

            def out_mean(h):
                dve.wait_ge(S("o_summed"), h + 1)
                dve.tensor_scalar(o_rs, psum[3][:, 0:T], 1.0 / P, EPS, ALU.mult, ALU.add).then_inc(S("o_mean"), 1)

            def out_gated(h, p):
                dve.wait_ge(S("o_rstd"), h + 1)
                dve.tensor_tensor(o_n, psum[5][:, T:2 * T], o_rs, ALU.mult).then_inc(S("o_n"), 1)
                dve.wait_ge(S("o_n"), h + 1)
                dve.scalar_tensor_tensor(y_f, o_n, p1("gnorm"), qg[p][:, T:2 * T], ALU.mult, ALU.mult).then_inc(S("y_full"), 1)

            def out_lo(h):
                dve.wait_ge(S("y_hi"), h + 1)
                dve.tensor_tensor(y_lo[:, bass.ds(h * T, T)], y_f, y_hi[:, bass.ds(h * T, T)].bitcast(F32),
                                  ALU.subtract).then_inc(S("y_lo"), 1)

            def forget(h):
                dve.wait_ge(S("f_exp"), h * 2 + 2)
                dve.tensor_scalar(f_buf, f_buf, 1.0, None, ALU.add).then_inc(S("f_1"), 1)
                dve.wait_ge(S("f_1"), h + 1)
                dve.reciprocal(f_buf, f_buf).then_inc(S("f_r"), 1)
                dve.wait_ge(S("f_r"), h + 1)
                for d in range(2):
                    x = f_buf[:, d * TC:(d + 1) * TC]
                    dve.tensor_scalar(x, x, lb_om[:, bass.ds(h + d * HEADS, 1)], lb[:, bass.ds(h + d * HEADS, 1)],
                                      ALU.mult, ALU.add).then_inc(S("f"), 1)

            def values_and_mask(h, old):
                if old:
                    dve.wait_ge(S("o"), h)
                dve.wait_ge(S("scores"), h + 1)
                dve.tensor_copy(v_cur, v_all[:, bass.ds(h * 512, 512)]).then_inc(S("v_cur"), 1)
                for odd in range(2):
                    rows = slice(CH * odd, CH * odd + CH)
                    dst = sc_T.rearrange("p (n q t) -> p n q t", q=2, t=CH)[rows, :, odd, :]
                    dve.copy_predicated(dst, by_tile(msk[rows, :], 4), by_tile(psum[5][rows, 0:T], 4)).then_inc(S("masked"), 1)

            def states(h):
                dve.wait_ge(S("kv"), h + 1)
                for s in range(NCH):
                    for d in range(2):
                        dst = state[:, (4 * d + s) * P:(4 * d + s + 1) * P]
                        kv = kv_at(d, s)
                        if s == 0:
                            dve.tensor_copy(dst, kv).then_inc(S("state"), 1)
                            continue
                        c = s - 1 if d == 0 else NCH - s
                        end = d * T + c * CH + (CH - 1 if d == 0 else 0)
                        dve.wait_ge(S("state"), h * 8 + (2 * s + d - 1))
                        dve.scalar_tensor_tensor(dst, state[:, (4 * d + s - 1) * P:(4 * d + s) * P], e_qd[:, end:end + 1],
                                                 kv, ALU.mult, ALU.add).then_inc(S("state"), 1)

            def scan(h):
                dve.wait_ge(S("log_f"), h + 1)
                dve.tensor_tensor_scan(b_buf[:, 0:TC], scan_mask[0], f_buf[:, 0:TC], 0.0, ALU.mult, ALU.add).then_inc(S("scanned"), 1)
                dve.tensor_tensor_scan(b_buf[:, TC:2 * TC][:, ::-1], scan_mask[1], f_buf[:, TC:2 * TC][:, ::-1], 0.0,
                                       ALU.mult, ALU.add).then_inc(S("scanned"), 1)

            def head(h, u, at, new, prev, prev2):
                if new:
                    lo(dve, at(AHEAD))
                if prev:
                    distances(h - 1, prev2)
                    silu_qg(h - 1, 1 - u)
                if prev2:
                    out_mean(h - 2)
                if new:
                    lo(dve, at(1 + AHEAD))
                if prev:
                    scale_qk(h - 1, 1 - u, prev2)
                if prev2:
                    out_gated(h - 2, u)
                if prev2:
                    out_lo(h - 2)
                if new:
                    lo(dve, at(2 + AHEAD))
                    forget(h)
                if prev:
                    values_and_mask(h - 1, prev2)
                if new:
                    lo(dve, at(3 + AHEAD))
                if prev:
                    states(h - 1)
                if new:
                    scan(h)

            dve.wait_ge(S("late_in"), 32)
            dve.wait_ge(S("con_in"), 16)
            for h in range(2):
                head(h, h, lambda m: Chunk(N_HEAD, 4 * h + m), True, h >= 1, False)
            with dve.Fori(0, (HEADS - 2) // 2) as i:
                for u in range(2):
                    head(i * 2 + (2 + u), u, lambda m: Chunk(N_HEAD + 8, 4 * u + m, i, 8), True, True, True)
            head(HEADS, 0, None, False, True, True)
            for k in range(KT - AHEAD):
                lo(dve, Chunk(N_HOUT, k + AHEAD))
            out_mean(HEADS - 1)
            out_gated(HEADS - 1, 1)
            out_lo(HEADS - 1)
            lo(dve, Chunk(N_HOUT, KT))
            lo(dve, Chunk(N_HOUT, KT + 1))
            dve.wait_ge(S("xres_in"), 16)
            add_product(dve, lambda m: mod[:, 2 * KT + m:2 * KT + m + 1], N_FFN, HOUT_BANKS)
            norm_mean(dve, 0)
            scale_residual(dve, 0, lambda m: gain_2[:, m:m + 1], normed).then_inc(S("ffn_scaled"), 1)
            dve.wait_ge(S("ffn_scaled"), 1)
            for m in range(KT):
                x = normed[:, m * T:m * T + T]
                last = dve.tensor_scalar(x, x, mod[:, 3 * KT + m:3 * KT + m + 1], None, ALU.add)
            last.then_inc(S("h_full"), 1)
            split_h_lo(dve, 1)

            def ffn_tile(t, p, s):
                for half in range(2):
                    z = psum[4 + 2 * half + p]
                    x = conv[p][half]
                    dve.wait_ge(S("conv_mid"), t * 2 + (1 + half))
                    dve.scalar_tensor_tensor(x[:, 1:T], z[:, 0:T - 1], p1("conv_w", t + half * JF), x[:, 1:T],
                                             ALU.mult, ALU.add).then_inc(S("conv_left"), 1)
                for half in range(2):
                    z = psum[4 + 2 * half + p]
                    x = conv[p][half]
                    dve.wait_ge(S("conv_left"), t * 2 + (1 + half))
                    dve.scalar_tensor_tensor(x[:, 0:T - 1], z[:, 1:T], p1("conv_w", t + (4 * JF + half * JF)), x[:, 0:T - 1],
                                             ALU.mult, ALU.add).then_inc(S("conv"), 1)
                dve.wait_ge(S("conv"), t * 2 + 2)
                dve.wait_ge(S("f_silu"), t + 1)
                dve.tensor_tensor(u_f[p], f_silu[p], conv[p][1], ALU.mult).then_inc(S("u_full"), 1)
                dve.wait_ge(S("u_hi"), t + 1)
                dve.tensor_tensor(y_lo[:, s * T:s * T + T], u_f[p], y_hi[:, s * T:s * T + T].bitcast(F32),
                                  ALU.subtract).then_inc(S("u_lo"), 1)

            for j in range(FFN_PEEL):
                c = ffn_first(j)
                lo(dve, Chunk(c, AHEAD))
                lo(dve, Chunk(c, 1 + AHEAD))
                if j >= 1:
                    ffn_tile(j - 1, (j - 1) % 2, (j - 1) % 4)
                if j >= 2:
                    lo(dve, Chunk(c, 2 + AHEAD))
            with dve.Fori(0, (JF - FFN_PEEL) // 4) as i:
                for u in range(4):
                    lo(dve, Chunk(ffn_first(FFN_PEEL), 3 * u + AHEAD, i, 12))
                    lo(dve, Chunk(ffn_first(FFN_PEEL), 3 * u + 1 + AHEAD, i, 12))
                    t = FFN_PEEL + u - 1
                    ffn_tile(i * 4 + t, t % 2, t % 4)
                    lo(dve, Chunk(ffn_first(FFN_PEEL), 3 * u + 2 + AHEAD, i, 12))
            lo(dve, Chunk(N_IN2 - 2, AHEAD))
            ffn_tile(JF - 1, (JF - 1) % 2, (JF - 1) % 4)
            lo(dve, Chunk(N_IN2 - 1, AHEAD))
            add_product(dve, lambda m: mod[:, 5 * KT + m:5 * KT + m + 1], N_IN2, LOW_BANKS)
            norm_mean(dve, 1)
            scale_residual(dve, 1, lambda m: p1("final", m), xres).then_inc(S("residual"), 1)
            norm_mean(dve, 2)
            scale_residual(dve, 2, lambda m: p1("pre_mix", m), normed).then_inc(S("h_full"), 1)
            split_h_lo(dve, 2)

            def values2(t):
                v = v_index(t)
                dve.wait_ge(S("v2_turned"), v + 1)
                z = psum[4 + v % 2][:, 0:T]
                if v == 0:
                    dve.tensor_copy(s_v, z).then_inc(S("v2"), 1)
                else:
                    x = (v - 1) * P
                    dve.tensor_copy(split2(r_v)[:, :, x:x + P], split2(z)).then_inc(S("v2"), 1)

            def centre_values():
                x = r_v.rearrange("p (n e) -> p n e", e=R_DV)
                dve.wait_ge(S("v2"), 9)
                dve.tensor_reduce(v_mean, x, AX, ALU.add).then_inc(S("v_sum"), 1)
                dve.wait_ge(S("v_sum"), 1)
                dve.tensor_scalar(v_mean, v_mean, 1.0 / R_DV, None, ALU.mult).then_inc(S("v_mean"), 1)
                dve.wait_ge(S("v_mean"), 1)
                dve.tensor_tensor(x, x, v_mean.rearrange("p (n o) -> p n o", o=1).broadcast_to([P, 8, R_DV]),
                                  ALU.subtract).then_inc(S("v_centred"), 1)

            def gates(t):
                n = t - T_GR + 1
                x = gate_dst(t)
                dve.wait_ge(S("gate_exp"), n)
                dve.tensor_scalar(x, x, 1.0, None, ALU.add).then_inc(S("gate_1"), 1)
                dve.wait_ge(S("gate_1"), n)
                if t >= T_GS:
                    dve.reciprocal(x, x).then_inc(S("gate"), 1)
                    return
                dve.reciprocal(x, x).then_inc(S("gate_r"), 1)
                dve.wait_ge(S("gate_r"), n)
                dve.tensor_tensor(x, psum[t % 4][:, 0:T], x, ALU.mult).then_inc(S("gate"), 1)

            def softmax_max(e):
                p = e % 2
                slope = 2.0 ** (-8.0 / S_HEADS * (e + 1))
                dve.wait_ge(S("s_scores"), e + 1)
                if e >= 2:
                    dve.wait_ge(S("s_exp"), 3 * (e - 1))
                dve.scalar_tensor_tensor(s_b[p], dist, -slope * S_DH ** 0.5, psum[5 + p][:, 0:3 * P], ALU.mult,
                                         ALU.add).then_inc(S("s_biased"), 1)
                dve.wait_ge(S("s_biased"), e + 1)
                dve.reduce_max(s_max[p][:, 0:1], s_b[p][:, 0:P], AX)
                dve.reduce_max(s_max[p][:, 1:2], s_b[p][:, P:3 * P], AX).then_inc(S("s_max"), 1)
                dve.wait_ge(S("s_max"), e + 1)
                dve.tensor_scalar(s_neg[p], s_max[p], -(S_DH ** -0.5), sink_neg[:, e:e + 1], ALU.mult,
                                  ALU.min).then_inc(S("s_neg"), 1)

            def softmax_norm(e):
                p = e % 2
                dve.wait_ge(S("s_exp"), 3 * e + 3)
                dve.tensor_tensor(s_den[p], s_sum[p], s_sink[p], ALU.add).then_inc(S("s_den"), 1)
                dve.wait_ge(S("s_den"), e + 1)
                dve.reciprocal(s_den[p], s_den[p]).then_inc(S("s_rden"), 1)
                dve.wait_ge(S("s_rden"), e + 1)
                for x, b in ((slice(0, P), 0), (slice(P, 3 * P), 1)):
                    dve.tensor_scalar(s_p[p][:, x], s_p[p][:, x], s_den[p][:, b:b + 1], None, ALU.mult).then_inc(S("p_norm"), 1)

            def swa_copy(e):
                q = S_DH * (e % 2)
                dve.wait_ge(S("pv"), e + 1)
                dve.tensor_copy(swa[q:q + S_DH, (e // 2) * T:(e // 2 + 1) * T], psum[4][q:q + S_DH, 0:T]).then_inc(S("swa"), 1)

            def ret_decay(r):
                dve.wait_ge(S("r_scores"), r + 1)
                if r >= 2:
                    dve.wait_ge(S("r_o"), r - 1)
                x = CON["decay"] + 3 * P * r
                dve.tensor_tensor(r_sc[r % 2], psum[5 + r % 2][:, 0:3 * P], con[:, x:x + 3 * P], ALU.mult).then_inc(S("r_sc"), 1)

            def ret_norm(r):
                dve.wait_ge(S("r_summed"), r + 1)
                dve.tensor_scalar(r_rs, psum[7][:, 0:T], 1.0 / R_DV, EPS, ALU.mult, ALU.add).then_inc(S("r_mean"), 1)
                dve.wait_ge(S("r_rstd"), r + 1)
                dve.tensor_tensor(split2(r_t), split2(psum[4][:, :]), over_tiles(r_rs, 2), ALU.mult).then_inc(S("r_normed"), 1)
                dve.wait_ge(S("r_normed"), r + 1)
                dve.tensor_tensor(r_t, r_t, silu_g[:, 2 * r * T:2 * (r + 1) * T], ALU.mult).then_inc(S("r_full"), 1)
                dve.wait_ge(S("r_hi"), r + 1)
                dve.tensor_tensor(y_lo[:, 2 * r * T:2 * (r + 1) * T], r_t, y_hi[:, 2 * r * T:2 * (r + 1) * T].bitcast(F32),
                                  ALU.subtract).then_inc(S("r_lo"), 1)

            dve.tensor_scalar(sink_neg, sink[:, :], -1.0, None, ALU.mult).then_inc(S("sink_neg"), 1)
            dve.wait_ge(S("sink_neg"), 1)
            for t in range(TILES_IN2 + 1):
                if t < TILES_IN2:
                    lo(dve, Chunk(N_IN2, t + AHEAD))
                if t >= 2 and v_index(t - 2) is not None:
                    values2(t - 2)
                if t == T_GR + 2:
                    centre_values()
                if t - 1 >= T_GR:
                    gates(t - 1)
                e = t - T_GR
                if 3 <= e <= S_HEADS + 2:
                    swa_copy(e - 3)
                if 1 <= e <= S_HEADS:
                    softmax_norm(e - 1)
                if 0 <= e < S_HEADS:
                    softmax_max(e)
                if e == S_HEADS + 3:
                    dve.wait_ge(S("swa_hi"), 1)
                    dve.tensor_tensor(h_lo[:, 8 * T:12 * T], swa, h_hi[:, 8 * T:12 * T].bitcast(F32),
                                      ALU.subtract).then_inc(S("swa_lo"), 1)
                r = t - RET_FIRST
                if r >= 3 and r % 2 == 1 and (r - 3) // 2 < R_HEADS:
                    ret_norm((r - 3) // 2)
                if 0 <= r < 2 * R_HEADS and r % 2 == 0:
                    ret_decay(r // 2)
            for n in range(N_SOUT, N_MOUT):
                lo(dve, Chunk(n, AHEAD))
                if n == N_ROUT:
                    dve.wait_ge(S("multiplied"), N_ROUT)
                    for b in range(4):
                        x = gate_s[:, b * 512:b * 512 + 512]
                        last = dve.tensor_tensor(x, psum[HIGH_BANKS[b]][:, :], x, ALU.mult)
                    last.then_inc(S("swa_gated"), 1)
            dve.wait_ge(S("swa_gated"), 1)
            dve.wait_ge(S("multiplied"), N_MOUT)
            for b in range(4):
                x = gate_r[:, b * 512:b * 512 + 512]
                dve.tensor_tensor(x, psum[b][:, :], x, ALU.mult).then_inc(S("ret_gated"), 1)
                dve.wait_ge(S("ret_gated"), b + 1)
                dve.tensor_tensor(x, x, gate_s[:, b * 512:b * 512 + 512], ALU.add).then_inc(S("mg_full"), 1)
                dve.wait_ge(S("mg_hi"), b + 1)
                dve.tensor_tensor(h_lo[:, b * 512:b * 512 + 512], x, h_hi[:, b * 512:b * 512 + 512].bitcast(F32),
                                  ALU.subtract).then_inc(S("mg_lo"), 1)
                lo(dve, Chunk(N_MOUT, b + AHEAD))
            for n in range(N_MOUT + 4, N_MLP):
                lo(dve, Chunk(n, AHEAD))
            norm_mean(dve, 3, bank=0)
            add_normed_product(dve, 3, lambda m: p1("post_mix", m), 1, HIGH_BANKS)
            norm_mean(dve, 4)
            scale_residual(dve, 4, lambda m: p1("pre_mlp", m), normed).then_inc(S("h_full"), 1)
            split_h_lo(dve, 3)

            def mlp_tile(t, p, s):
                dve.wait_ge(S("m_relu"), t + 1)
                dve.tensor_tensor(u_f[p], m_relu[p], m_relu[p], ALU.mult).then_inc(S("m_full"), 1)
                dve.wait_ge(S("m_hi"), t + 1)
                dve.tensor_tensor(y_lo[:, s * T:s * T + T], u_f[p], y_hi[:, s * T:s * T + T].bitcast(F32),
                                  ALU.subtract).then_inc(S("m_lo"), 1)

            for j in range(MLP_PEEL):
                lo(dve, Chunk(mlp_first(j), AHEAD))
                if j >= 1:
                    mlp_tile(j - 1, (j - 1) % 2, (j - 1) % 4)
                if j >= 2:
                    lo(dve, Chunk(mlp_first(j), 1 + AHEAD))
            with dve.Fori(0, (JM - MLP_PEEL) // 4 - 1) as i:
                for u in range(4):
                    lo(dve, Chunk(mlp_first(MLP_PEEL), 2 * u + AHEAD, i, 8))
                    t = MLP_PEEL + u - 1
                    mlp_tile(i * 4 + t, t % 2, t % 4)
                    lo(dve, Chunk(mlp_first(MLP_PEEL), 2 * u + 1 + AHEAD, i, 8))
            for j in range(JM - 4, JM):
                lo(dve, Chunk(mlp_first(j), AHEAD))
                mlp_tile(j - 1, (j - 1) % 2, (j - 1) % 4)
                lo(dve, Chunk(mlp_first(j), 1 + AHEAD))
            mlp_tile(JM - 1, (JM - 1) % 2, (JM - 1) % 4)
            norm_mean(dve, 5)
            add_normed_product(dve, 5, lambda m: p1("post_mlp", m), 2, LOW_BANKS)


def _columns(w):
    n = w.shape[1]
    return w.reshape(KT, P, n // P, P).transpose(2, 1, 0, 3).reshape(n // P, P, D)


def _rows(w):
    return w.reshape(-1, P, D)


def _vec(v):
    return v.reshape(-1, P).T


def _tiles(x):
    return x.T.reshape(KT, P, -1).transpose(1, 0, 2)


def kernel(**inputs):
    import concourse.bacc as bacc
    from concourse.bass_utils import run_bass_kernel_spmd as run

    a = {k: np.asarray(v) for k, v in inputs.items()}
    x, ctx = _tiles(a["x"][0]), _tiles(a["ctx"][0])
    tok = np.concatenate([x, ctx], axis=2).reshape(P, KT * TC)
    cc = np.stack([_vec(a["c"][0]), _vec(a["c_ctx"])], axis=2).reshape(P, 2 * KT)
    ada = _columns(a["w_ada"][0])

    hg = _columns(a["hg_w_in"][0]).reshape(5, HEADS, P, D)
    heads = np.stack([hg[1], hg[2], hg[0], hg[4]], axis=1).reshape(4 * HEADS, P, D)
    up = _columns(a["ffn_w_up"][0]).reshape(2, JF, P, D)
    down = _rows(a["ffn_w_down"][0])
    ffn = []
    for j in range(JF + 2):
        ffn += [up[0, j], up[1, j]] if j < JF else []
        ffn += [down[j - 2]] if j >= 2 else []
    w2 = a["w_in_2"][0]
    edges = np.cumsum([0, 512, 512, 1024, 1024, 512, 128, 128, D, D])
    r_q, r_k, r_v, r_g, s_q, s_k, s_v, g_r, g_s = (w2[:, i:j] for i, j in zip(edges[:-1], edges[1:]))
    s_q = s_q.reshape(D, 2, 4, S_DH).transpose(0, 2, 1, 3).reshape(D, 512)
    in2 = _columns(np.concatenate([s_q, s_k, s_v, r_q, r_k, r_v, r_g, g_s, g_r], axis=1))
    up2, down2 = _columns(a["w_up_2"][0]), _rows(a["w_down_2"][0])
    mlp = []
    for j in range(JM + 2):
        mlp += [up2[j]] if j < JM else []
        mlp += [down2[j - 2]] if j >= 2 else []
    stream = np.concatenate([hg[3], heads, _rows(a["hg_w_out"][0]), np.stack(ffn), in2, _rows(a["w_swa_out_2"][0]),
                             _rows(a["w_ret_out_2"][0]), _rows(a["w_out_2"][0]), np.stack(mlp)])
    lb = a["hg_lb_logits"]
    par = np.concatenate([_vec(v) for v in (
        a["norm_g"][0, 0], a["norm_g"][0, 1], a["b_ada"][0], lb[0], lb[1], a["hg_gnorm"][0], a["ffn_conv_w"][0],
        a["ffn_conv_b"][0], a["final_g"], a["pre_mix_norm_2"][0], a["post_mix_norm_2"][0], a["pre_mlp_norm_2"][0],
        a["post_mlp_norm_2"][0])], axis=1)
    con, msk = constants()
    arrays = {"tok": tok, "cc": cc, "ada": ada.reshape(ADA * P, D), "stream": stream.reshape(N_ALL * P, D), "par": par,
              "con": con, "msk": msk, "sink": a["sinks_2"][0]}
    arrays = {"in_" + k: np.ascontiguousarray(v) for k, v in arrays.items()}

    nc = bacc.Bacc("TRN2", target_bir_lowering=False, num_devices=1)
    args = [nc.dram_tensor(k, v.shape, mybir.dt.from_np(v.dtype), kind="ExternalInput").ap() for k, v in arrays.items()]
    args.append(nc.dram_tensor("out", (P, KT * T), F32, kind="ExternalOutput").ap())
    build(nc, *args)
    y = run(nc, [arrays], core_ids=[0]).results[0]["out"]
    return np.ascontiguousarray(y.reshape(P, KT, T).transpose(2, 1, 0).reshape(1, T, D))
```

```python
from contextlib import ExitStack

import numpy as np

import concourse.bass as bass
from concourse import mybir

F32 = mybir.dt.float32
F32R = mybir.dt.float32r
I32 = mybir.dt.int32
ACT = mybir.ActivationFunctionType
ALU = mybir.AluOpType
AX = mybir.AxisListType.X

P = 128
D = 1024
KT = D // P
T = 256
TC = 2 * T
EPS = 1e-6
RING = 4
AHEAD = 2
ADA = 6 * KT
ADA_FIRST = 2 * KT
GROUPS = 3
HEADS = 8
CH = 64
HALF = CH // 2
NCH = T // CH
D_FF = 2816
JF = D_FF // P
R_HEADS = 4
R_DV = 256
S_HEADS = 8
S_DH = 64
D_FF2 = 4096
JM = D_FF2 // P

N_V = 0
N_HEAD = N_V + HEADS
N_HOUT = N_HEAD + 4 * HEADS
N_FFN = N_HOUT + KT
N_IN2 = N_FFN + 3 * JF
TILES_IN2 = 46
N_SOUT = N_IN2 + TILES_IN2
N_ROUT = N_SOUT + 4
N_MOUT = N_ROUT + KT
N_MLP = N_MOUT + KT
N_ALL = N_MLP + 2 * JM

T_QS, T_KS, T_VS, T_QR, T_KR, T_VR, T_GR, T_GS, T_GT = 0, 4, 5, 6, 10, 14, 22, 30, 38

PAR = {}
_at = 0
for _name, _n in (("norm1", 8), ("norm2", 8), ("b_ada", 48), ("lb0", 16), ("lb1", 16), ("gnorm", 1),
                  ("conv_w", 3 * 2 * JF), ("conv_b", 2 * JF), ("final", 8), ("pre_mix", 8),
                  ("post_mix", 8), ("pre_mlp", 8), ("post_mlp", 8)):
    PAR[_name] = _at
    _at += _n
N_PAR = _at

CON = {"ident": 0, "ones": P, "scan": 2 * P, "decay": 2 * P + 2 * TC, "dist": 2 * P + 2 * TC + 3 * P * R_HEADS}
N_CON = CON["dist"] + 3 * P
ARENA = 14080
FAR = 1e30


def constants():
    c = np.zeros((P, N_CON), np.float32)
    c[:, 0:P] = np.eye(P)
    c[:, P:2 * P] = 1.0
    scan = np.ones(TC, np.float32)
    scan[0:T:CH] = 0.0
    scan[T] = 0.0
    c[:, CON["scan"]:CON["scan"] + TC] = scan
    c[:, CON["scan"] + TC:CON["scan"] + 2 * TC] = np.roll(scan, T)
    j = np.arange(P)[:, None]
    i = np.arange(T)[None, :]
    for h in range(R_HEADS):
        lg = np.log(np.float32(1.0) - np.exp2(np.float32(-5.0 - h)))
        d0 = np.where(i >= j, np.exp(lg * np.maximum(i - j, 0)), 0.0)
        at = CON["decay"] + 3 * P * h
        c[:, at:at + T] = d0 * P ** -0.5
        c[:, at + T:at + 3 * P] = d0[:, :P] * P ** -0.5
    q = np.arange(P)[:, None]
    k = np.arange(P)[None, :]
    own = np.where(k <= q, q - k, FAR)
    prev = np.where(k > q, q + P - k, FAR)
    c[:, CON["dist"]:] = np.concatenate([own, prev, own], axis=1)
    j, i = np.arange(CH)[:, None], np.arange(CH)[None, :]
    m = np.zeros((2, CH, 2, 2, CH), np.int32)
    m[:, :, 0] = (j <= i).astype(np.int32)[None, :, None, :]
    m[:, :, 1] = (j >= i).astype(np.int32)[None, :, None, :]
    return c, m.reshape(P, 4 * CH)


HOUT_BANKS = (0, 1, 2, 4)
LOW_BANKS = (0, 1, 2, 3)
HIGH_BANKS = (4, 5, 6, 7)
FFN_PEEL = 6
MLP_PEEL = 4
RET_FIRST = T_GS + 1


def ffn_first(j):
    return N_FFN + (2 * j if j < 2 else 3 * j - 2)


def mlp_first(j):
    return N_MLP + (j if j < 2 else 2 * j - 2)


def v_index(t):
    return 0 if t == T_VS else t - T_VR + 1 if T_VR <= t < T_GR else None


class Chunk:

    def __init__(self, base, m=0, i=0, per=0):
        assert per % RING == 0
        self.n = i * per + (base + m)
        self.slot = (base + m) % RING
        self.round = i * (per // RING) + (base + m) // RING
        self.least = base + m


def build(nc, tok_in, cc_in, ada_in, stream_in, par_in, con_in, msk_in, sink_in, out):
    ctx = ExitStack()
    with ctx:
        def sb(name, cols, dt=F32):
            return ctx.enter_context(nc.sbuf_tensor(name, [P, cols], dt))

        sems = {}

        def S(name):
            if name not in sems:
                sems[name] = ctx.enter_context(nc.semaphore(name))
            return sems[name]

        raw = [sb(f"raw{i}", D) for i in range(RING)]
        w_hi = [sb(f"w_hi{i}", D, F32R) for i in range(RING)]
        w_lo = [sb(f"w_lo{i}", D, F32R) for i in range(RING)]
        con = sb("con", N_CON)
        msk = sb("msk", 4 * CH, I32)
        par = sb("par", N_PAR)
        sink = sb("sink", S_HEADS)
        cc = sb("cc", 2 * KT)
        xres = sb("xres", KT * T)
        tok = sb("tok", KT * TC)
        wide = sb("wide", KT * TC)
        h_hi = sb("h_hi", KT * TC, F32R)
        h_lo = sb("h_lo", KT * TC, F32R)
        y_hi = sb("y_hi", KT * T, F32R)
        y_lo = sb("y_lo", KT * T, F32R)
        small = sb("small", 512)
        arena = sb("arena", ARENA)
        psum = [ctx.enter_context(nc.psum_tensor(f"bank{i}", [P, 512], F32)) for i in range(8)]

        ident = con[:, 0:P]
        ones = con[:, P:2 * P]
        scan_mask = [con[:, CON["scan"] + d * TC:CON["scan"] + (d + 1) * TC] for d in range(2)]
        dist = con[:, CON["dist"]:CON["dist"] + 3 * P]

        used = [0]

        def part(cols):
            used[0] += cols
            assert used[0] <= ARENA
            return arena[:, used[0] - cols:used[0]]

        def p1(name, k=0, n=1):
            return par[:, bass.ds(k + PAR[name], n)]

        used_small = [0]

        def tiny(cols):
            used_small[0] += cols
            assert used_small[0] <= 512
            return small[:, used_small[0] - cols:used_small[0]]

        cs = tiny(2 * KT)
        cs_e = tiny(2 * KT)
        lb = tiny(16)
        lb_om = tiny(16)
        lb_m = tiny(16)
        lb_d = tiny(32)
        mod = tiny(ADA)
        mod_c = tiny(ADA_FIRST)
        gain_l = tiny(KT)
        gain_c = tiny(KT)
        gain_2 = tiny(KT)
        sink_neg = tiny(S_HEADS)
        s_max = [tiny(2) for _ in range(2)]
        s_neg = [tiny(2) for _ in range(2)]
        s_sum = [tiny(2) for _ in range(2)]
        s_sink = [tiny(2) for _ in range(2)]
        s_den = [tiny(2) for _ in range(2)]
        v_mean = tiny(8)

        rstd = part(TC)
        f_buf = part(2 * TC)
        b_buf = part(2 * TC)
        k_buf = part(2 * TC)
        q_e = part(2 * T)
        q_d = [part(2 * T) for _ in range(2)]
        k_e = part(2 * T)
        k_d = part(2 * TC)
        qg = [part(2 * T) for _ in range(2)]
        k_dT = part(8 * P)
        state = part(8 * P)
        sc_T = part(8 * CH)
        v_cur = part(4 * P)
        o_sq = part(T)
        o_rs = part(T)
        o_n = part(T)
        y_f = part(T)
        gate2_sum = part(D)
        gate2_raw = part(D)
        used[0] = TC
        mod_sum = [part(D) for _ in range(GROUPS)]
        mod_raw = [part(D) for _ in range(2 * GROUPS)]
        assert used[0] <= 9728
        mod_rows = mod_raw[0]
        mod_rows2 = mod_raw[1]
        used[0] = TC
        conv = [[part(T) for _ in range(2)] for _ in range(2)]
        f_silu = [part(T) for _ in range(2)]
        u_f = [part(T) for _ in range(2)]
        m_relu = [part(T) for _ in range(2)]
        used[0] = TC
        s_q = part(4 * T)
        s_k = part(T)
        s_v = part(T)
        r_q = part(4 * T)
        r_k = part(4 * T)
        r_v = part(8 * T)
        gate_r = part(8 * T)
        s_b = [part(3 * P) for _ in range(2)]
        s_p = [part(3 * P) for _ in range(2)]
        s_pT = [part(3 * P) for _ in range(2)]
        swa = part(4 * T)
        r_sc = [part(3 * P) for _ in range(2)]
        r_t = part(2 * T)
        r_sq = part(2 * T)
        r_rs = part(T)
        v_tmp = [part(T) for _ in range(2)]
        silu_g = tok[:, 0:KT * T]
        gate_s = tok[:, KT * T:2 * KT * T]

        def in2_dst(t):
            for first, n, dst in ((T_QS, 4, s_q), (T_KS, 1, s_k), (T_QR, 4, r_q), (T_KR, 4, r_k)):
                if first <= t < first + n:
                    return dst[:, (t - first) * T:(t - first + 1) * T]
            return None

        def gate_dst(t):
            dst, k = (silu_g, t - T_GR) if t < T_GS else (gate_s, t - T_GS) if t < T_GT else (gate_r, t - T_GT)
            return dst[:, k * T:(k + 1) * T]

        d1 = wide[:, 0:2 * T]
        qg_s = wide[:, 3072:3584]
        e_qe = wide[:, 512:1024]
        e_ke = wide[:, 1024:1536]
        e_qd = wide[:, 1536:2048]
        e_kd = wide[:, 2048:3072]
        v_T = [wide[:, 3072:3584], wide[:, 3584:4096]]

        def kv_at(d, s):
            c = s - 1 if d == 0 else NCH - s
            col = 0 if s == 0 else {(0, 1): 1, (0, 3): 2, (1, 2): 3, (0, 2): 1, (1, 1): 2, (1, 3): 3}[d, s]
            return psum[6 + (d if s == 0 else c % 2)][:, col * P:(col + 1) * P]

        v_all = tok

        def hi(act, c):
            if c.least >= N_ALL:
                return
            act.wait_ge(S(f"loaded{c.slot}"), c.round * 16 + 16 * (ADA_FIRST // RING + 1))
            if c.least >= RING:
                act.wait_ge(S("multiplied"), c.n - (RING - 1))
            act.activation(w_hi[c.slot][:, :], raw[c.slot][:, :], ACT.Copy).then_inc(S("split_hi"), 1)

        def lo(dve, c):
            if c.least >= N_ALL:
                return
            dve.wait_ge(S("split_hi"), c.n + 1)
            dve.tensor_tensor(w_lo[c.slot][:, :], raw[c.slot][:, :], w_hi[c.slot][:, :].bitcast(F32),
                              ALU.subtract).then_inc(S("split_lo"), 1)

        def three(pe, dst, w, cols, a_hi, a_lo, start, stop):
            hi_w, lo_w = w_hi[w][:, cols], w_lo[w][:, cols]
            pe.matmul(dst, hi_w, a_hi, start=start, stop=False, skip_group_check=True)
            pe.matmul(dst, hi_w, a_lo, start=False, stop=False, skip_group_check=True)
            return pe.matmul(dst, lo_w, a_hi, start=False, stop=stop, skip_group_check=True)

        def column_tile(pe, c, dst, width, n_tok, input_tiles=None, halfway=None):
            pe.wait_ge(S("split_lo"), c.n + 1)
            for k in range(KT):
                if input_tiles is not None:
                    pe.wait_ge(S("h_lo"), input_tiles + k + 1)
                last = three(pe, dst, c.slot, slice(k * P, k * P + P), h_hi[:, k * width:k * width + n_tok],
                             h_lo[:, k * width:k * width + n_tok], k == 0, k == KT - 1)
                if halfway is not None and k == KT // 2 - 1:
                    halfway()
            last.then_inc(S("multiplied"), 1)

        def row_tile(pe, c, banks, a_hi, a_lo, first, stop):
            pe.wait_ge(S("split_lo"), c.n + 1)
            for m in range(KT):
                last = three(pe, psum[banks[m // 2]][:, (m % 2) * T:(m % 2) * T + T], c.slot,
                             slice(m * P, m * P + P), a_hi, a_lo, first and m % 2 == 0, stop)
            last.then_inc(S("multiplied"), 1)

        def log_exp_tables(act):
            act.preload_act_table_set("natural_log_exp_and_others")

        def by_tile(x, n=KT):
            return x.rearrange("p (k t) -> p k t", k=n)

        def over_tiles(x, n=KT):
            return x.rearrange("p (o t) -> p o t", o=1).broadcast_to([P, n, x.shape[1]])

        def norm_sum(pe, k, bank=7):
            for m in range(KT):
                pe.wait_ge(S("norm_squares"), k * KT + m + 1)
                last = pe.matmul(psum[bank][:, 0:T], ones, wide[:, m * T:m * T + T], start=m == 0, stop=m == KT - 1)
            last.then_inc(S("norm_summed"), 1)

        def norm_mean(dve, k, bank=7):
            dve.wait_ge(S("norm_summed"), k + 1)
            dve.tensor_scalar(rstd[:, 0:T], psum[bank][:, 0:T], 1.0 / D, EPS, ALU.mult, ALU.add).then_inc(S("norm_mean"), 1)

        def norm_rstd(act, k):
            act.wait_ge(S("norm_mean"), k + 1)
            act.activation(rstd[:, 0:T], rstd[:, 0:T], ACT.Ln).then_inc(S("norm_log"), 1)
            act.wait_ge(S("norm_log"), k + 1)
            act.activation(rstd[:, 0:T], rstd[:, 0:T], ACT.Exp, scale=-0.5).then_inc(S("norm_rstd"), 1)

        def square_residual(act, update):
            for m in range(KT):
                act.wait_ge(S("residual"), update * KT + m + 1)
                act.activation(wide[:, m * T:m * T + T], xres[:, m * T:m * T + T], ACT.Square).then_inc(S("norm_squares"), 1)

        def square_banks(act, n_done, banks):
            act.wait_ge(S("multiplied"), n_done)
            for b in range(4):
                act.activation(wide[:, b * 512:b * 512 + 512], psum[banks[b]][:, :], ACT.Square).then_inc(S("norm_squares"), 2)

        normed = wide[:, KT * T:2 * KT * T]

        def scale_residual(dve, k, gain):
            dve.wait_ge(S("norm_rstd"), k + 1)
            for m in range(KT):
                x = xres[:, m * T:m * T + T]
                dve.scalar_tensor_tensor(x, x, gain(m), rstd[:, 0:T], ALU.mult, ALU.mult).then_inc(S("residual"), 1)

        def split_h_hi(act, q, shift=None):
            for m in range(KT):
                act.wait_ge(S("h_full"), (q - 1) * KT + m + 1)
                x, dst = normed[:, m * T:m * T + T], h_hi[:, m * T:m * T + T]
                if shift is None:
                    act.activation(dst, x, ACT.Copy).then_inc(S("h_hi"), 1)
                else:
                    act.activation(dst, x, ACT.Identity, bias=shift(m)).then_inc(S("h_hi"), 1)

        def norm_input(dve, k, q, gain, shift=None):
            dve.wait_ge(S("norm_rstd"), k + 1)
            behind = 2
            for m in range(KT + behind):
                if m < KT:
                    dve.scalar_tensor_tensor(normed[:, m * T:m * T + T], xres[:, m * T:m * T + T], gain(m), rstd[:, 0:T],
                                             ALU.mult, ALU.mult).then_inc(S("h_full"), 1)
                if m >= behind:
                    t = m - behind
                    x, dst = normed[:, t * T:t * T + T], h_lo[:, t * T:t * T + T]
                    high = h_hi[:, t * T:t * T + T].bitcast(F32)
                    dve.wait_ge(S("h_hi"), q * KT + t + 1)
                    if shift is None:
                        dve.tensor_tensor(dst, x, high, ALU.subtract).then_inc(S("h_lo"), 1)
                    else:
                        dve.scalar_tensor_tensor(dst, x, shift(t), high, ALU.add, ALU.subtract).then_inc(S("h_lo"), 1)

        def add_product(dve, gain, n_done, banks):
            dve.wait_ge(S("multiplied"), n_done)
            for m in range(KT):
                x = xres[:, m * T:m * T + T]
                dve.scalar_tensor_tensor(x, psum[banks[m // 2]][:, (m % 2) * T:(m % 2) * T + T], gain(m), x,
                                         ALU.mult, ALU.add).then_inc(S("residual"), 1)

        def add_normed_product(dve, k, gain, count, banks):
            dve.wait_ge(S("norm_rstd"), k + 1)
            for m in range(KT + 1):
                if m < KT:
                    dve.scalar_tensor_tensor(normed[:, m * T:m * T + T], psum[banks[m // 2]][:, (m % 2) * T:(m % 2) * T + T],
                                             gain(m), rstd[:, 0:T], ALU.mult, ALU.mult).then_inc(S("product_normed"), 1)
                if m >= 1:
                    dve.wait_ge(S("product_normed"), count * KT + m)
                    x = xres[:, (m - 1) * T:m * T]
                    dve.tensor_tensor(x, x, normed[:, (m - 1) * T:m * T], ALU.add).then_inc(S("residual"), 1)

        block = ctx.enter_context(nc.Block())

        @block.sync
        def _(sp):
            def load(src, row, slot):
                sp.dma_start(raw[slot][:, :], src[bass.ds(row, P), :]).then_inc(S(f"loaded{slot}"), 16)

            for a in range(RING):
                load(ada_in, a * P, a)
            with sp.Fori(1, ADA_FIRST // RING) as i:
                for u in range(RING):
                    sp.wait_ge(S("ada_done"), i * RING + (u + 1 - RING))
                    load(ada_in, i * (RING * P) + u * P, u)
            for n in range(RING):
                sp.wait_ge(S("ada_done"), ADA_FIRST - RING + 1 + n)
                load(stream_in, n * P, n)
            for h in range(HEADS):
                for g in range(GROUPS):
                    n = GROUPS * h + g
                    slot = n % (2 * GROUPS)
                    if h >= 2:
                        sp.wait_ge(S("mod_summed"), n - 2 * GROUPS + 1)
                    elif slot < 2:
                        sp.wait_ge(S("mod_turned"), 2)
                    sp.dma_start(mod_raw[slot], ada_in[(ADA_FIRST + n) * P:(ADA_FIRST + n + 1) * P, :]).then_inc(
                        S(f"mod_loaded{slot}"), 16)
                sp.wait_ge(S("split_lo"), h + 1)
                load(stream_in, (RING + h) * P, (RING + h) % RING)
            gate2_row = (ADA_FIRST + GROUPS * KT) * P

            def load_stream(i):
                for u in range(RING):
                    sp.wait_ge(S("split_lo"), i * RING + (u + 1 - RING))
                    load(stream_in, i * (RING * P) + u * P, u)

            i_head = (RING + HEADS) // RING
            sp.dma_start(gate2_raw, ada_in[gate2_row:gate2_row + P, :]).then_inc(S("gate2_in"), 16)
            load_stream(i_head)
            with sp.Fori(1, HEADS) as h:
                sp.wait_ge(S("gate2_summed"), h)
                sp.dma_start(gate2_raw, ada_in[bass.ds(h * P + gate2_row, P), :]).then_inc(S("gate2_in"), 16)
                load_stream(h + i_head)
            with sp.Fori(i_head + HEADS, N_ALL // RING) as i:
                load_stream(i)
            for half in range(2):
                x = slice(half * 4 * T, half * 4 * T + 4 * T)
                sp.wait_ge(S("residual"), 4 * KT + 4 * half + 4)
                sp.dma_start(out[:, x], xres[:, x]).then_inc(S("stored"), 16)
            sp.wait_ge(S("stored"), 32)

        @block.scalar
        def _(act):
            act.dma_start(cc[:, :], cc_in).then_inc(S("cc_in"), 16)
            act.dma_start(con[:, 0:2 * P], con_in[:, 0:2 * P]).then_inc(S("con_in"), 16)
            for b in range(4):
                x = slice(b * 2 * TC, (b + 1) * 2 * TC)
                act.dma_start(tok[:, x], tok_in[:, x]).then_inc(S(f"tok_in{b}"), 16)
            act.dma_start(par[:, :], par_in).then_inc(S("par_in"), 16)

            log_exp_tables(act)
            act.wait_ge(S("cc_in"), 16)
            act.activation(cs_e, cc[:, :], ACT.Exp, scale=-1.0).then_inc(S("cs_exp"), 1)
            for b in range(4):
                x = slice(b * 2 * TC, (b + 1) * 2 * TC)
                act.wait_ge(S(f"tok_in{b}"), 16)
                act.activation(wide[:, x], tok[:, x], ACT.Square).then_inc(S("tok_squares"), 1)
            act.wait_ge(S("lb_diff"), 1)
            act.activation(lb_d, lb_d, ACT.Exp).then_inc(S("lb_exp"), 1)
            act.wait_ge(S("tok_mean"), 1)
            act.activation(rstd, rstd, ACT.Ln).then_inc(S("tok_log"), 1)
            act.wait_ge(S("tok_log"), 1)
            act.activation(rstd, rstd, ACT.Exp, scale=-0.5).then_inc(S("tok_rstd"), 1)
            for a, rows in enumerate((mod_rows, mod_rows2)):
                act.wait_ge(S("ada_done"), (a + 1) * KT)
                for b in range(2):
                    act.activation(rows[0:2, b * 512:b * 512 + 512], psum[4 + 2 * a + b][0:2, :],
                                   ACT.Copy).then_inc(S("mod_rows"), 1)
            act.wait_ge(S("mod_first"), 1)
            act.wait_ge(S("tok_normed"), 1)
            for k in range(KT):
                for at, gain, shift in ((k * TC, gain_l, mod), (k * TC + T, gain_c, mod_c)):
                    last = act.activation(h_hi[:, at:at + T], tok[:, at:at + T], ACT.Identity, scale=gain[:, k:k + 1],
                                          bias=shift[:, k:k + 1])
                last.then_inc(S("h_hi"), 1)
                if k < AHEAD:
                    hi(act, Chunk(k))
            act.dma_start(con[:, 2 * P:N_CON], con_in[:, 2 * P:N_CON]).then_inc(S("con_late_in"), 16)
            act.dma_start(msk[:, :], msk_in).then_inc(S("late_in"), 16)
            act.dma_start(sink[:, :], sink_in.partition_broadcast(P)).then_inc(S("late_in"), 16)

            for h in range(HEADS + 1):
                if h < HEADS:
                    hi(act, Chunk(N_V, h + AHEAD))
                if h >= 1:
                    act.wait_ge(S("multiplied"), h)
                    if h >= 3:
                        act.wait_ge(S("v_turned"), h - 2)
                    act.activation(v_T[(h - 1) % 2], psum[(h - 1) % 2][:, :], ACT.Copy).then_inc(S("v_T"), 1)

            act.dma_start(by_tile(xres[:, :]), by_tile(tok_in)[:, :, 0:T]).then_inc(S("xres_in"), 16)

            def silu_parts(h, n_done):
                act.wait_ge(S("multiplied"), n_done)
                act.activation(qg_s, psum[2][:, :], ACT.Sigmoid).then_inc(S("qg_sigmoid"), 1)
                log_exp_tables(act)
                act.wait_ge(S("f"), h * 2 + 2)
                act.activation(f_buf, f_buf, ACT.Ln).then_inc(S("log_f"), 1)

            def exps(h, old):
                act.wait_ge(S("scanned"), h * 2 + 2)
                if old:
                    act.wait_ge(S("k_d"), h)
                    act.wait_ge(S("state"), h * 8)
                act.activation(e_qd.rearrange("p (d t) -> p d t", d=2),
                               b_buf.rearrange("p (d t) -> p d t", d=2)[:, :, 0:T], ACT.Exp).then_inc(S("e_qd"), 1)
                for d in range(2):
                    total = d * TC + (TC - 1 if d == 0 else T)
                    act.activation(e_kd[:, d * TC + T:(d + 1) * TC], b_buf[:, d * TC + T:(d + 1) * TC], ACT.Exp,
                                   scale=-1.0, bias=b_buf[:, total:total + 1]).then_inc(S("e_kc"), 1)
                act.wait_ge(S("d1"), h * 2 + 2)
                act.activation(e_qe, d1, ACT.Exp).then_inc(S("e_qe"), 1)
                act.activation(e_ke, d1, ACT.Exp, scale=-1.0).then_inc(S("e_ke"), 1)
                act.wait_ge(S("d3"), h * 2 + 2)
                x = e_kd.rearrange("p (d t) -> p d t", d=2)[:, :, 0:T]
                act.activation(x, x, ACT.Exp).then_inc(S("e_kd"), 1)

            def out_squares(h):
                act.wait_ge(S("o"), h + 1)
                act.activation(o_sq, psum[5][:, T:2 * T], ACT.Square).then_inc(S("o_squares"), 1)

            def out_rstd(h):
                act.wait_ge(S("o_mean"), h + 1)
                act.activation(o_rs, o_rs, ACT.Ln).then_inc(S("o_log"), 1)
                act.wait_ge(S("o_log"), h + 1)
                act.activation(o_rs, o_rs, ACT.Exp, scale=-0.5).then_inc(S("o_rstd"), 1)

            def out_hi(h):
                act.wait_ge(S("y_full"), h + 1)
                act.activation(y_hi[:, bass.ds(h * T, T)], y_f, ACT.Copy).then_inc(S("y_hi"), 1)

            def copy_turned(n_done, src, dst):
                act.wait_ge(S("k_turned"), n_done)
                act.activation(dst, src, ACT.Copy).then_inc(S("k_dT"), 1)

            def head(h, at, prev, prev2):
                if prev:
                    silu_parts(h - 1, h * 4 + N_HEAD)
                hi(act, at(AHEAD))
                if prev:
                    exps(h - 1, prev2)
                if prev2:
                    out_squares(h - 2)
                hi(act, at(1 + AHEAD))
                if prev2:
                    out_rstd(h - 2)
                act.preload_act_table_set("sigmoid_and_others")
                for d in range(2):
                    act.wait_ge(S("multiplied"), at(d).n + 1)
                    act.activation(f_buf[:, d * TC:(d + 1) * TC], psum[d][:, :], ACT.Sigmoid).then_inc(S("f_sigmoid"), 1)
                if prev2:
                    out_hi(h - 2)
                if prev:
                    copy_turned(h * 2 - 1, psum[3][:, :], k_dT[:, 0:512])
                    copy_turned(h * 2, psum[4][:, :], k_dT[:, 512:1024])
                hi(act, at(2 + AHEAD))
                act.wait_ge(S("f"), h * 2 + 2)
                if prev:
                    act.wait_ge(S("k_d"), h)
                act.activation(k_buf, f_buf, ACT.Copy, scale=-1.0, bias=1.0).then_inc(S("k"), 1)
                hi(act, at(3 + AHEAD))

            for h in range(2):
                head(h, lambda m: Chunk(N_HEAD, 4 * h + m), h >= 1, False)
            with act.Fori(0, (HEADS - 2) // 2) as i:
                for u in range(2):
                    head(i * 2 + (2 + u), lambda m: Chunk(N_HEAD + 8, 4 * u + m, i, 8), True, True)
            silu_parts(HEADS - 1, N_HOUT)
            hi(act, Chunk(N_HOUT, 2))
            exps(HEADS - 1, True)
            hi(act, Chunk(N_HOUT, 3))
            out_squares(HEADS - 2)
            hi(act, Chunk(N_HOUT, 4))
            hi(act, Chunk(N_HOUT, 5))
            out_rstd(HEADS - 2)
            copy_turned(2 * HEADS - 1, psum[3][:, :], k_dT[:, 0:512])
            hi(act, Chunk(N_HOUT, 6))
            out_hi(HEADS - 2)
            copy_turned(2 * HEADS, psum[3][:, :], k_dT[:, 512:1024])
            hi(act, Chunk(N_HOUT, 7))
            hi(act, Chunk(N_FFN))
            out_squares(HEADS - 1)
            hi(act, Chunk(N_FFN, 1))
            out_rstd(HEADS - 1)
            out_hi(HEADS - 1)
            square_residual(act, 0)
            norm_rstd(act, 0)
            split_h_hi(act, 1, lambda m: mod[:, 3 * KT + m:3 * KT + m + 1])

            def ffn_tile(t, p, s, n_done, has_old):
                act.wait_ge(S("multiplied"), n_done)
                if has_old:
                    act.wait_ge(S("u_full"), t - 1)
                for half in range(2):
                    act.activation(conv[p][half], psum[4 + 2 * half + p][:, 0:T], ACT.Identity,
                                   scale=p1("conv_w", t + (2 * JF + half * JF)),
                                   bias=p1("conv_b", t + half * JF)).then_inc(S("conv_mid"), 1)
                act.wait_ge(S("conv"), t * 2 + 2)
                act.activation(f_silu[p], conv[p][0], ACT.Silu).then_inc(S("f_silu"), 1)
                act.wait_ge(S("u_full"), t + 1)
                act.activation(y_hi[:, s * T:s * T + T], u_f[p], ACT.Copy).then_inc(S("u_hi"), 1)

            for j in range(FFN_PEEL):
                c = ffn_first(j)
                hi(act, Chunk(c, AHEAD))
                hi(act, Chunk(c, 1 + AHEAD))
                if j >= 1:
                    ffn_tile(j - 1, (j - 1) % 2, (j - 1) % 4, ffn_first(j - 1) + 2, j >= 3)
                if j >= 2:
                    hi(act, Chunk(c, 2 + AHEAD))
            with act.Fori(0, (JF - FFN_PEEL) // 4) as i:
                for u in range(4):
                    hi(act, Chunk(ffn_first(FFN_PEEL), 3 * u + AHEAD, i, 12))
                    hi(act, Chunk(ffn_first(FFN_PEEL), 3 * u + 1 + AHEAD, i, 12))
                    t = FFN_PEEL + u - 1
                    ffn_tile(i * 4 + t, t % 2, t % 4, i * 12 + (ffn_first(t) + 2), True)
                    hi(act, Chunk(ffn_first(FFN_PEEL), 3 * u + 2 + AHEAD, i, 12))
            hi(act, Chunk(N_IN2 - 2, AHEAD))
            ffn_tile(JF - 1, (JF - 1) % 2, (JF - 1) % 4, ffn_first(JF - 1) + 2, True)
            hi(act, Chunk(N_IN2 - 1, AHEAD))
            log_exp_tables(act)
            square_residual(act, 1)
            norm_rstd(act, 1)
            square_residual(act, 2)
            norm_rstd(act, 2)
            split_h_hi(act, 2)

            def evacuate(t):
                act.wait_ge(S("multiplied"), N_IN2 + t + 1)
                z = psum[t % 4][:, 0:T]
                dst = in2_dst(t)
                if dst is not None:
                    act.activation(dst, z, ACT.Copy).then_inc(S("in2_copied"), 1)
                elif t < T_GR:
                    v = v_index(t)
                    if v >= 2:
                        act.wait_ge(S("v2_turned"), v - 1)
                    act.activation(v_tmp[v % 2], z, ACT.Copy).then_inc(S("in2_copied"), 1)
                else:
                    act.activation(gate_dst(t), z, ACT.Exp, scale=-1.0).then_inc(S("gate_exp"), 1)

            def softmax_exp(e):
                p = e % 2
                act.wait_ge(S("s_neg"), e + 1)
                if e >= 2:
                    act.wait_ge(S("p_turned"), e - 1)
                act.activation(s_p[p][:, 0:P], s_b[p][:, 0:P], ACT.Exp, scale=S_DH ** -0.5, bias=s_neg[p][:, 0:1],
                               accum_out=s_sum[p][:, 0:1]).then_inc(S("s_exp"), 1)
                act.activation(s_p[p][:, P:3 * P], s_b[p][:, P:3 * P], ACT.Exp, scale=S_DH ** -0.5,
                               bias=s_neg[p][:, 1:2], accum_out=s_sum[p][:, 1:2]).then_inc(S("s_exp"), 1)
                act.activation(s_sink[p], s_neg[p], ACT.Exp, bias=sink[:, e:e + 1]).then_inc(S("s_exp"), 1)

            def probs_copy(e):
                act.wait_ge(S("p_turned"), e + 1)
                if e >= 2:
                    act.wait_ge(S("pv"), e - 1)
                act.activation(s_pT[e % 2], psum[7][:, 0:3 * P], ACT.Copy).then_inc(S("p_T"), 1)

            def ret_squares(r):
                act.wait_ge(S("r_o"), r + 1)
                act.activation(r_sq, psum[4][:, :], ACT.Square).then_inc(S("r_squares"), 1)

            def ret_rstd(r):
                act.wait_ge(S("r_mean"), r + 1)
                act.activation(r_rs, r_rs, ACT.Ln).then_inc(S("r_log"), 1)
                act.wait_ge(S("r_log"), r + 1)
                act.activation(r_rs, r_rs, ACT.Exp, scale=-0.5).then_inc(S("r_rstd"), 1)

            def ret_hi(r):
                act.wait_ge(S("r_full"), r + 1)
                act.activation(y_hi[:, 2 * r * T:2 * (r + 1) * T], r_t, ACT.Copy).then_inc(S("r_hi"), 1)

            act.wait_ge(S("late_in"), 32)
            for t in range(TILES_IN2 + 1):
                if t < TILES_IN2:
                    hi(act, Chunk(N_IN2, t + AHEAD))
                if t >= 1:
                    evacuate(t - 1)
                e = t - T_GR
                if 1 <= e <= S_HEADS:
                    softmax_exp(e - 1)
                    probs_copy(e - 1)
                if e == S_HEADS + 3:
                    act.wait_ge(S("swa"), S_HEADS)
                    act.activation(h_hi[:, 8 * T:12 * T], swa, ACT.Copy).then_inc(S("swa_hi"), 1)
                r = t - RET_FIRST
                if r >= 3 and r % 2 == 1 and (r - 3) // 2 < R_HEADS:
                    ret_rstd((r - 3) // 2)
                    ret_hi((r - 3) // 2)
                if r >= 1 and r % 2 == 1 and (r - 1) // 2 < R_HEADS:
                    ret_squares((r - 1) // 2)
            for n in range(N_SOUT, N_MOUT):
                hi(act, Chunk(n, AHEAD))
            for b in range(4):
                act.wait_ge(S("mg_full"), b + 1)
                act.activation(h_hi[:, b * 512:b * 512 + 512], gate_r[:, b * 512:b * 512 + 512], ACT.Copy).then_inc(S("mg_hi"), 1)
                hi(act, Chunk(N_MOUT, b + AHEAD))
            for n in range(N_MOUT + 4, N_MLP):
                hi(act, Chunk(n, AHEAD))
            square_banks(act, N_MLP, HIGH_BANKS)
            norm_rstd(act, 3)
            square_residual(act, 3)
            norm_rstd(act, 4)
            split_h_hi(act, 3)

            def mlp_tile(t, p, s, n_done, has_old):
                act.wait_ge(S("multiplied"), n_done)
                if has_old:
                    act.wait_ge(S("m_full"), t - 1)
                act.activation(m_relu[p], psum[4 + p][:, 0:T], ACT.Relu).then_inc(S("m_relu"), 1)
                act.wait_ge(S("m_full"), t + 1)
                act.activation(y_hi[:, s * T:s * T + T], u_f[p], ACT.Copy).then_inc(S("m_hi"), 1)

            for j in range(MLP_PEEL):
                hi(act, Chunk(mlp_first(j), AHEAD))
                if j >= 1:
                    mlp_tile(j - 1, (j - 1) % 2, (j - 1) % 4, mlp_first(j - 1) + 1, j >= 3)
                if j >= 2:
                    hi(act, Chunk(mlp_first(j), 1 + AHEAD))
            with act.Fori(0, (JM - MLP_PEEL) // 4 - 1) as i:
                for u in range(4):
                    hi(act, Chunk(mlp_first(MLP_PEEL), 2 * u + AHEAD, i, 8))
                    t = MLP_PEEL + u - 1
                    mlp_tile(i * 4 + t, t % 2, t % 4, i * 8 + (mlp_first(t) + 1), True)
                    hi(act, Chunk(mlp_first(MLP_PEEL), 2 * u + 1 + AHEAD, i, 8))
            for j in range(JM - 4, JM):
                hi(act, Chunk(mlp_first(j), AHEAD))
                mlp_tile(j - 1, (j - 1) % 2, (j - 1) % 4, mlp_first(j - 1) + 1, True)
                hi(act, Chunk(mlp_first(j), 1 + AHEAD))
            mlp_tile(JM - 1, (JM - 1) % 2, (JM - 1) % 4, mlp_first(JM - 1) + 1, True)
            square_banks(act, N_ALL, LOW_BANKS)
            norm_rstd(act, 5)

        @block.tensor
        def _(pe):
            pe.wait_ge(S("cs"), 1)
            pe.wait_ge(S("con_in"), 16)

            def ada(k, group, slot, rounds, first, last):
                pe.wait_ge(S(f"loaded{slot}"), rounds * 16 + 16)
                for b in range(2):
                    done = pe.matmul(psum[4 + 2 * group + b][0:2, :], cs[:, 2 * k:2 * k + 2], raw[slot][:, b * 512:b * 512 + 512],
                                     start=first, stop=last, skip_group_check=True)
                done.then_inc(S("ada_done"), 1)

            def turn_rows(rows, group):
                pe.wait_ge(S("mod_rows"), 2 * group + 2)
                for m in range(KT):
                    last = pe.transpose(psum[2 * group][:, 2 * m:2 * m + 2], rows[0:2, m * P:m * P + P], ident[0:2, 0:2])
                last.then_inc(S("mod_turned"), 1)

            for a in range(ADA_FIRST):
                ada(a % KT, a // KT, a % RING, a // RING, a % KT == 0, a % KT == KT - 1)
                if a < 4:
                    pe.wait_ge(S("tok_squares"), a + 1)
                    for k in range(2 * a, 2 * a + 2):
                        last = pe.matmul(psum[1][:, :], ones, wide[:, k * TC:(k + 1) * TC], start=k == 0, stop=k == KT - 1)
                    if a == 3:
                        last.then_inc(S("tok_summed"), 1)
                if a == KT + 1:
                    turn_rows(mod_rows, 0)
            turn_rows(mod_rows2, 1)

            for h in range(HEADS + 1):
                if h < HEADS:
                    if h >= 2:
                        pe.wait_ge(S("v_T"), h - 1)
                    column_tile(pe, Chunk(N_V, h), psum[h % 2][:, :], TC, TC, input_tiles=0 if h == 0 else None)
                if h >= 1:
                    pe.wait_ge(S("v_T"), h)
                    if h >= 3:
                        pe.wait_ge(S("v"), h - 2)
                    for b in range(4):
                        last = pe.transpose(psum[3 + (h - 1) % 2][:, b * P:b * P + P],
                                            v_T[(h - 1) % 2][:, b * P:b * P + P], ident)
                    last.then_inc(S("v_turned"), 1)

            def mod_columns(total, dst, col):
                for m in range(KT):
                    last = pe.matmul(dst[:, col + m:col + m + 1], total[:, m * P:m * P + P], ones[:, 0:1], start=True, stop=True,
                                     skip_group_check=True)
                return last

            pe.wait_ge(S("mod_summed"), GROUPS * KT)
            for g in range(GROUPS):
                last = mod_columns(mod_sum[g], psum[2], g * KT)
            last.then_inc(S("mod_columns"), 1)

            def out_sum(h, dst):
                pe.wait_ge(S("o_squares"), h + 1)
                pe.matmul(dst, ones, o_sq, start=True, stop=True, skip_group_check=True).then_inc(S("o_summed"), 1)

            def turn(p, part_, bank):
                for d in range(2):
                    for b in range(2):
                        at = d * TC + part_ * T + b * P
                        last = pe.transpose(psum[bank][:, (2 * d + b) * P:(2 * d + b + 1) * P], k_d[:, at:at + P], ident)
                last.then_inc(S("k_turned"), 1)

            def chunk_scores(p):
                for d in range(2):
                    behind, ahead = (HALF, 0) if d == 0 else (0, HALF)
                    for c in range(NCH):
                        x = d * T + c * CH
                        y = (2 * d + c // 2) * CH
                        row = CH * (c % 2)
                        pe.matmul(psum[5][row:row + CH, y + behind:y + behind + HALF], k_e[:, x:x + CH],
                                  q_e[:, x + behind:x + behind + HALF], start=True, stop=True, skip_group_check=True)
                        last = pe.matmul(psum[5][row + ahead:row + ahead + HALF, y + ahead:y + ahead + HALF],
                                         k_e[:, x + ahead:x + ahead + HALF], q_e[:, x + ahead:x + ahead + HALF],
                                         start=True, stop=True, skip_group_check=True)
                last.then_inc(S("scores"), 1)

            def key_values(h):
                pe.wait_ge(S("k_dT"), h * 2 + 2)
                pe.wait_ge(S("v_cur"), h + 1)
                for d in range(2):
                    for b in range(2):
                        x = 512 + (2 * d + b) * P
                        pe.matmul(psum[6 + d][:, 0:P], k_dT[:, x:x + P], v_cur[:, (2 + b) * P:(3 + b) * P],
                                  start=b == 0, stop=b == 1)
                    for s in range(1, NCH):
                        c = s - 1 if d == 0 else NCH - s
                        rows = slice(CH * (c % 2), CH * (c % 2) + CH)
                        x = (2 * d + c // 2) * P
                        last = pe.matmul(kv_at(d, s), k_dT[rows, x:x + P], v_cur[rows, (c // 2) * P:(c // 2 + 1) * P],
                                         start=True, stop=True, skip_group_check=True)
                last.then_inc(S("kv"), 1)

            def outputs(h, p):
                pe.wait_ge(S("masked"), h * 2 + 2)
                pe.wait_ge(S("state"), h * 8 + 8)
                for c in range(NCH):
                    dst = psum[5][:, T + c * CH:T + (c + 1) * CH]
                    for d in range(2):
                        pos = c if d == 0 else NCH - 1 - c
                        pe.matmul(dst, v_cur[:, (c // 2) * P:(c // 2 + 1) * P],
                                  sc_T[:, (NCH * d + c) * CH:(NCH * d + c + 1) * CH],
                                  start=d == 0, stop=False, skip_group_check=True)
                        last = pe.matmul(dst, state[:, (4 * d + pos) * P:(4 * d + pos + 1) * P],
                                         q_d[p][:, d * T + c * CH:d * T + (c + 1) * CH],
                                         start=False, stop=d == 1, skip_group_check=True)
                last.then_inc(S("o"), 1)

            def head(h, u, at, prev, prev2):
                if prev:
                    pe.wait_ge(S("f_sigmoid"), h * 2)
                else:
                    pe.wait_ge(S("v_T"), HEADS)
                column_tile(pe, at(0), psum[0][:, :], TC, TC)
                if prev2:
                    outputs(h - 2, u)

                def last_sum():
                    pe.wait_ge(S("qg"), h)
                    out_sum(h - 2, psum[2][:, T:2 * T])

                column_tile(pe, at(1), psum[1][:, :], TC, TC, halfway=last_sum if prev2 else None)
                if prev:
                    if not prev2:
                        pe.wait_ge(S("scores_cleared"), 1)
                        pe.wait_ge(S("v"), HEADS)
                    pe.wait_ge(S("k_d"), h)
                    turn(1 - u, 0, 3)
                    turn(1 - u, 1, 4)
                    if prev2:
                        pe.wait_ge(S("o_n"), h - 1)
                    chunk_scores(1 - u)
                    pe.wait_ge(S("qg"), h)
                else:
                    pe.wait_ge(S("mod_late"), 1)
                column_tile(pe, at(2), psum[2][:, 0:T], TC, T)
                if prev:
                    key_values(h - 1)
                column_tile(pe, at(3), psum[2][:, T:2 * T], TC, T)

            for h in range(2):
                head(h, h, lambda m: Chunk(N_HEAD, 4 * h + m), h >= 1, False)
            with pe.Fori(0, (HEADS - 2) // 2) as i:
                for u in range(2):
                    head(i * 2 + (2 + u), u, lambda m: Chunk(N_HEAD + 8, 4 * u + m, i, 8), True, True)

            def out_row(k):
                pe.wait_ge(S("y_lo"), k + 1)
                row_tile(pe, Chunk(N_HOUT, k), HOUT_BANKS, y_hi[:, k * T:k * T + T], y_lo[:, k * T:k * T + T],
                         k == 0, k == KT - 1)

            outputs(HEADS - 2, 0)
            pe.wait_ge(S("f_sigmoid"), 2 * HEADS)
            pe.wait_ge(S("qg"), HEADS)
            for k in range(3):
                out_row(k)
            out_sum(HEADS - 2, psum[3][:, 0:T])
            pe.wait_ge(S("k_d"), HEADS)
            pe.wait_ge(S("o_n"), HEADS - 1)
            turn(1, 0, 3)
            chunk_scores(1)
            out_row(3)
            pe.wait_ge(S("k_dT"), 2 * HEADS - 1)
            turn(1, 1, 3)
            out_row(4)
            key_values(HEADS - 1)
            out_row(5)
            outputs(HEADS - 1, 1)
            out_row(6)
            pe.wait_ge(S("gate2_summed"), HEADS)
            mod_columns(gate2_sum, psum[6], 0).then_inc(S("gate2_columns"), 1)
            out_sum(HEADS - 1, psum[3][:, 0:T])
            out_row(7)
            norm_sum(pe, 0)

            def ffn_up(j, p, c, has_old, first=False):
                if has_old:
                    pe.wait_ge(S("conv"), j * 2 - 2)
                column_tile(pe, c[0], psum[4 + p][:, 0:T], T, T, input_tiles=KT if first else None)
                if first:
                    pe.wait_ge(S("mod_gate2"), 1)
                column_tile(pe, c[1], psum[6 + p][:, 0:T], T, T)

            def ffn_down(t, s, c, first, last):
                pe.wait_ge(S("u_lo"), t + 1)
                row_tile(pe, c, LOW_BANKS, y_hi[:, s * T:s * T + T], y_lo[:, s * T:s * T + T], first, last)

            for j in range(FFN_PEEL):
                c = ffn_first(j)
                ffn_up(j, j % 2, [Chunk(c), Chunk(c, 1)], j >= 2, j == 0)
                if j >= 2:
                    ffn_down(j - 2, (j - 2) % 4, Chunk(c, 2), j == 2, False)
            with pe.Fori(0, (JF - FFN_PEEL) // 4) as i:
                for u in range(4):
                    j = FFN_PEEL + u
                    c = [Chunk(ffn_first(FFN_PEEL), 3 * u + m, i, 12) for m in range(3)]
                    ffn_up(i * 4 + j, j % 2, c, True)
                    ffn_down(i * 4 + (j - 2), (j - 2) % 4, c[2], False, False)
            for t in range(JF - 2, JF):
                ffn_down(t, t % 4, Chunk(N_IN2 - JF + t), False, t == JF - 1)
            norm_sum(pe, 1)
            norm_sum(pe, 2)

            def turn_values(t):
                v = v_index(t)
                pe.wait_ge(S("in2_copied"), t + 1)
                if v >= 2:
                    pe.wait_ge(S("v2"), v - 1)
                for b in range(2):
                    last = pe.transpose(psum[4 + v % 2][:, b * P:b * P + P], v_tmp[v % 2][:, b * P:b * P + P], ident)
                last.then_inc(S("v2_turned"), 1)

            def swa_scores(e):
                g, x = e // 4, (e % 4) * T
                rows = slice(S_DH * g, S_DH * g + S_DH)
                if e == 0:
                    pe.wait_ge(S("v2"), 8)
                if e >= 2:
                    pe.wait_ge(S("s_biased"), e - 1)
                dst = psum[5 + e % 2]
                pe.matmul(dst[:, 0:P], s_q[rows, x:x + P], s_k[rows, 0:P], start=True, stop=True, skip_group_check=True)
                pe.matmul(dst[:, P:3 * P], s_q[rows, x + P:x + T], s_k[rows, 0:T], start=True, stop=True,
                          skip_group_check=True).then_inc(S("s_scores"), 1)

            def turn_probs(e):
                pe.wait_ge(S("p_norm"), 2 * e + 2)
                if e >= 1:
                    pe.wait_ge(S("p_T"), e)
                for b in range(3):
                    last = pe.transpose(psum[7][:, b * P:b * P + P], s_p[e % 2][:, b * P:b * P + P], ident)
                last.then_inc(S("p_turned"), 1)

            def swa_values(e):
                g, q = e // 4, S_DH * (e % 2)
                pe.wait_ge(S("p_T"), e + 1)
                if e == 0:
                    pe.wait_ge(S("v2"), 9)
                if e >= 2:
                    pe.wait_ge(S("swa"), e - 1)
                pe.matmul(psum[4][q:q + S_DH, 0:T], s_v[:, S_DH * g:S_DH * g + S_DH], s_pT[e % 2][:, 0:T],
                          start=True, stop=False, skip_group_check=True)
                pe.matmul(psum[4][q:q + S_DH, P:T], s_v[:, P + S_DH * g:P + S_DH * g + S_DH], s_pT[e % 2][:, T:3 * P],
                          start=False, stop=True, skip_group_check=True).then_inc(S("pv"), 1)

            def ret_scores(r):
                dst = psum[5 + r % 2]
                if r == 0:
                    pe.wait_ge(S("s_biased"), S_HEADS)
                if r >= 2:
                    pe.wait_ge(S("r_sc"), r - 1)
                pe.matmul(dst[:, 0:T], r_k[:, r * T:r * T + P], r_q[:, r * T:(r + 1) * T], start=True, stop=True,
                          skip_group_check=True)
                pe.matmul(dst[:, T:3 * P], r_k[:, r * T + P:(r + 1) * T], r_q[:, r * T + P:(r + 1) * T], start=True,
                          stop=True, skip_group_check=True).then_inc(S("r_scores"), 1)

            def ret_values(r):
                pe.wait_ge(S("r_sc"), r + 1)
                if r == 0:
                    pe.wait_ge(S("swa"), S_HEADS)
                    pe.wait_ge(S("v_centred"), 1)
                else:
                    pe.wait_ge(S("r_normed"), r)
                for m in range(2):
                    x = r * R_DV + m * P
                    pe.matmul(psum[4][:, m * T:m * T + T], r_v[:, x:x + P], r_sc[r % 2][:, 0:T], start=True, stop=False,
                              skip_group_check=True)
                    last = pe.matmul(psum[4][:, m * T + P:m * T + T], r_v[:, 4 * T + x:4 * T + x + P],
                                     r_sc[r % 2][:, T:3 * P], start=False, stop=True, skip_group_check=True)
                last.then_inc(S("r_o"), 1)

            def ret_sum(r):
                pe.wait_ge(S("r_squares"), r + 1)
                if r == 0:
                    pe.wait_ge(S("p_T"), S_HEADS)
                else:
                    pe.wait_ge(S("r_mean"), r)
                for m in range(2):
                    last = pe.matmul(psum[7][:, 0:T], ones, r_sq[:, m * T:m * T + T], start=m == 0, stop=m == 1)
                last.then_inc(S("r_summed"), 1)

            for t in range(TILES_IN2):
                if 4 <= t < T_GR + 4:
                    pe.wait_ge(S("in2_copied"), t - 3)
                elif t >= T_GR + 4:
                    pe.wait_ge(S("gate"), t - T_GR - 3)
                column_tile(pe, Chunk(N_IN2, t), psum[t % 4][:, 0:T], T, T, input_tiles=2 * KT if t == 0 else None)
                if t >= 1 and v_index(t - 1) is not None:
                    turn_values(t - 1)
                e = t - T_GR
                if 0 <= e < S_HEADS:
                    swa_scores(e)
                if 1 <= e <= S_HEADS:
                    turn_probs(e - 1)
                if 2 <= e <= S_HEADS + 1:
                    swa_values(e - 2)
                r = t - RET_FIRST
                if 0 <= r < 2 * R_HEADS and r % 2 == 0:
                    ret_scores(r // 2)
                if r >= 1 and r % 2 == 1 and (r - 1) // 2 < R_HEADS:
                    ret_values((r - 1) // 2)
                if r >= 2 and r % 2 == 0 and (r - 2) // 2 < R_HEADS:
                    ret_sum((r - 2) // 2)

            pe.wait_ge(S("swa_lo"), 1)
            pe.wait_ge(S("r_lo"), R_HEADS)
            for k in range(4):
                x = slice((8 + k) * T, (9 + k) * T)
                row_tile(pe, Chunk(N_SOUT, k), HIGH_BANKS, h_hi[:, x], h_lo[:, x], k == 0, k == 3)
            pe.wait_ge(S("gate"), TILES_IN2 - T_GR)
            for k in range(KT):
                x = slice(k * T, (k + 1) * T)
                row_tile(pe, Chunk(N_ROUT, k), LOW_BANKS, y_hi[:, x], y_lo[:, x], k == 0, k == KT - 1)
            for k in range(KT):
                x = slice(k * T, (k + 1) * T)
                pe.wait_ge(S("mg_lo"), k // 2 + 1)
                row_tile(pe, Chunk(N_MOUT, k), HIGH_BANKS, h_hi[:, x], h_lo[:, x], k == 0, k == KT - 1)
            norm_sum(pe, 3, bank=0)
            norm_sum(pe, 4, bank=0)

            def mlp_up(j, p, c, has_old, first=False):
                if has_old:
                    pe.wait_ge(S("m_relu"), j - 1)
                column_tile(pe, c, psum[4 + p][:, 0:T], T, T, input_tiles=3 * KT if first else None)

            def mlp_down(t, s, c, first, last):
                pe.wait_ge(S("m_lo"), t + 1)
                row_tile(pe, c, LOW_BANKS, y_hi[:, s * T:s * T + T], y_lo[:, s * T:s * T + T], first, last)

            for j in range(MLP_PEEL):
                mlp_up(j, j % 2, Chunk(mlp_first(j)), j >= 2, j == 0)
                if j >= 2:
                    mlp_down(j - 2, (j - 2) % 4, Chunk(mlp_first(j), 1), j == 2, False)
            with pe.Fori(0, (JM - MLP_PEEL) // 4) as i:
                for u in range(4):
                    j = MLP_PEEL + u
                    mlp_up(i * 4 + j, j % 2, Chunk(mlp_first(MLP_PEEL), 2 * u, i, 8), True)
                    mlp_down(i * 4 + (j - 2), (j - 2) % 4, Chunk(mlp_first(MLP_PEEL), 2 * u + 1, i, 8), False, False)
            for t in range(JM - 2, JM):
                mlp_down(t, t % 4, Chunk(N_ALL - JM + t), False, t == JM - 1)
            norm_sum(pe, 5)

        @block.vector
        def _(dve):
            dve.wait_ge(S("cs_exp"), 1)
            dve.tensor_scalar(cs_e, cs_e, 1.0, None, ALU.add).then_inc(S("cs_1"), 1)
            dve.wait_ge(S("cs_1"), 1)
            dve.reciprocal(cs_e, cs_e).then_inc(S("cs_r"), 1)
            dve.wait_ge(S("cs_r"), 1)
            dve.tensor_tensor(cs, cc[:, :], cs_e, ALU.mult).then_inc(S("cs"), 1)
            dve.wait_ge(S("par_in"), 16)
            dve.tensor_tensor(lb_m, p1("lb0", 0, 16), p1("lb1", 0, 16), ALU.max).then_inc(S("lb_max"), 1)
            dve.wait_ge(S("lb_max"), 1)
            dve.tensor_tensor(lb_d[:, 0:16], p1("lb0", 0, 16), lb_m, ALU.subtract)
            dve.tensor_tensor(lb_d[:, 16:32], p1("lb1", 0, 16), lb_m, ALU.subtract).then_inc(S("lb_diff"), 1)
            dve.wait_ge(S("lb_exp"), 1)
            dve.tensor_tensor(lb_m, lb_d[:, 0:16], lb_d[:, 16:32], ALU.add).then_inc(S("lb_sum"), 1)
            dve.wait_ge(S("lb_sum"), 1)
            dve.reciprocal(lb_m, lb_m).then_inc(S("lb_r"), 1)
            dve.wait_ge(S("lb_r"), 1)
            dve.tensor_tensor(lb, lb_d[:, 0:16], lb_m, ALU.mult).then_inc(S("lb"), 1)
            dve.wait_ge(S("lb"), 1)
            dve.tensor_scalar(lb_om, lb, -1.0, 1.0, ALU.mult, ALU.add).then_inc(S("lb_om"), 1)
            dve.memset(sc_T, 0.0)
            dve.wait_ge(S("tok_summed"), 1)
            dve.tensor_scalar(rstd, psum[1][:, :], 1.0 / D, EPS, ALU.mult, ALU.add).then_inc(S("tok_mean"), 1)
            dve.wait_ge(S("tok_rstd"), 1)
            dve.tensor_tensor(by_tile(tok[:, :]), by_tile(tok[:, :]), over_tiles(rstd), ALU.mult).then_inc(S("tok_normed"), 1)
            scales, shifts = (psum[b][:, 0:2 * KT].rearrange("p (m w) -> p m w", w=2) for b in (0, 2))
            dve.wait_ge(S("mod_turned"), 1)
            for w, scale in ((0, mod), (1, mod_c)):
                dve.tensor_tensor(scale[:, KT:2 * KT], scales[:, :, w], p1("b_ada", KT, KT), ALU.add).then_inc(S("scale_first"), 1)
            dve.wait_ge(S("scale_first"), 2)
            for gain, scale in ((gain_l, mod), (gain_c, mod_c)):
                dve.scalar_tensor_tensor(gain, scale[:, KT:2 * KT], 1.0, p1("norm1", 0, KT), ALU.add, ALU.mult)
            dve.wait_ge(S("mod_turned"), 2)
            for w, shift in ((0, mod), (1, mod_c)):
                last = dve.tensor_tensor(shift[:, 0:KT], shifts[:, :, w], p1("b_ada", 0, KT), ALU.add)
            last.then_inc(S("mod_first"), 1)
            dve.wait_ge(S("mod_first"), 1)
            dve.wait_ge(S("tok_normed"), 1)
            for k in range(KT + 1):
                if k < KT:
                    dve.wait_ge(S("h_hi"), k + 1)
                    for at, gain, shift in ((k * TC, gain_l, mod), (k * TC + T, gain_c, mod_c)):
                        last = dve.tensor_scalar(tok[:, at:at + T], tok[:, at:at + T], gain[:, k:k + 1], shift[:, k:k + 1],
                                                 ALU.mult, ALU.add)
                    last.then_inc(S("modulated"), 1)
                if k >= 1:
                    dve.wait_ge(S("modulated"), k)
                    x = slice((k - 1) * TC, k * TC)
                    dve.tensor_tensor(h_lo[:, x], tok[:, x], h_hi[:, x].bitcast(F32), ALU.subtract).then_inc(S("h_lo"), 1)
                if k < AHEAD:
                    lo(dve, Chunk(k))

            def mod_row(k, dst, src, first):
                c_k = cs[:, bass.ds(2 * k, 1)]
                if first:
                    return dve.tensor_scalar(dst, src, c_k, None, ALU.mult)
                return dve.scalar_tensor_tensor(dst, src, c_k, dst, ALU.mult, ALU.add)

            for h in range(HEADS + 1):
                if h < HEADS:
                    lo(dve, Chunk(N_V, h + AHEAD))
                if h >= 1:
                    dve.wait_ge(S("v_turned"), h)
                    dve.tensor_copy(v_all[:, (h - 1) * 512:h * 512], psum[3 + (h - 1) % 2][:, :]).then_inc(S("v"), 1)
                for g in range(GROUPS if h < HEADS else 0):
                    n = GROUPS * h + g
                    slot = n % (2 * GROUPS)
                    dve.wait_ge(S(f"mod_loaded{slot}"), 16 * (h // 2 + 1))
                    if h >= 1:
                        dve.wait_ge(S("mod_summed"), n - GROUPS + 1)
                    mod_row(h, mod_sum[g], mod_raw[slot], h == 0).then_inc(S("mod_summed"), 1)
            dve.memset(psum[5][:, 0:T], 0.0).then_inc(S("scores_cleared"), 1)
            late = slice(ADA_FIRST, ADA_FIRST + GROUPS * KT)
            dve.wait_ge(S("mod_columns"), 1)
            dve.tensor_tensor(mod[:, late], psum[2][:, 0:GROUPS * KT], p1("b_ada", ADA_FIRST, GROUPS * KT),
                              ALU.add).then_inc(S("mod_late"), 1)
            dve.wait_ge(S("mod_late"), 1)
            dve.scalar_tensor_tensor(gain_2, mod[:, 4 * KT:5 * KT], 1.0, p1("norm2", 0, KT), ALU.add, ALU.mult)

            def split2(x):
                return x.rearrange("p (d t) -> p d t", d=2)

            def chunks(x):
                return x.rearrange("p (c t) -> p c t", c=NCH)

            def distances(h):
                dve.wait_ge(S("scanned"), h * 2 + 2)
                for d in range(2):
                    b = chunks(b_buf[:, d * TC:d * TC + T])
                    at = CH // 2 if d == 0 else CH - 1 - CH // 2
                    dve.tensor_tensor(chunks(d1[:, d * T:(d + 1) * T]), b, b[:, :, at:at + 1].broadcast_to([P, NCH, CH]),
                                      ALU.subtract).then_inc(S("d1"), 1)
                for d in range(2):
                    b = chunks(b_buf[:, d * TC:d * TC + T])
                    at = CH - 1 if d == 0 else 0
                    dve.tensor_tensor(chunks(e_kd[:, d * TC:d * TC + T]), b[:, :, at:at + 1].broadcast_to([P, NCH, CH]), b,
                                      ALU.subtract).then_inc(S("d3"), 1)

            def silu_qg(h, p):
                dve.wait_ge(S("qg_sigmoid"), h + 1)
                dve.tensor_tensor(qg[p], psum[2][:, :], qg_s, ALU.mult).then_inc(S("qg"), 1)

            def scale_qk(h, p):
                dve.wait_ge(S("qg"), h + 1)
                q = over_tiles(qg[p][:, 0:T], 2)
                dve.wait_ge(S("e_qd"), h + 1)
                dve.tensor_tensor(split2(q_d[p]), split2(e_qd), q, ALU.mult)
                dve.wait_ge(S("e_qe"), h + 1)
                dve.tensor_tensor(split2(q_e), split2(e_qe), q, ALU.mult)
                dve.wait_ge(S("e_ke"), h + 1)
                dve.wait_ge(S("k"), h + 1)
                dve.tensor_tensor(split2(k_e), split2(e_ke), split2(k_buf)[:, :, 0:T], ALU.mult)
                dve.wait_ge(S("e_kd"), h + 1)
                dve.tensor_tensor(k_d, e_kd, k_buf, ALU.mult).then_inc(S("k_d"), 1)

            def out_mean(h, total):
                dve.wait_ge(S("o_summed"), h + 1)
                dve.tensor_scalar(o_rs, total, 1.0 / P, EPS, ALU.mult, ALU.add).then_inc(S("o_mean"), 1)

            def out_gated(h, p):
                dve.wait_ge(S("o_rstd"), h + 1)
                dve.tensor_tensor(o_n, psum[5][:, T:2 * T], o_rs, ALU.mult).then_inc(S("o_n"), 1)
                dve.wait_ge(S("o_n"), h + 1)
                dve.scalar_tensor_tensor(y_f, o_n, p1("gnorm"), qg[p][:, T:2 * T], ALU.mult, ALU.mult).then_inc(S("y_full"), 1)

            def out_lo(h):
                dve.wait_ge(S("y_hi"), h + 1)
                dve.tensor_tensor(y_lo[:, bass.ds(h * T, T)], y_f, y_hi[:, bass.ds(h * T, T)].bitcast(F32),
                                  ALU.subtract).then_inc(S("y_lo"), 1)

            def forget(h):
                for d in range(2):
                    dve.wait_ge(S("f_sigmoid"), h * 2 + (d + 1))
                    x = f_buf[:, d * TC:(d + 1) * TC]
                    dve.tensor_scalar(x, x, lb_om[:, bass.ds(h + d * HEADS, 1)], lb[:, bass.ds(h + d * HEADS, 1)],
                                      ALU.mult, ALU.add).then_inc(S("f"), 1)

            def values_and_mask(h, old):
                if old:
                    dve.wait_ge(S("o"), h)
                dve.wait_ge(S("scores"), h + 1)
                dve.tensor_copy(v_cur, v_all[:, bass.ds(h * 512, 512)]).then_inc(S("v_cur"), 1)
                for odd in range(2):
                    rows = slice(CH * odd, CH * odd + CH)
                    dst = sc_T.rearrange("p (n q t) -> p n q t", q=2, t=CH)[rows, :, odd, :]
                    dve.copy_predicated(dst, by_tile(msk[rows, :], 4), by_tile(psum[5][rows, 0:T], 4)).then_inc(S("masked"), 1)

            def states(h):
                dve.wait_ge(S("kv"), h + 1)
                for s in range(NCH):
                    for d in range(2):
                        dst = state[:, (4 * d + s) * P:(4 * d + s + 1) * P]
                        kv = kv_at(d, s)
                        if s == 0:
                            dve.tensor_copy(dst, kv).then_inc(S("state"), 1)
                            continue
                        c = s - 1 if d == 0 else NCH - s
                        end = d * T + c * CH + (CH - 1 if d == 0 else 0)
                        dve.wait_ge(S("state"), h * 8 + (2 * s + d - 1))
                        dve.scalar_tensor_tensor(dst, state[:, (4 * d + s - 1) * P:(4 * d + s) * P], e_qd[:, end:end + 1],
                                                 kv, ALU.mult, ALU.add).then_inc(S("state"), 1)

            def scan(h):
                dve.wait_ge(S("log_f"), h + 1)
                dve.tensor_tensor_scan(b_buf[:, 0:TC], scan_mask[0], f_buf[:, 0:TC], 0.0, ALU.mult, ALU.add).then_inc(S("scanned"), 1)
                dve.tensor_tensor_scan(b_buf[:, TC:2 * TC][:, ::-1], scan_mask[1], f_buf[:, TC:2 * TC][:, ::-1], 0.0,
                                       ALU.mult, ALU.add).then_inc(S("scanned"), 1)

            def head(h, u, at, prev, prev2):
                if prev:
                    silu_qg(h - 1, 1 - u)
                    scan(h - 1)
                    distances(h - 1)
                    scale_qk(h - 1, 1 - u)
                lo(dve, at(AHEAD))
                if prev2:
                    out_mean(h - 2, psum[2][:, T:2 * T])
                lo(dve, at(1 + AHEAD))
                if prev2:
                    out_gated(h - 2, u)
                forget(h)
                if prev:
                    values_and_mask(h - 1, prev2)
                if prev2:
                    out_lo(h - 2)
                lo(dve, at(2 + AHEAD))
                if prev:
                    states(h - 1)
                lo(dve, at(3 + AHEAD))
                dve.wait_ge(S("gate2_in"), h * 16 + 16)
                if prev:
                    dve.wait_ge(S("gate2_summed"), h)
                mod_row(h, gate2_sum, gate2_raw, not prev).then_inc(S("gate2_summed"), 1)

            dve.wait_ge(S("late_in"), 32)
            dve.wait_ge(S("con_late_in"), 16)
            for h in range(2):
                head(h, h, lambda m: Chunk(N_HEAD, 4 * h + m), h >= 1, False)
            with dve.Fori(0, (HEADS - 2) // 2) as i:
                for u in range(2):
                    head(i * 2 + (2 + u), u, lambda m: Chunk(N_HEAD + 8, 4 * u + m, i, 8), True, True)
            silu_qg(HEADS - 1, 1)
            scan(HEADS - 1)
            distances(HEADS - 1)
            lo(dve, Chunk(N_HOUT, 2))
            scale_qk(HEADS - 1, 1)
            lo(dve, Chunk(N_HOUT, 3))
            lo(dve, Chunk(N_HOUT, 4))
            lo(dve, Chunk(N_HOUT, 5))
            out_mean(HEADS - 2, psum[3][:, 0:T])
            out_gated(HEADS - 2, 0)
            values_and_mask(HEADS - 1, True)
            lo(dve, Chunk(N_HOUT, 6))
            out_lo(HEADS - 2)
            lo(dve, Chunk(N_HOUT, 7))
            states(HEADS - 1)
            lo(dve, Chunk(N_FFN))
            lo(dve, Chunk(N_FFN, 1))
            out_mean(HEADS - 1, psum[3][:, 0:T])
            out_gated(HEADS - 1, 1)
            out_lo(HEADS - 1)
            dve.wait_ge(S("xres_in"), 16)
            dve.wait_ge(S("gate2_columns"), 1)
            dve.tensor_tensor(mod[:, 5 * KT:ADA], psum[6][:, 0:KT], p1("b_ada", 5 * KT, KT), ALU.add).then_inc(S("mod_gate2"), 1)
            add_product(dve, lambda m: mod[:, 2 * KT + m:2 * KT + m + 1], N_FFN, HOUT_BANKS)
            norm_mean(dve, 0)
            norm_input(dve, 0, 1, lambda m: gain_2[:, m:m + 1], lambda m: mod[:, 3 * KT + m:3 * KT + m + 1])

            def ffn_tile(t, p, s):
                for half in range(2):
                    z = psum[4 + 2 * half + p]
                    x = conv[p][half]
                    dve.wait_ge(S("conv_mid"), t * 2 + (1 + half))
                    dve.scalar_tensor_tensor(x[:, 1:T], z[:, 0:T - 1], p1("conv_w", t + half * JF), x[:, 1:T],
                                             ALU.mult, ALU.add).then_inc(S("conv_left"), 1)
                for half in range(2):
                    z = psum[4 + 2 * half + p]
                    x = conv[p][half]
                    dve.wait_ge(S("conv_left"), t * 2 + (1 + half))
                    dve.scalar_tensor_tensor(x[:, 0:T - 1], z[:, 1:T], p1("conv_w", t + (4 * JF + half * JF)), x[:, 0:T - 1],
                                             ALU.mult, ALU.add).then_inc(S("conv"), 1)
                dve.wait_ge(S("conv"), t * 2 + 2)
                dve.wait_ge(S("f_silu"), t + 1)
                dve.tensor_tensor(u_f[p], f_silu[p], conv[p][1], ALU.mult).then_inc(S("u_full"), 1)
                dve.wait_ge(S("u_hi"), t + 1)
                dve.tensor_tensor(y_lo[:, s * T:s * T + T], u_f[p], y_hi[:, s * T:s * T + T].bitcast(F32),
                                  ALU.subtract).then_inc(S("u_lo"), 1)

            for j in range(FFN_PEEL):
                c = ffn_first(j)
                lo(dve, Chunk(c, AHEAD))
                lo(dve, Chunk(c, 1 + AHEAD))
                if j >= 1:
                    ffn_tile(j - 1, (j - 1) % 2, (j - 1) % 4)
                if j >= 2:
                    lo(dve, Chunk(c, 2 + AHEAD))
            with dve.Fori(0, (JF - FFN_PEEL) // 4) as i:
                for u in range(4):
                    lo(dve, Chunk(ffn_first(FFN_PEEL), 3 * u + AHEAD, i, 12))
                    lo(dve, Chunk(ffn_first(FFN_PEEL), 3 * u + 1 + AHEAD, i, 12))
                    t = FFN_PEEL + u - 1
                    ffn_tile(i * 4 + t, t % 2, t % 4)
                    lo(dve, Chunk(ffn_first(FFN_PEEL), 3 * u + 2 + AHEAD, i, 12))
            lo(dve, Chunk(N_IN2 - 2, AHEAD))
            ffn_tile(JF - 1, (JF - 1) % 2, (JF - 1) % 4)
            lo(dve, Chunk(N_IN2 - 1, AHEAD))
            add_product(dve, lambda m: mod[:, 5 * KT + m:5 * KT + m + 1], N_IN2, LOW_BANKS)
            norm_mean(dve, 1)
            scale_residual(dve, 1, lambda m: p1("final", m))
            norm_mean(dve, 2)
            norm_input(dve, 2, 2, lambda m: p1("pre_mix", m))

            def values2(t):
                v = v_index(t)
                dve.wait_ge(S("v2_turned"), v + 1)
                z = psum[4 + v % 2][:, 0:T]
                if v == 0:
                    dve.tensor_copy(s_v, z).then_inc(S("v2"), 1)
                else:
                    x = (v - 1) * P
                    dve.tensor_copy(split2(r_v)[:, :, x:x + P], split2(z)).then_inc(S("v2"), 1)

            def centre_values():
                x = r_v.rearrange("p (n e) -> p n e", e=R_DV)
                dve.wait_ge(S("v2"), 9)
                dve.tensor_reduce(v_mean, x, AX, ALU.add).then_inc(S("v_sum"), 1)
                dve.wait_ge(S("v_sum"), 1)
                dve.tensor_scalar(v_mean, v_mean, 1.0 / R_DV, None, ALU.mult).then_inc(S("v_mean"), 1)
                dve.wait_ge(S("v_mean"), 1)
                dve.tensor_tensor(x, x, v_mean.rearrange("p (n o) -> p n o", o=1).broadcast_to([P, 8, R_DV]),
                                  ALU.subtract).then_inc(S("v_centred"), 1)

            def gates(t):
                n = t - T_GR + 1
                x = gate_dst(t)
                dve.wait_ge(S("gate_exp"), n)
                dve.tensor_scalar(x, x, 1.0, None, ALU.add).then_inc(S("gate_1"), 1)
                dve.wait_ge(S("gate_1"), n)
                if t >= T_GS:
                    dve.reciprocal(x, x).then_inc(S("gate"), 1)
                    return
                dve.reciprocal(x, x).then_inc(S("gate_r"), 1)
                dve.wait_ge(S("gate_r"), n)
                dve.tensor_tensor(x, psum[t % 4][:, 0:T], x, ALU.mult).then_inc(S("gate"), 1)

            def softmax_max(e):
                p = e % 2
                slope = 2.0 ** (-8.0 / S_HEADS * (e + 1))
                dve.wait_ge(S("s_scores"), e + 1)
                if e >= 2:
                    dve.wait_ge(S("s_exp"), 3 * (e - 1))
                dve.scalar_tensor_tensor(s_b[p], dist, -slope * S_DH ** 0.5, psum[5 + p][:, 0:3 * P], ALU.mult,
                                         ALU.add).then_inc(S("s_biased"), 1)
                dve.wait_ge(S("s_biased"), e + 1)
                dve.reduce_max(s_max[p][:, 0:1], s_b[p][:, 0:P], AX)
                dve.reduce_max(s_max[p][:, 1:2], s_b[p][:, P:3 * P], AX).then_inc(S("s_max"), 1)
                dve.wait_ge(S("s_max"), e + 1)
                dve.tensor_scalar(s_neg[p], s_max[p], -(S_DH ** -0.5), sink_neg[:, e:e + 1], ALU.mult,
                                  ALU.min).then_inc(S("s_neg"), 1)

            def softmax_norm(e):
                p = e % 2
                dve.wait_ge(S("s_exp"), 3 * e + 3)
                dve.tensor_tensor(s_den[p], s_sum[p], s_sink[p], ALU.add).then_inc(S("s_den"), 1)
                dve.wait_ge(S("s_den"), e + 1)
                dve.reciprocal(s_den[p], s_den[p]).then_inc(S("s_rden"), 1)
                dve.wait_ge(S("s_rden"), e + 1)
                for x, b in ((slice(0, P), 0), (slice(P, 3 * P), 1)):
                    dve.tensor_scalar(s_p[p][:, x], s_p[p][:, x], s_den[p][:, b:b + 1], None, ALU.mult).then_inc(S("p_norm"), 1)

            def swa_copy(e):
                q = S_DH * (e % 2)
                dve.wait_ge(S("pv"), e + 1)
                dve.tensor_copy(swa[q:q + S_DH, (e // 2) * T:(e // 2 + 1) * T], psum[4][q:q + S_DH, 0:T]).then_inc(S("swa"), 1)

            def ret_decay(r):
                dve.wait_ge(S("r_scores"), r + 1)
                if r >= 2:
                    dve.wait_ge(S("r_o"), r - 1)
                x = CON["decay"] + 3 * P * r
                dve.tensor_tensor(r_sc[r % 2], psum[5 + r % 2][:, 0:3 * P], con[:, x:x + 3 * P], ALU.mult).then_inc(S("r_sc"), 1)

            def ret_norm(r):
                dve.wait_ge(S("r_summed"), r + 1)
                dve.tensor_scalar(r_rs, psum[7][:, 0:T], 1.0 / R_DV, EPS, ALU.mult, ALU.add).then_inc(S("r_mean"), 1)
                dve.wait_ge(S("r_rstd"), r + 1)
                dve.tensor_tensor(split2(r_t), split2(psum[4][:, :]), over_tiles(r_rs, 2), ALU.mult).then_inc(S("r_normed"), 1)
                dve.wait_ge(S("r_normed"), r + 1)
                dve.tensor_tensor(r_t, r_t, silu_g[:, 2 * r * T:2 * (r + 1) * T], ALU.mult).then_inc(S("r_full"), 1)
                dve.wait_ge(S("r_hi"), r + 1)
                dve.tensor_tensor(y_lo[:, 2 * r * T:2 * (r + 1) * T], r_t, y_hi[:, 2 * r * T:2 * (r + 1) * T].bitcast(F32),
                                  ALU.subtract).then_inc(S("r_lo"), 1)

            dve.tensor_scalar(sink_neg, sink[:, :], -1.0, None, ALU.mult).then_inc(S("sink_neg"), 1)
            dve.wait_ge(S("sink_neg"), 1)
            for t in range(TILES_IN2 + 1):
                if t < TILES_IN2:
                    lo(dve, Chunk(N_IN2, t + AHEAD))
                if t >= 2 and v_index(t - 2) is not None:
                    values2(t - 2)
                if t == T_GR + 2:
                    centre_values()
                if t - 1 >= T_GR:
                    gates(t - 1)
                e = t - T_GR
                if 3 <= e <= S_HEADS + 2:
                    swa_copy(e - 3)
                if 1 <= e <= S_HEADS:
                    softmax_norm(e - 1)
                if 0 <= e < S_HEADS:
                    softmax_max(e)
                if e == S_HEADS + 3:
                    dve.wait_ge(S("swa_hi"), 1)
                    dve.tensor_tensor(h_lo[:, 8 * T:12 * T], swa, h_hi[:, 8 * T:12 * T].bitcast(F32),
                                      ALU.subtract).then_inc(S("swa_lo"), 1)
                r = t - RET_FIRST
                if r >= 3 and r % 2 == 1 and (r - 3) // 2 < R_HEADS:
                    ret_norm((r - 3) // 2)
                if 0 <= r < 2 * R_HEADS and r % 2 == 0:
                    ret_decay(r // 2)
            for n in range(N_SOUT, N_MOUT):
                lo(dve, Chunk(n, AHEAD))
                if n == N_ROUT:
                    dve.wait_ge(S("multiplied"), N_ROUT)
                    for b in range(4):
                        x = gate_s[:, b * 512:b * 512 + 512]
                        last = dve.tensor_tensor(x, psum[HIGH_BANKS[b]][:, :], x, ALU.mult)
                    last.then_inc(S("swa_gated"), 1)
            dve.wait_ge(S("swa_gated"), 1)
            dve.wait_ge(S("multiplied"), N_MOUT)
            for b in range(4):
                x = gate_r[:, b * 512:b * 512 + 512]
                dve.tensor_tensor(x, psum[b][:, :], x, ALU.mult).then_inc(S("ret_gated"), 1)
                dve.wait_ge(S("ret_gated"), b + 1)
                dve.tensor_tensor(x, x, gate_s[:, b * 512:b * 512 + 512], ALU.add).then_inc(S("mg_full"), 1)
                dve.wait_ge(S("mg_hi"), b + 1)
                dve.tensor_tensor(h_lo[:, b * 512:b * 512 + 512], x, h_hi[:, b * 512:b * 512 + 512].bitcast(F32),
                                  ALU.subtract).then_inc(S("mg_lo"), 1)
                lo(dve, Chunk(N_MOUT, b + AHEAD))
            for n in range(N_MOUT + 4, N_MLP):
                lo(dve, Chunk(n, AHEAD))
            norm_mean(dve, 3, bank=0)
            add_normed_product(dve, 3, lambda m: p1("post_mix", m), 0, HIGH_BANKS)
            norm_mean(dve, 4, bank=0)
            norm_input(dve, 4, 3, lambda m: p1("pre_mlp", m))

            def mlp_tile(t, p, s):
                dve.wait_ge(S("m_relu"), t + 1)
                dve.tensor_tensor(u_f[p], m_relu[p], m_relu[p], ALU.mult).then_inc(S("m_full"), 1)
                dve.wait_ge(S("m_hi"), t + 1)
                dve.tensor_tensor(y_lo[:, s * T:s * T + T], u_f[p], y_hi[:, s * T:s * T + T].bitcast(F32),
                                  ALU.subtract).then_inc(S("m_lo"), 1)

            for j in range(MLP_PEEL):
                lo(dve, Chunk(mlp_first(j), AHEAD))
                if j >= 1:
                    mlp_tile(j - 1, (j - 1) % 2, (j - 1) % 4)
                if j >= 2:
                    lo(dve, Chunk(mlp_first(j), 1 + AHEAD))
            with dve.Fori(0, (JM - MLP_PEEL) // 4 - 1) as i:
                for u in range(4):
                    lo(dve, Chunk(mlp_first(MLP_PEEL), 2 * u + AHEAD, i, 8))
                    t = MLP_PEEL + u - 1
                    mlp_tile(i * 4 + t, t % 2, t % 4)
                    lo(dve, Chunk(mlp_first(MLP_PEEL), 2 * u + 1 + AHEAD, i, 8))
            for j in range(JM - 4, JM):
                lo(dve, Chunk(mlp_first(j), AHEAD))
                mlp_tile(j - 1, (j - 1) % 2, (j - 1) % 4)
                lo(dve, Chunk(mlp_first(j), 1 + AHEAD))
            mlp_tile(JM - 1, (JM - 1) % 2, (JM - 1) % 4)
            norm_mean(dve, 5)
            add_normed_product(dve, 5, lambda m: p1("post_mlp", m), 1, LOW_BANKS)


def _columns(w):
    n = w.shape[1]
    return w.reshape(KT, P, n // P, P).transpose(2, 1, 0, 3).reshape(n // P, P, D)


def _rows(w):
    return w.reshape(-1, P, D)


def _vec(v):
    return v.reshape(-1, P).T


def _tiles(x):
    return x.T.reshape(KT, P, -1).transpose(1, 0, 2)


def kernel(**inputs):
    import concourse.bacc as bacc
    from concourse.bass_utils import run_bass_kernel_spmd as run

    a = {k: np.asarray(v) for k, v in inputs.items()}
    x, ctx = _tiles(a["x"][0]), _tiles(a["ctx"][0])
    tok = np.concatenate([x, ctx], axis=2).reshape(P, KT * TC)
    cc = np.stack([_vec(a["c"][0]), _vec(a["c_ctx"])], axis=2).reshape(P, 2 * KT)
    w = a["w_ada"][0].reshape(KT, P, 6, D)
    ada = np.concatenate([w[:, :, 1], w[:, :, 0], w[:, :, 2:5].transpose(0, 2, 1, 3).reshape(GROUPS * KT, P, D), w[:, :, 5]])

    hg = _columns(a["hg_w_in"][0]).reshape(5, HEADS, P, D)
    heads = np.stack([hg[1], hg[2], hg[0], hg[4]], axis=1).reshape(4 * HEADS, P, D)
    up = _columns(a["ffn_w_up"][0]).reshape(2, JF, P, D)
    down = _rows(a["ffn_w_down"][0])
    ffn = []
    for j in range(JF + 2):
        ffn += [up[0, j], up[1, j]] if j < JF else []
        ffn += [down[j - 2]] if j >= 2 else []
    w2 = a["w_in_2"][0]
    edges = np.cumsum([0, 512, 512, 1024, 1024, 512, 128, 128, D, D])
    r_q, r_k, r_v, r_g, s_q, s_k, s_v, g_r, g_s = (w2[:, i:j] for i, j in zip(edges[:-1], edges[1:]))
    s_q = s_q.reshape(D, 2, 4, S_DH).transpose(0, 2, 1, 3).reshape(D, 512)
    in2 = _columns(np.concatenate([s_q, s_k, s_v, r_q, r_k, r_v, r_g, g_s, g_r], axis=1))
    up2, down2 = _columns(a["w_up_2"][0]), _rows(a["w_down_2"][0])
    mlp = []
    for j in range(JM + 2):
        mlp += [up2[j]] if j < JM else []
        mlp += [down2[j - 2]] if j >= 2 else []
    stream = np.concatenate([hg[3], heads, _rows(a["hg_w_out"][0]), np.stack(ffn), in2, _rows(a["w_swa_out_2"][0]),
                             _rows(a["w_ret_out_2"][0]), _rows(a["w_out_2"][0]), np.stack(mlp)])
    lb = a["hg_lb_logits"]
    par = np.concatenate([_vec(v) for v in (
        a["norm_g"][0, 0], a["norm_g"][0, 1], a["b_ada"][0], lb[0], lb[1], a["hg_gnorm"][0], a["ffn_conv_w"][0],
        a["ffn_conv_b"][0], a["final_g"], a["pre_mix_norm_2"][0], a["post_mix_norm_2"][0], a["pre_mlp_norm_2"][0],
        a["post_mlp_norm_2"][0])], axis=1)
    con, msk = constants()
    arrays = {"tok": tok, "cc": cc, "ada": ada.reshape(ADA * P, D), "stream": stream.reshape(N_ALL * P, D), "par": par,
              "con": con, "msk": msk, "sink": a["sinks_2"][0]}
    arrays = {"in_" + k: np.ascontiguousarray(v) for k, v in arrays.items()}

    nc = bacc.Bacc("TRN2", target_bir_lowering=False, num_devices=1)
    args = [nc.dram_tensor(k, v.shape, mybir.dt.from_np(v.dtype), kind="ExternalInput").ap() for k, v in arrays.items()]
    args.append(nc.dram_tensor("out", (P, KT * T), F32, kind="ExternalOutput").ap())
    build(nc, *args)
    y = run(nc, [arrays], core_ids=[0]).results[0]["out"]
    return np.ascontiguousarray(y.reshape(P, KT, T).transpose(2, 1, 0).reshape(1, T, D))
```

```python
from contextlib import ExitStack

import numpy as np

import concourse.bass as bass
from concourse import mybir

F32 = mybir.dt.float32
F32R = mybir.dt.float32r
I32 = mybir.dt.int32
ACT = mybir.ActivationFunctionType
ALU = mybir.AluOpType
AX = mybir.AxisListType.X

P = 128
D = 1024
KT = D // P
T = 256
TC = 2 * T
EPS = 1e-6
RING = 4
AHEAD = 2
ADA = 6 * KT
ADA_FIRST = 2 * KT
GROUPS = 2
LATE = 2
HEADS = 8
CH = 64
HALF = CH // 2
NCH = T // CH
D_FF = 2816
JF = D_FF // P
R_HEADS = 4
R_DV = 256
S_HEADS = 8
S_DH = 64
D_FF2 = 4096
JM = D_FF2 // P

N_HEAD = ADA_FIRST + KT
N_HOUT = N_HEAD + 4 * HEADS
N_FFN = N_HOUT + KT
N_IN2 = N_FFN + 3 * JF
TILES_IN2 = 46
N_SOUT = N_IN2 + TILES_IN2
N_ROUT = N_SOUT + 4
N_MOUT = N_ROUT + KT
N_MLP = N_MOUT + KT
N_ALL = N_MLP + 2 * JM

T_QS, T_KS, T_VS, T_QR, T_KR, T_VR, T_GR, T_GS, T_GT = 0, 4, 5, 6, 10, 14, 22, 30, 38

PAR = {}
_at = 0
for _name, _n in (("norm1", 8), ("norm2", 8), ("b_ada", 48), ("lb0", 16), ("lb1", 16), ("gnorm", 1),
                  ("conv_w", 3 * 2 * JF), ("conv_b", 2 * JF), ("final", 8), ("pre_mix", 8),
                  ("post_mix", 8), ("pre_mlp", 8), ("post_mlp", 8)):
    PAR[_name] = _at
    _at += _n
N_PAR = _at

CON = {"ident": 0, "ones": P, "scan": 2 * P, "decay": 2 * P + 2 * TC, "dist": 2 * P + 2 * TC + 3 * P * R_HEADS}
N_CON = CON["dist"] + 3 * P
ARENA = 14080
FAR = 1e30


def constants():
    c = np.zeros((P, N_CON), np.float32)
    c[:, 0:P] = np.eye(P)
    c[:, P:2 * P] = 1.0
    scan = np.ones(TC, np.float32)
    scan[0:T:CH] = 0.0
    scan[T] = 0.0
    c[:, CON["scan"]:CON["scan"] + TC] = scan
    c[:, CON["scan"] + TC:CON["scan"] + 2 * TC] = np.roll(scan, T)
    j = np.arange(P)[:, None]
    i = np.arange(T)[None, :]
    for h in range(R_HEADS):
        lg = np.log(np.float32(1.0) - np.exp2(np.float32(-5.0 - h)))
        d0 = np.where(i >= j, np.exp(lg * np.maximum(i - j, 0)), 0.0)
        at = CON["decay"] + 3 * P * h
        c[:, at:at + T] = d0 * P ** -0.5
        c[:, at + T:at + 3 * P] = d0[:, :P] * P ** -0.5
    q = np.arange(P)[:, None]
    k = np.arange(P)[None, :]
    own = np.where(k <= q, q - k, FAR)
    prev = np.where(k > q, q + P - k, FAR)
    c[:, CON["dist"]:] = np.concatenate([own, prev, own], axis=1)
    j, i = np.arange(CH)[:, None], np.arange(CH)[None, :]
    m = np.zeros((2, CH, 2, 2, CH), np.int32)
    m[:, :, 0] = (j <= i).astype(np.int32)[None, :, None, :]
    m[:, :, 1] = (j >= i).astype(np.int32)[None, :, None, :]
    return c, m.reshape(P, 4 * CH)


OWN_TILES = (0, 1, 4)
POOL_TILES = (2, 3, 5, 6, 7)
IDLE = 10
TURN_BANKS = (6, 7, 4, 5)
HOUT_BANKS = (0, 1, 2, 4)
LOW_BANKS = (0, 1, 2, 3)
HIGH_BANKS = (4, 5, 6, 7)
FFN_PEEL = 6
MLP_PEEL = 4
SWA_FIRST = T_QR
RET_FIRST = SWA_FIRST + 2 * S_HEADS + 2
IN2_BANKS = 3
V_BANK = 3


def swa_at(t, after):
    e, odd = divmod(t - SWA_FIRST - after, 2)
    return e if odd == 0 and 0 <= e < S_HEADS else None


def ret_at(t, after):
    r, off = divmod(t - RET_FIRST - after, 4)
    return r if off == 0 and 0 <= r < R_HEADS else None


V_FIRST = KT + AHEAD
EARLY = KT + 1 + KT


def ada_number(i):
    return i if i < V_FIRST else i + 1


def value_number(j):
    return V_FIRST if j == 0 else 2 * KT + j


def ffn_first(j):
    return N_FFN + (2 * j if j < 2 else 3 * j - 2)


def mlp_first(j):
    return N_MLP + (j if j < 2 else 2 * j - 2)


def v_index(t):
    return 0 if t == T_VS else t - T_VR + 1 if T_VR <= t < T_GR else None


class Chunk:

    def __init__(self, base, m=0, i=0, per=0):
        assert per % RING == 0
        self.n = i * per + (base + m)
        self.slot = (base + m) % RING
        self.round = i * (per // RING) + (base + m) // RING
        self.least = base + m


def build(nc, tok_in, cc_in, ada_in, stream_in, par_in, con_in, msk_in, sink_in, out):
    ctx = ExitStack()
    with ctx:
        def sb(name, cols, dt=F32):
            return ctx.enter_context(nc.sbuf_tensor(name, [P, cols], dt))

        sems = {}

        def S(name):
            if name not in sems:
                sems[name] = ctx.enter_context(nc.semaphore(name))
            return sems[name]

        raw = [sb(f"raw{i}", D) for i in range(RING)]
        w_hi = [sb(f"w_hi{i}", D, F32R) for i in range(RING)]
        w_lo = [sb(f"w_lo{i}", D, F32R) for i in range(RING)]
        con = sb("con", N_CON)
        msk = sb("msk", 4 * CH, I32)
        par = sb("par", N_PAR)
        sink = sb("sink", S_HEADS)
        cc = sb("cc", 2 * KT)
        xres = sb("xres", KT * T)
        tok = sb("tok", KT * TC)
        wide = sb("wide", KT * TC)
        h_hi = sb("h_hi", KT * TC, F32R)
        h_lo = sb("h_lo", KT * TC, F32R)
        y_hi = sb("y_hi", KT * T, F32R)
        y_lo = sb("y_lo", KT * T, F32R)
        cs_w = sb("cs_w", 4 * KT, F32R)
        small = sb("small", 480)
        arena = sb("arena", ARENA)
        psum = [ctx.enter_context(nc.psum_tensor(f"bank{i}", [P, 512], F32)) for i in range(8)]

        ident = con[:, 0:P]
        ones = con[:, P:2 * P]
        scan_mask = [con[:, CON["scan"] + d * TC:CON["scan"] + (d + 1) * TC] for d in range(2)]
        dist = con[:, CON["dist"]:CON["dist"] + 3 * P]

        used = [0]

        def part(cols):
            used[0] += cols
            assert used[0] <= ARENA
            return arena[:, used[0] - cols:used[0]]

        def p1(name, k=0, n=1):
            return par[:, bass.ds(k + PAR[name], n)]

        used_small = [0]

        def tiny(cols):
            used_small[0] += cols
            assert used_small[0] <= 480
            return small[:, used_small[0] - cols:used_small[0]]

        cs = tiny(2 * KT)
        eps = tiny(1)
        lb = tiny(16)
        lb_om = tiny(16)
        lb_m = tiny(16)
        lb_d = tiny(32)
        mod = tiny(ADA)
        mod_c = tiny(ADA_FIRST)
        gain_l = tiny(KT)
        gain_c = tiny(KT)
        gain_2 = tiny(KT)
        eps_sq = tiny(1)
        final_sq = tiny(KT)
        final_pre = tiny(KT)
        sink_neg = tiny(S_HEADS)
        s_max = [tiny(2) for _ in range(2)]
        s_neg = [tiny(2) for _ in range(2)]
        s_sum = [tiny(2) for _ in range(2)]
        s_sink = [tiny(2) for _ in range(2)]
        s_den = [tiny(2) for _ in range(2)]
        v_mean = tiny(8)

        rstd = part(TC)
        f_buf = part(2 * TC)
        b_buf = part(2 * TC)
        k_buf = part(2 * TC)
        q_e = part(2 * T)
        q_d = [part(2 * T) for _ in range(2)]
        k_e = part(2 * T)
        k_d = part(2 * TC)
        qg = [part(2 * T) for _ in range(2)]
        k_dT = part(8 * P)
        state = part(8 * P)
        sc_T = part(8 * CH)
        v_cur = part(4 * P)
        o_sq = part(T)
        o_rs = part(T)
        o_n = part(T)
        y_f = part(T)
        late_sum = [xres[:, 0:D], part(D)]
        late_raw = [xres[:, D:2 * D], part(D)]
        used[0] = TC
        mod_sum = [part(D) for _ in range(GROUPS)]
        mod_raw = [part(D) for _ in range(2 * GROUPS)]
        assert used[0] <= 9728
        used[0] = 10240
        mod_rows = [part(512) for _ in range(4)]
        used[0] = TC
        conv = [[part(T) for _ in range(2)] for _ in range(2)]
        f_silu = [part(T) for _ in range(2)]
        u_f = [part(T) for _ in range(2)]
        m_relu = [part(T) for _ in range(2)]
        used[0] = TC
        s_q = part(4 * T)
        s_k = part(T)
        s_v = part(T)
        r_q = part(4 * T)
        r_k = part(4 * T)
        r_v = part(8 * T)
        gate_r = part(8 * T)
        s_b = [part(3 * P) for _ in range(2)]
        s_p = [part(3 * P) for _ in range(2)]
        s_pT = [part(3 * P) for _ in range(2)]
        swa = part(4 * T)
        r_sc = [part(3 * P) for _ in range(2)]
        r_t = wide[:, 0:8 * T]
        r_sq = part(2 * T)
        r_rs = wide[:, 8 * T:(8 + R_HEADS) * T]
        v_tmp = [part(T) for _ in range(2)]
        silu_g = tok[:, 0:KT * T]
        gate_s = tok[:, KT * T:2 * KT * T]

        def in2_dst(t):
            for first, n, dst in ((T_QS, 4, s_q), (T_KS, 1, s_k), (T_QR, 4, r_q), (T_KR, 4, r_k)):
                if first <= t < first + n:
                    return dst[:, (t - first) * T:(t - first + 1) * T]
            return None

        def gate_dst(t):
            dst, k = (silu_g, t - T_GR) if t < T_GS else (gate_s, t - T_GS) if t < T_GT else (gate_r, t - T_GT)
            return dst[:, k * T:(k + 1) * T]

        d1 = wide[:, 0:2 * T]
        qg_s = wide[:, 3072:3584]
        e_qe = wide[:, 512:1024]
        e_ke = wide[:, 1024:1536]
        e_qd = wide[:, 1536:2048]
        e_kd = wide[:, 2048:3072]

        def kv_at(d, s):
            c = s - 1 if d == 0 else NCH - s
            col = 0 if s == 0 else {(0, 1): 1, (0, 3): 2, (1, 2): 3, (0, 2): 1, (1, 1): 2, (1, 3): 3}[d, s]
            return psum[6 + (d if s == 0 else c % 2)][:, col * P:(col + 1) * P]

        v_all = tok
        cs_parts = cs_w[:, :].rearrange("p (k w) -> p k w", w=4)
        cs_pairs = cs.rearrange("p (k w) -> p k w", w=2)

        def move_values(engine_copy, i):
            half, tile = i // 4, i % 4
            dst = v_all[:, :].rearrange("p (h t v) -> p h t v", h=HEADS, t=4)[:, 4 * half:4 * half + 4, tile, :]
            return engine_copy(dst, psum[i][:, :].rearrange("p (h v) -> p h v", h=4))

        def hi(act, c):
            if c.least >= N_ALL:
                return
            act.wait_ge(S(f"loaded{c.slot}"), c.round * 16 + 16)
            if c.least >= RING:
                act.wait_ge(S("multiplied"), c.n - (RING - 1))
            act.activation(w_hi[c.slot][:, :], raw[c.slot][:, :], ACT.Copy).then_inc(S("split_hi"), 1)

        def lo(dve, c):
            if c.least >= N_ALL:
                return
            dve.wait_ge(S("split_hi"), c.n + 1)
            dve.tensor_tensor(w_lo[c.slot][:, :], raw[c.slot][:, :], w_hi[c.slot][:, :].bitcast(F32),
                              ALU.subtract).then_inc(S("split_lo"), 1)

        def three(pe, dst, w, cols, a_hi, a_lo, start, stop):
            hi_w, lo_w = w_hi[w][:, cols], w_lo[w][:, cols]
            pe.matmul(dst, hi_w, a_hi, start=start, stop=False, skip_group_check=True)
            pe.matmul(dst, hi_w, a_lo, start=False, stop=False, skip_group_check=True)
            return pe.matmul(dst, lo_w, a_hi, start=False, stop=stop, skip_group_check=True)

        def column_tile(pe, c, dst, width, n_tok, halfway=None):
            pe.wait_ge(S("split_lo"), c.n + 1)
            for k in range(KT):
                last = three(pe, dst, c.slot, slice(k * P, k * P + P), h_hi[:, k * width:k * width + n_tok],
                             h_lo[:, k * width:k * width + n_tok], k == 0, k == KT - 1)
                if halfway is not None and k == KT // 2 - 1:
                    halfway()
            last.then_inc(S("multiplied"), 1)

        def first_columns(pe, chunks, dsts, input_tiles):
            for c in chunks:
                pe.wait_ge(S("split_lo"), c.n + 1)
            for k in range(KT):
                pe.wait_ge(S("h_lo"), input_tiles + k + 1)
                x = slice(k * T, k * T + T)
                for c, dst in zip(chunks, dsts):
                    last = three(pe, dst, c.slot, slice(k * P, k * P + P), h_hi[:, x], h_lo[:, x], k == 0, k == KT - 1)
                    if k == KT - 1:
                        last.then_inc(S("multiplied"), 1)

        def row_tile(pe, c, banks, a_hi, a_lo, first, stop, halfway=None):
            pe.wait_ge(S("split_lo"), c.n + 1)
            for m in range(KT):
                last = three(pe, psum[banks[m // 2]][:, (m % 2) * T:(m % 2) * T + T], c.slot,
                             slice(m * P, m * P + P), a_hi, a_lo, first and m % 2 == 0, stop)
                if stop and m in (1, 3, 5):
                    last.then_inc(S("bank_done"), 1)
                if halfway is not None and m == KT // 2 - 1:
                    halfway()
            last.then_inc(S("multiplied"), 1)

        def wait_bank(engine, product, n_done, b):
            if b < 3:
                engine.wait_ge(S("bank_done"), 3 * product + b + 1)
            else:
                engine.wait_ge(S("multiplied"), n_done)

        def log_exp_tables(act):
            act.preload_act_table_set("natural_log_exp_and_others")

        def by_tile(x, n=KT):
            return x.rearrange("p (k t) -> p k t", k=n)

        def over_tiles(x, n=KT):
            return x.rearrange("p (o t) -> p o t", o=1).broadcast_to([P, n, x.shape[1]])

        def squares_before(k):
            return (k if k < 2 else k - 1) * KT

        def norm_sum(pe, k, bank=7):
            for m in range(KT):
                pe.wait_ge(S("norm_squares"), squares_before(k) + m + 1)
                last = pe.matmul(psum[bank][:, 0:T], ones, wide[:, m * T:m * T + T], start=m == 0, stop=m == KT - 1)
            last.then_inc(S("norm_summed"), 1)

        def keep_clock(pe, bank, n):
            for _ in range(n):
                pe.matmul(psum[bank][:, 0:P], ones, ones, start=True, stop=True, skip_group_check=True)

        def norm_rstd(act, k, bank=7, dst=rstd[:, 0:T], eps=eps):
            act.wait_ge(S("norm_summed"), k + 1)
            act.activation(dst, psum[bank][:, 0:T], ACT.Ln, scale=1.0 / D, bias=eps).then_inc(S("norm_log"), 1)
            act.wait_ge(S("norm_log"), k + 1)
            act.activation(dst, dst, ACT.Exp, scale=-0.5).then_inc(S("norm_rstd"), 1)

        def wait_residual(engine, update, m):
            if update < 3:
                engine.wait_ge(S("residual"), update * KT + m + 1)
            elif m < 4:
                engine.wait_ge(S("residual_pool"), 2 * (update - 3) + m // 2 + 1)
            else:
                engine.wait_ge(S("residual"), 3 * KT + 2 * (update - 3) + m // 2 - 1)

        def square_residual(act, update):
            for m in range(KT):
                wait_residual(act, update, m)
                act.activation(wide[:, m * T:m * T + T], xres[:, m * T:m * T + T], ACT.Square).then_inc(S("norm_squares"), 1)

        def square_banks(act, product, n_done, banks):
            for b in range(4):
                wait_bank(act, product, n_done, b)
                act.activation(wide[:, b * 512:b * 512 + 512], psum[banks[b]][:, :], ACT.Square).then_inc(S("norm_squares"), 2)

        def add_squares(dve, k, i):
            for b in (1, 2):
                dve.wait_ge(S("norm_squares"), squares_before(k) + 2 * b + 2)
                if b == 2:
                    dve.wait_ge(S("squares_added"), 2 * i + 1)
                dve.tensor_tensor(wide[:, 0:512], wide[:, 0:512], wide[:, b * 512:b * 512 + 512],
                                  ALU.add).then_inc(S("squares_added"), 1)

        def norm_sum_banks(pe, k, i, bank):
            pe.wait_ge(S("squares_added"), 2 * i + 2)
            for m in (0, 1, 6, 7):
                if m == 6:
                    pe.wait_ge(S("norm_squares"), squares_before(k) + 8)
                last = pe.matmul(psum[bank][:, 0:T], ones, wide[:, m * T:m * T + T], start=m == 0, stop=m == 7)
            last.then_inc(S("norm_summed"), 1)

        normed = wide[:, KT * T:2 * KT * T]

        final_rstd = rstd[:, T:2 * T]
        weighted = normed[:, (KT - 1) * T:KT * T]

        def add_weighted_squares(dve, m):
            square = wide[:, m * T:m * T + T]
            dve.wait_ge(S("norm_squares"), KT + m + 1)
            if m == 0:
                dve.wait_ge(S("final_weights"), 2)
                dve.tensor_scalar(weighted, square, final_sq[:, 0:1], None, ALU.mult).then_inc(S("weighted"), 1)
            else:
                dve.wait_ge(S("weighted"), m)
                dve.scalar_tensor_tensor(weighted, square, final_sq[:, m:m + 1], weighted, ALU.mult,
                                         ALU.add).then_inc(S("weighted"), 1)

        def weighted_sum(pe):
            pe.wait_ge(S("weighted"), KT)
            pe.matmul(psum[6][:, 0:T], ones, weighted, start=True, stop=True).then_inc(S("norm_summed"), 1)

        def scale_residual(dve, m):
            x = xres[:, m * T:m * T + T]
            if m == 0:
                dve.wait_ge(S("norm_rstd"), 2)
            dve.scalar_tensor_tensor(x, x, p1("final", m), final_rstd, ALU.mult, ALU.mult).then_inc(S("residual"), 1)

        def split_h_hi(act, q, shift=None):
            for m in range(KT):
                act.wait_ge(S("h_full"), (q - 1) * KT + m + 1)
                x, dst = normed[:, m * T:m * T + T], h_hi[:, m * T:m * T + T]
                if shift is None:
                    act.activation(dst, x, ACT.Copy).then_inc(S("h_hi"), 1)
                else:
                    act.activation(dst, x, ACT.Identity, bias=shift(m)).then_inc(S("h_hi"), 1)

        def norm_input(dve, q, gain, shift=None):
            behind = 2
            for m in range(KT + behind):
                if m < KT:
                    dve.scalar_tensor_tensor(normed[:, m * T:m * T + T], xres[:, m * T:m * T + T], gain(m), rstd[:, 0:T],
                                             ALU.mult, ALU.mult).then_inc(S("h_full"), 1)
                if m >= behind:
                    t = m - behind
                    x, dst = normed[:, t * T:t * T + T], h_lo[:, t * T:t * T + T]
                    high = h_hi[:, t * T:t * T + T].bitcast(F32)
                    dve.wait_ge(S("h_hi"), (q + 1) * KT + t + 1)
                    if shift is None:
                        dve.tensor_tensor(dst, x, high, ALU.subtract).then_inc(S("h_lo"), 1)
                    else:
                        dve.scalar_tensor_tensor(dst, x, shift(t), high, ALU.add, ALU.subtract).then_inc(S("h_lo"), 1)

        def add_product(dve, gain, product, n_done, banks, behind=None):
            for m in range(KT):
                if m % 2 == 0:
                    wait_bank(dve, product, n_done, m // 2)
                x = xres[:, m * T:m * T + T]
                dve.scalar_tensor_tensor(x, psum[banks[m // 2]][:, (m % 2) * T:(m % 2) * T + T], gain(m), x,
                                         ALU.mult, ALU.add).then_inc(S("residual"), 1)
                if behind is not None and m >= 2:
                    behind(m - 2)

        def product(m, banks):
            return psum[banks[m // 2]][:, (m % 2) * T:(m % 2) * T + T]

        def gain_product_act(act, gain, banks):
            for m in range(4):
                act.activation(normed[:, m * T:m * T + T], product(m, banks), ACT.Copy, scale=gain(m)).then_inc(S("gained_act"), 1)

        def add_normed_product(dve, k, i, gain, banks):
            for m in range(4, KT):
                dve.wait_ge(S("norm_squares"), squares_before(k) + 2 * (m // 2) + 2)
                dve.tensor_scalar(normed[:, m * T:m * T + T], product(m, banks), gain(m), None, ALU.mult).then_inc(S("gained_dve"), 1)
            dve.wait_ge(S("norm_rstd"), k + 1)
            for b in range(4):
                x = normed[:, b * 512:b * 512 + 512]
                if b < 2:
                    dve.wait_ge(S("gained_act"), 4 * i + 2 * b + 2)
                else:
                    dve.wait_ge(S("gained_dve"), 4 * i + 2 * b - 2)
                dve.tensor_tensor(by_tile(x, 2), by_tile(x, 2), over_tiles(rstd[:, 0:T], 2), ALU.mult).then_inc(S("product_normed"), 1)
                if b >= 2:
                    r = xres[:, b * 512:b * 512 + 512]
                    dve.wait_ge(S("product_normed"), 4 * i + b + 1)
                    dve.tensor_tensor(r, r, x, ALU.add).then_inc(S("residual"), 1)

        def add_normed_pool(pool, i):
            for b in range(2):
                r = xres[:, b * 512:b * 512 + 512]
                pool.wait_ge(S("product_normed"), 4 * i + b + 1)
                pool.tensor_tensor(r, r, normed[:, b * 512:b * 512 + 512], ALU.add).then_inc(S("residual_pool"), 1)

        block = ctx.enter_context(nc.Block())

        @block.sync
        def _(sp):
            def load(src, row, slot):
                sp.dma_start(raw[slot][:, :], src[bass.ds(row, P), :]).then_inc(S(f"loaded{slot}"), 16)

            def load_stream(i, first=0):
                for u in range(first, RING):
                    sp.wait_ge(S("split_lo"), i * RING + (u + 1 - RING))
                    load(stream_in, i * (RING * P) + u * P, u)

            sp.dma_start(cc[:, :], cc_in).then_inc(S("cc_in"), 16)
            load(stream_in, 0, 0)
            sp.dma_start(con[:, 0:2 * P], con_in[:, 0:2 * P]).then_inc(S("con_in"), 16)
            for n in range(1, RING):
                load(stream_in, n * P, n)
                x = slice((n - 1) * 2 * TC, n * 2 * TC)
                sp.dma_start(tok[:, x], tok_in[:, x]).then_inc(S(f"tok_in{n - 1}"), 16)
            sp.dma_start(tok[:, 6 * TC:8 * TC], tok_in[:, 6 * TC:8 * TC]).then_inc(S("tok_in3"), 16)
            sp.dma_start(par[:, :], par_in).then_inc(S("par_in"), 16)
            with sp.Fori(1, ADA_FIRST // RING) as i:
                load_stream(i)

            def load_one(n):
                sp.wait_ge(S("split_lo"), n - RING + 1)
                load(stream_in, n * P, n % RING)

            def load_mods(k):
                for g in range(GROUPS):
                    n = GROUPS * k + g
                    slot = n % (2 * GROUPS)
                    if k >= 2:
                        sp.wait_ge(S("mod_summed"), n - 2 * GROUPS + 1)
                    sp.dma_start(mod_raw[slot], ada_in[n * P:(n + 1) * P, :]).then_inc(S(f"mod_loaded{slot}"), 16)

            for n in range(ADA_FIRST, ADA_FIRST + 2 * AHEAD):
                load_one(n)
            load_mods(0)
            load_mods(1)
            for n in range(ADA_FIRST + 2 * AHEAD, ADA_FIRST + KT + AHEAD):
                load_one(n)
                if n >= ADA_FIRST + 3 * AHEAD:
                    load_mods(n - ADA_FIRST - 2 * AHEAD)
            load_mods(KT - 2)
            load_mods(KT - 1)
            late_row = GROUPS * KT * P
            i_head = N_HEAD // RING

            def load_late(g, row):
                sp.dma_start(late_raw[g], ada_in[bass.ds(row, P), :]).then_inc(S(f"late_in{g}"), 16)

            load_stream(i_head, AHEAD)
            for g in range(LATE):
                load_late(g, late_row + g * P)
            with sp.Fori(1, HEADS) as h:
                load_stream(h + i_head)
                for g in range(LATE):
                    sp.wait_ge(S("late_summed"), h * LATE + (g + 1 - LATE))
                    load_late(g, h * (LATE * P) + (late_row + g * P))
            with sp.Fori(i_head + HEADS, N_ALL // RING) as i:
                load_stream(i)
            for m in range(0, KT, 2):
                x = slice(m * T, (m + 2) * T)
                wait_residual(sp, 4, m)
                sp.dma_start(out[:, x], xres[:, x]).then_inc(S("stored"), 16)
            sp.wait_ge(S("stored"), 64)

        @block.scalar
        def _(act):
            act.preload_act_table_set("silu_and_others")
            act.wait_ge(S("cc_in"), 16)
            act.activation(cs, cc[:, :], ACT.Silu).then_inc(S("cs"), 1)
            act.wait_ge(S("cs"), 1)
            act.activation(cs_parts[:, :, 0:2], cs_pairs, ACT.Copy).then_inc(S("cs_hi"), 1)
            log_exp_tables(act)

            def copy_rows(q):
                act.wait_ge(S("multiplied"), ada_number(4 * q + 3) + 1)
                act.activation(mod_rows[q][0:4, :], psum[4 + q][0:4, :], ACT.Copy).then_inc(S("mod_rows"), 1)

            def modulate(k):
                act.wait_ge(S("mod_first"), k // 4 + 1)
                act.wait_ge(S("tok_normed"), k + 1)
                for at, gain, shift in ((k * TC, gain_l, mod), (k * TC + T, gain_c, mod_c)):
                    act.activation(h_hi[:, at:at + T], tok[:, at:at + T], ACT.Identity, scale=gain[:, k:k + 1],
                                   bias=shift[:, k:k + 1]).then_inc(S("h_hi"), 1)

            for n in range(KT):
                hi(act, Chunk(n))
                if n < 4:
                    x = slice(n * 2 * TC, (n + 1) * 2 * TC)
                    act.wait_ge(S(f"tok_in{n}"), 16)
                    act.activation(wide[:, x], tok[:, x], ACT.Square).then_inc(S("tok_squares"), 1)
                if n == 5:
                    act.wait_ge(S("lb_diff"), 1)
                    act.activation(lb_d, lb_d, ACT.Exp).then_inc(S("lb_exp"), 1)
                    copy_rows(0)
                if n == 7:
                    act.wait_ge(S("tok_summed"), 1)
                    act.wait_ge(S("eps"), 1)
                    act.activation(rstd, psum[1][:, :], ACT.Ln, scale=1.0 / D, bias=eps).then_inc(S("tok_log"), 1)
                    act.wait_ge(S("tok_log"), 1)
                    act.activation(rstd, rstd, ACT.Exp, scale=-0.5).then_inc(S("tok_rstd"), 1)
            hi(act, Chunk(KT))
            copy_rows(1)
            hi(act, Chunk(KT + 1))
            modulate(0)
            hi(act, Chunk(V_FIRST))
            modulate(1)
            hi(act, Chunk(V_FIRST + 1))
            modulate(2)
            modulate(3)
            for n in range(V_FIRST + 2, EARLY):
                hi(act, Chunk(n))
            copy_rows(2)
            hi(act, Chunk(EARLY))
            hi(act, Chunk(EARLY + 1))
            copy_rows(3)
            for k in range(4, KT):
                modulate(k)
                if k == 5:
                    hi(act, Chunk(EARLY + AHEAD))

            def move_even(first):
                for i in (first, first + 2):
                    act.wait_ge(S("v_bank"), i // 4 * 3 + i % 4 + 1)
                    move_values(lambda dst, src: act.activation(dst, src, ACT.Copy), i).then_inc(S("v_even"), 1)

            for n in range(EARLY + AHEAD + 1, N_HEAD):
                hi(act, Chunk(n))
            move_even(0)
            hi(act, Chunk(N_HEAD))
            hi(act, Chunk(N_HEAD, 1))
            move_even(4)
            act.dma_start(con[:, 2 * P:N_CON], con_in[:, 2 * P:N_CON]).then_inc(S("con_small_in"), 16)
            act.dma_start(msk[:, :], msk_in).then_inc(S("small_in"), 16)
            act.dma_start(sink[:, :], sink_in.partition_broadcast(P)).then_inc(S("small_in"), 16)

            def silu_parts(h, n_done):
                act.wait_ge(S("multiplied"), n_done)
                act.activation(qg_s, psum[2][:, :], ACT.Sigmoid).then_inc(S("qg_sigmoid"), 1)
                log_exp_tables(act)
                act.wait_ge(S("f"), h * 2 + 2)
                act.activation(f_buf, f_buf, ACT.Ln).then_inc(S("log_f"), 1)

            def exps(h, old):
                act.wait_ge(S("scanned"), h * 2 + 2)
                if old:
                    act.wait_ge(S("k_d"), h)
                    act.wait_ge(S("state"), h * 8)
                act.activation(e_qd.rearrange("p (d t) -> p d t", d=2),
                               b_buf.rearrange("p (d t) -> p d t", d=2)[:, :, 0:T], ACT.Exp).then_inc(S("e_qd"), 1)
                for d in range(2):
                    total = d * TC + (TC - 1 if d == 0 else T)
                    act.activation(e_kd[:, d * TC + T:(d + 1) * TC], b_buf[:, d * TC + T:(d + 1) * TC], ACT.Exp,
                                   scale=-1.0, bias=b_buf[:, total:total + 1]).then_inc(S("e_kc"), 1)
                act.wait_ge(S("d1"), h * 2 + 2)
                act.activation(e_qe, d1, ACT.Exp).then_inc(S("e_qe"), 1)
                act.activation(e_ke, d1, ACT.Exp, scale=-1.0).then_inc(S("e_ke"), 1)
                act.wait_ge(S("d3"), h * 2 + 2)
                x = e_kd.rearrange("p (d t) -> p d t", d=2)[:, :, 0:T]
                act.activation(x, x, ACT.Exp).then_inc(S("e_kd"), 1)

            def out_squares(h):
                act.wait_ge(S("o"), h + 1)
                act.activation(o_sq, psum[5][:, T:2 * T], ACT.Square).then_inc(S("o_squares"), 1)

            def out_rstd(h, total):
                act.wait_ge(S("o_summed"), h + 1)
                act.activation(o_rs, total, ACT.Ln, scale=1.0 / P, bias=eps).then_inc(S("o_log"), 1)
                act.wait_ge(S("o_log"), h + 1)
                act.activation(o_rs, o_rs, ACT.Exp, scale=-0.5).then_inc(S("o_rstd"), 1)

            def out_hi(h):
                act.wait_ge(S("y_full"), h + 1)
                act.activation(y_hi[:, bass.ds(h * T, T)], y_f, ACT.Copy).then_inc(S("y_hi"), 1)

            def copy_turned(n_done, src, dst):
                act.wait_ge(S("k_turned"), n_done)
                act.activation(dst, src, ACT.Copy).then_inc(S("k_dT"), 1)

            def head(h, at, prev, prev2):
                if prev:
                    silu_parts(h - 1, h * 4 + N_HEAD)
                hi(act, at(AHEAD))
                if prev:
                    exps(h - 1, prev2)
                if prev2:
                    out_squares(h - 2)
                hi(act, at(1 + AHEAD))
                if prev2:
                    out_rstd(h - 2, psum[2][:, T:2 * T])
                act.preload_act_table_set("sigmoid_and_others")
                if not prev:
                    act.wait_ge(S("mod_columns"), GROUPS)
                for d in range(2):
                    act.wait_ge(S("multiplied"), at(d).n + 1)
                    act.activation(f_buf[:, d * TC:(d + 1) * TC], psum[d][:, :], ACT.Sigmoid).then_inc(S("f_sigmoid"), 1)
                if prev2:
                    out_hi(h - 2)
                if prev:
                    copy_turned(h * 2 - 1, psum[3][:, :], k_dT[:, 0:512])
                    copy_turned(h * 2, psum[4][:, :], k_dT[:, 512:1024])
                hi(act, at(2 + AHEAD))
                act.wait_ge(S("f"), h * 2 + 2)
                if prev:
                    act.wait_ge(S("k_d"), h)
                act.activation(k_buf, f_buf, ACT.Copy, scale=-1.0, bias=1.0).then_inc(S("k"), 1)
                hi(act, at(3 + AHEAD))

            for h in range(2):
                head(h, lambda m: Chunk(N_HEAD, 4 * h + m), h >= 1, False)
            with act.Fori(0, (HEADS - 2) // 2) as i:
                for u in range(2):
                    head(i * 2 + (2 + u), lambda m: Chunk(N_HEAD + 8, 4 * u + m, i, 8), True, True)
            last_sum = psum[3][:, 0:T]
            silu_parts(HEADS - 1, N_HOUT)
            hi(act, Chunk(N_HOUT, 2))
            exps(HEADS - 1, True)
            out_squares(HEADS - 2)
            hi(act, Chunk(N_HOUT, 3))
            hi(act, Chunk(N_HOUT, 4))
            out_rstd(HEADS - 2, last_sum)
            hi(act, Chunk(N_HOUT, 5))
            copy_turned(2 * HEADS - 1, psum[3][:, :], k_dT[:, 0:512])
            act.wait_ge(S("late_columns"), LATE)
            act.dma_start(by_tile(xres[:, :]), by_tile(tok_in)[:, :, 0:T]).then_inc(S("xres_in"), 16)
            out_hi(HEADS - 2)
            copy_turned(2 * HEADS, psum[3][:, :], k_dT[:, 512:1024])
            hi(act, Chunk(N_HOUT, 6))
            hi(act, Chunk(N_HOUT, 7))
            out_squares(HEADS - 1)
            out_rstd(HEADS - 1, last_sum)
            hi(act, Chunk(N_FFN))
            out_hi(HEADS - 1)
            hi(act, Chunk(N_FFN, 1))
            square_residual(act, 0)
            norm_rstd(act, 0)
            split_h_hi(act, 1, lambda m: mod[:, 3 * KT + m:3 * KT + m + 1])

            def ffn_tile(t, p, s, n_done, has_old):
                act.wait_ge(S("multiplied"), n_done)
                if has_old:
                    act.wait_ge(S("u_full"), t - 1)
                for half in range(2):
                    act.activation(conv[p][half], psum[4 + 2 * half + p][:, 0:T], ACT.Identity,
                                   scale=p1("conv_w", t + (2 * JF + half * JF)),
                                   bias=p1("conv_b", t + half * JF)).then_inc(S("conv_mid"), 1)
                act.wait_ge(S("conv"), t * 2 + 2)
                act.activation(f_silu[p], conv[p][0], ACT.Silu).then_inc(S("f_silu"), 1)
                act.wait_ge(S("u_full"), t + 1)
                act.activation(y_hi[:, s * T:s * T + T], u_f[p], ACT.Copy).then_inc(S("u_hi"), 1)

            for j in range(FFN_PEEL):
                c = ffn_first(j)
                hi(act, Chunk(c, AHEAD))
                hi(act, Chunk(c, 1 + AHEAD))
                if j >= 1:
                    ffn_tile(j - 1, (j - 1) % 2, (j - 1) % 4, ffn_first(j - 1) + 2, j >= 3)
                if j >= 2:
                    hi(act, Chunk(c, 2 + AHEAD))
            with act.Fori(0, (JF - FFN_PEEL) // 4) as i:
                for u in range(4):
                    hi(act, Chunk(ffn_first(FFN_PEEL), 3 * u + AHEAD, i, 12))
                    hi(act, Chunk(ffn_first(FFN_PEEL), 3 * u + 1 + AHEAD, i, 12))
                    t = FFN_PEEL + u - 1
                    ffn_tile(i * 4 + t, t % 2, t % 4, i * 12 + (ffn_first(t) + 2), True)
                    hi(act, Chunk(ffn_first(FFN_PEEL), 3 * u + 2 + AHEAD, i, 12))
            ffn_tile(JF - 1, (JF - 1) % 2, (JF - 1) % 4, ffn_first(JF - 1) + 2, True)
            hi(act, Chunk(N_IN2 - 2, AHEAD))
            hi(act, Chunk(N_IN2 - 1, AHEAD))
            log_exp_tables(act)
            square_residual(act, 1)
            norm_rstd(act, 1, dst=final_rstd)
            norm_rstd(act, 2, bank=6, eps=eps_sq)
            split_h_hi(act, 2)

            def evacuate(t):
                act.wait_ge(S("multiplied"), N_IN2 + t + 1)
                z = psum[t % IN2_BANKS][:, 0:T]
                dst = in2_dst(t)
                if dst is not None:
                    act.activation(dst, z, ACT.Copy).then_inc(S("in2_copied"), 1)
                elif t < T_GR:
                    v = v_index(t)
                    if v >= 2:
                        act.wait_ge(S("v2_turned"), v - 1)
                    act.activation(v_tmp[v % 2], z, ACT.Copy).then_inc(S("in2_copied"), 1)
                elif t < T_GS:
                    act.activation(gate_dst(t), z, ACT.Sigmoid).then_inc(S("g_sigmoid"), 1)
                else:
                    act.activation(gate_dst(t), z, ACT.Sigmoid).then_inc(S("gate"), 1)

            def softmax_exp(e):
                p = e % 2
                act.wait_ge(S("s_neg"), e + 1)
                if e >= 2:
                    act.wait_ge(S("p_turned"), e - 1)
                act.activation(s_p[p][:, 0:P], s_b[p][:, 0:P], ACT.Exp, scale=S_DH ** -0.5, bias=s_neg[p][:, 0:1],
                               accum_out=s_sum[p][:, 0:1]).then_inc(S("s_exp"), 1)
                act.activation(s_p[p][:, P:3 * P], s_b[p][:, P:3 * P], ACT.Exp, scale=S_DH ** -0.5,
                               bias=s_neg[p][:, 1:2], accum_out=s_sum[p][:, 1:2]).then_inc(S("s_exp"), 1)
                act.activation(s_sink[p], s_neg[p], ACT.Exp, bias=sink[:, e:e + 1]).then_inc(S("s_exp"), 1)

            def probs_copy(e):
                act.wait_ge(S("p_turned"), e + 1)
                if e >= 2:
                    act.wait_ge(S("pv"), e - 1)
                act.activation(s_pT[e % 2], psum[7][:, 0:3 * P], ACT.Copy).then_inc(S("p_T"), 1)

            def ret_squares(r):
                act.wait_ge(S("r_o"), r + 1)
                if r >= 1:
                    act.wait_ge(S("r_summed"), r)
                act.activation(r_sq, psum[4][:, :], ACT.Square).then_inc(S("r_squares"), 1)

            def ret_rstd():
                act.wait_ge(S("r_mean"), R_HEADS)
                act.activation(r_rs, r_rs, ACT.Ln).then_inc(S("r_log"), 1)
                act.wait_ge(S("r_log"), 1)
                act.activation(r_rs, r_rs, ACT.Exp, scale=-0.5).then_inc(S("r_rstd"), 1)

            def ret_hi(r):
                act.wait_ge(S("r_full"), r + 1)
                x = slice(2 * r * T, 2 * (r + 1) * T)
                act.activation(y_hi[:, x], r_t[:, x], ACT.Copy).then_inc(S("r_hi"), 1)

            act.wait_ge(S("small_in"), 32)
            for t in range(TILES_IN2 + 1):
                if t < TILES_IN2:
                    hi(act, Chunk(N_IN2, t + AHEAD))
                e = swa_at(t, 2)
                if e is not None:
                    softmax_exp(e)
                if t == T_GR + 1:
                    act.preload_act_table_set("sigmoid_and_others")
                if t >= 1:
                    evacuate(t - 1)
                e = swa_at(t, 4)
                if e is not None:
                    probs_copy(e)
                if swa_at(t, 6) == S_HEADS - 1:
                    act.wait_ge(S("swa"), S_HEADS)
                    act.activation(h_hi[:, 8 * T:12 * T], swa, ACT.Copy).then_inc(S("swa_hi"), 1)
                r = ret_at(t, 3)
                if r is not None:
                    ret_squares(r)
            hi(act, Chunk(N_SOUT, AHEAD))
            log_exp_tables(act)
            ret_rstd()
            for n in range(N_SOUT, N_MOUT):
                if n > N_SOUT:
                    hi(act, Chunk(n, AHEAD))
                if n - N_SOUT < R_HEADS:
                    ret_hi(n - N_SOUT)
            for m in range(KT):
                act.wait_ge(S("mg_full"), m + 1)
                act.activation(h_hi[:, m * T:m * T + T], gate_r[:, m * T:m * T + T], ACT.Copy).then_inc(S("mg_hi"), 1)
                if m < 4:
                    hi(act, Chunk(N_MOUT, m + AHEAD))
            for n in range(N_MOUT + 4, N_MLP):
                hi(act, Chunk(n, AHEAD))
            square_banks(act, 4, N_MLP, HIGH_BANKS)
            gain_product_act(act, lambda m: p1("post_mix", m), HIGH_BANKS)
            norm_rstd(act, 3, bank=0)
            square_residual(act, 3)
            norm_rstd(act, 4, bank=0)
            split_h_hi(act, 3)

            def mlp_tile(t, p, s, n_done, has_old):
                act.wait_ge(S("multiplied"), n_done)
                if has_old:
                    act.wait_ge(S("m_full"), t - 1)
                act.activation(m_relu[p], psum[4 + p][:, 0:T], ACT.Relu).then_inc(S("m_relu"), 1)
                act.wait_ge(S("m_full"), t + 1)
                act.activation(y_hi[:, s * T:s * T + T], u_f[p], ACT.Copy).then_inc(S("m_hi"), 1)

            for j in range(MLP_PEEL):
                hi(act, Chunk(mlp_first(j), AHEAD))
                if j >= 1:
                    mlp_tile(j - 1, (j - 1) % 2, (j - 1) % 4, mlp_first(j - 1) + 1, j >= 3)
                if j >= 2:
                    hi(act, Chunk(mlp_first(j), 1 + AHEAD))
            with act.Fori(0, (JM - MLP_PEEL) // 4 - 1) as i:
                for u in range(4):
                    hi(act, Chunk(mlp_first(MLP_PEEL), 2 * u + AHEAD, i, 8))
                    t = MLP_PEEL + u - 1
                    mlp_tile(i * 4 + t, t % 2, t % 4, i * 8 + (mlp_first(t) + 1), True)
                    hi(act, Chunk(mlp_first(MLP_PEEL), 2 * u + 1 + AHEAD, i, 8))
            for j in range(JM - 4, JM):
                hi(act, Chunk(mlp_first(j), AHEAD))
                mlp_tile(j - 1, (j - 1) % 2, (j - 1) % 4, mlp_first(j - 1) + 1, True)
                hi(act, Chunk(mlp_first(j), 1 + AHEAD))
            mlp_tile(JM - 1, (JM - 1) % 2, (JM - 1) % 4, mlp_first(JM - 1) + 1, True)
            square_banks(act, 5, N_ALL, LOW_BANKS)
            gain_product_act(act, lambda m: p1("post_mlp", m), LOW_BANKS)
            norm_rstd(act, 5)

        @block.tensor
        def _(pe):
            pe.wait_ge(S("cs_lo"), 1)
            pe.wait_ge(S("con_in"), 16)

            def ada(i):
                c, q = Chunk(ada_number(i)), i // 4
                pe.wait_ge(S("split_lo"), c.n + 1)
                for b in range(2):
                    k = 2 * (i % 4) + b
                    for part_ in (w_hi, w_lo):
                        last = pe.matmul(psum[4 + q][0:4, :], cs_w[:, 4 * k:4 * k + 4], part_[c.slot][:, b * 512:b * 512 + 512],
                                         start=k == 0 and part_ is w_hi, stop=k == KT - 1 and part_ is w_lo,
                                         skip_group_check=True)
                last.then_inc(S("multiplied"), 1)

            def turn_rows(q):
                pe.wait_ge(S("mod_rows"), q + 1)
                for m in range(4):
                    last = pe.transpose(psum[TURN_BANKS[q]][:, 4 * m:4 * m + 4], mod_rows[q][0:4, m * P:m * P + P],
                                        ident[0:4, 0:4])
                last.then_inc(S("mod_turned"), 1)

            def values(j, halfway=None):
                c, half = Chunk(value_number(j)), j // 4
                pe.wait_ge(S("split_lo"), c.n + 1)
                for b in range(2):
                    k = 2 * (j % 4) + b
                    pe.wait_ge(S("h_lo"), 2 * k + 2)
                    for tile in range(4):
                        x = slice(k * TC + tile * P, k * TC + (tile + 1) * P)
                        for a, w in ((h_hi, w_hi), (h_hi, w_lo), (h_lo, w_hi)):
                            last = pe.matmul(psum[4 * half + tile][:, :], a[:, x], w[c.slot][:, b * 512:b * 512 + 512],
                                             start=k == 0 and w is w_hi and a is h_hi, stop=k == KT - 1 and a is h_lo,
                                             skip_group_check=True)
                        if k == KT - 1 and tile < 3:
                            last.then_inc(S("v_bank"), 1)
                    if b == 0 and halfway is not None:
                        halfway()
                last.then_inc(S("multiplied"), 1)

            for i in range(KT):
                ada(i)
                if i < 4:
                    pe.wait_ge(S("tok_squares"), i + 1)
                    for k in range(2 * i, 2 * i + 2):
                        last = pe.matmul(psum[1][:, :], ones, wide[:, k * TC:(k + 1) * TC], start=k == 0, stop=k == KT - 1)
                    if i == 3:
                        last.then_inc(S("tok_summed"), 1)
                if i == 5:
                    turn_rows(0)
            turn_rows(1)
            for i in range(KT, 2 * KT):
                if ada_number(i) == V_FIRST + 1:
                    values(0)
                ada(i)
                if i == KT + 6:
                    turn_rows(2)
            values(1, lambda: turn_rows(3))
            for j in range(2, KT):
                values(j)

            def mod_columns(total, dst, col):
                for m in range(KT):
                    last = pe.matmul(dst[:, col + m:col + m + 1], total[:, m * P:m * P + P], ones[:, 0:1], start=True, stop=True,
                                     skip_group_check=True)
                return last

            def out_sum(h, dst):
                pe.wait_ge(S("o_squares"), h + 1)
                pe.matmul(dst, ones, o_sq, start=True, stop=True, skip_group_check=True).then_inc(S("o_summed"), 1)

            def turn(p, part_, bank):
                for d in range(2):
                    for b in range(2):
                        at = d * TC + part_ * T + b * P
                        last = pe.transpose(psum[bank][:, (2 * d + b) * P:(2 * d + b + 1) * P], k_d[:, at:at + P], ident)
                last.then_inc(S("k_turned"), 1)

            def chunk_scores(p):
                for d in range(2):
                    behind, ahead = (HALF, 0) if d == 0 else (0, HALF)
                    for c in range(NCH):
                        x = d * T + c * CH
                        y = (2 * d + c // 2) * CH
                        row = CH * (c % 2)
                        pe.matmul(psum[5][row:row + CH, y + behind:y + behind + HALF], k_e[:, x:x + CH],
                                  q_e[:, x + behind:x + behind + HALF], start=True, stop=True, skip_group_check=True)
                        last = pe.matmul(psum[5][row + ahead:row + ahead + HALF, y + ahead:y + ahead + HALF],
                                         k_e[:, x + ahead:x + ahead + HALF], q_e[:, x + ahead:x + ahead + HALF],
                                         start=True, stop=True, skip_group_check=True)
                last.then_inc(S("scores"), 1)

            def key_values(h):
                pe.wait_ge(S("k_dT"), h * 2 + 2)
                pe.wait_ge(S("v_cur"), h + 1)
                for d in range(2):
                    for b in range(2):
                        x = 512 + (2 * d + b) * P
                        pe.matmul(psum[6 + d][:, 0:P], k_dT[:, x:x + P], v_cur[:, (2 + b) * P:(3 + b) * P],
                                  start=b == 0, stop=b == 1)
                    for s in range(1, NCH):
                        c = s - 1 if d == 0 else NCH - s
                        rows = slice(CH * (c % 2), CH * (c % 2) + CH)
                        x = (2 * d + c // 2) * P
                        last = pe.matmul(kv_at(d, s), k_dT[rows, x:x + P], v_cur[rows, (c // 2) * P:(c // 2 + 1) * P],
                                         start=True, stop=True, skip_group_check=True)
                last.then_inc(S("kv"), 1)

            def outputs(h, p):
                pe.wait_ge(S("masked"), h * 2 + 2)
                pe.wait_ge(S("state"), h * 8 + 8)
                for b in range(NCH // 2):
                    for d in range(2):
                        x = (NCH * d + 2 * b) * CH
                        pe.matmul(psum[5][:, T + b * P:T + b * P + P], v_cur[:, b * P:b * P + P], sc_T[:, x:x + P],
                                  start=d == 0, stop=False, skip_group_check=True)
                    for c in (2 * b, 2 * b + 1):
                        for d in range(2):
                            pos = c if d == 0 else NCH - 1 - c
                            last = pe.matmul(psum[5][:, T + c * CH:T + (c + 1) * CH], state[:, (4 * d + pos) * P:(4 * d + pos + 1) * P],
                                             q_d[p][:, d * T + c * CH:d * T + (c + 1) * CH],
                                             start=False, stop=d == 1, skip_group_check=True)
                last.then_inc(S("o"), 1)

            def early_columns(g):
                pe.wait_ge(S("mod_summed"), GROUPS * (KT - 1) + g + 1)
                mod_columns(mod_sum[g], psum[7], g * KT).then_inc(S("mod_columns"), 1)

            def head(h, u, at, prev, prev2):
                if prev:
                    pe.wait_ge(S("f_sigmoid"), h * 2)
                else:
                    pe.wait_ge(S("v_even"), 1)
                    pe.wait_ge(S("v_odd"), 1)
                column_tile(pe, at(0), psum[0][:, :], TC, TC)
                if prev2:
                    outputs(h - 2, u)

                def last_sum():
                    pe.wait_ge(S("qg"), h)
                    out_sum(h - 2, psum[2][:, T:2 * T])

                column_tile(pe, at(1), psum[1][:, :], TC, TC, halfway=last_sum if prev2 else None)
                if prev:
                    if not prev2:
                        pe.wait_ge(S("scores_cleared"), 1)
                    pe.wait_ge(S("k_d"), h)
                    turn(1 - u, 0, 3)
                    turn(1 - u, 1, 4)
                    if prev2:
                        pe.wait_ge(S("o_n"), h - 1)
                    chunk_scores(1 - u)
                    pe.wait_ge(S("qg"), h)
                else:
                    pe.wait_ge(S("v_even"), 4)
                    pe.wait_ge(S("v_odd"), 4)
                    early_columns(0)
                column_tile(pe, at(2), psum[2][:, 0:T], TC, T)
                if not prev:
                    early_columns(1)
                if prev:
                    key_values(h - 1)
                column_tile(pe, at(3), psum[2][:, T:2 * T], TC, T)

            for h in range(2):
                head(h, h, lambda m: Chunk(N_HEAD, 4 * h + m), h >= 1, False)
            with pe.Fori(0, (HEADS - 2) // 2) as i:
                for u in range(2):
                    head(i * 2 + (2 + u), u, lambda m: Chunk(N_HEAD + 8, 4 * u + m, i, 8), True, True)

            def out_row(k, halfway=None):
                pe.wait_ge(S("y_lo"), k + 1)
                row_tile(pe, Chunk(N_HOUT, k), HOUT_BANKS, y_hi[:, k * T:k * T + T], y_lo[:, k * T:k * T + T],
                         k == 0, k == KT - 1, halfway)

            def turn_context():
                pe.wait_ge(S("k_dT"), 2 * HEADS - 1)
                turn(1, 1, 3)

            outputs(HEADS - 2, 0)
            pe.wait_ge(S("f_sigmoid"), 2 * HEADS)
            pe.wait_ge(S("qg"), HEADS)
            for g in range(LATE):
                out_row(g)
                pe.wait_ge(S("late_summed"), LATE * HEADS)
                mod_columns(late_sum[g], psum[6], g * KT).then_inc(S("late_columns"), 1)
            out_sum(HEADS - 2, psum[3][:, 0:T])
            out_row(2)
            pe.wait_ge(S("k_d"), HEADS)
            pe.wait_ge(S("o_n"), HEADS - 1)
            turn(1, 0, 3)
            chunk_scores(1)
            out_row(3, turn_context)
            pe.wait_ge(S("mod_all"), 1)
            key_values(HEADS - 1)
            out_row(4)
            outputs(HEADS - 1, 1)
            out_row(5, lambda: out_sum(HEADS - 1, psum[3][:, 0:T]))
            out_row(6)
            out_row(7)
            norm_sum(pe, 0)
            keep_clock(pe, HOUT_BANKS[0], IDLE)

            def ffn_up(j, p, c, has_old, first=False):
                if first:
                    first_columns(pe, c, [psum[4][:, 0:T], psum[6][:, 0:T]], 2 * KT)
                    return
                if has_old:
                    pe.wait_ge(S("conv"), j * 2 - 2)
                column_tile(pe, c[0], psum[4 + p][:, 0:T], T, T)
                column_tile(pe, c[1], psum[6 + p][:, 0:T], T, T)

            def ffn_down(t, s, c, first, last):
                pe.wait_ge(S("u_lo"), t + 1)
                row_tile(pe, c, LOW_BANKS, y_hi[:, s * T:s * T + T], y_lo[:, s * T:s * T + T], first, last)

            for j in range(FFN_PEEL):
                c = ffn_first(j)
                ffn_up(j, j % 2, [Chunk(c), Chunk(c, 1)], j >= 2, j == 0)
                if j >= 2:
                    ffn_down(j - 2, (j - 2) % 4, Chunk(c, 2), j == 2, False)
            with pe.Fori(0, (JF - FFN_PEEL) // 4) as i:
                for u in range(4):
                    j = FFN_PEEL + u
                    c = [Chunk(ffn_first(FFN_PEEL), 3 * u + m, i, 12) for m in range(3)]
                    ffn_up(i * 4 + j, j % 2, c, True)
                    ffn_down(i * 4 + (j - 2), (j - 2) % 4, c[2], False, False)
            for t in range(JF - 2, JF):
                ffn_down(t, t % 4, Chunk(N_IN2 - JF + t), False, t == JF - 1)
            norm_sum(pe, 1)
            weighted_sum(pe)
            keep_clock(pe, LOW_BANKS[0], IDLE)

            def turn_values(t):
                v = v_index(t)
                pe.wait_ge(S("in2_copied"), t + 1)
                if v >= 1:
                    pe.wait_ge(S("v2"), v)
                for b in range(2):
                    last = pe.transpose(psum[V_BANK][:, b * P:b * P + P], v_tmp[v % 2][:, b * P:b * P + P], ident)
                last.then_inc(S("v2_turned"), 1)

            def swa_scores(e):
                g, x = e // 4, (e % 4) * T
                rows = slice(S_DH * g, S_DH * g + S_DH)
                if e == 0:
                    pe.wait_ge(S("in2_copied"), T_VS)
                if e >= 2:
                    pe.wait_ge(S("s_biased"), e - 1)
                dst = psum[5 + e % 2]
                pe.matmul(dst[:, 0:P], s_q[rows, x:x + P], s_k[rows, 0:P], start=True, stop=True, skip_group_check=True)
                pe.matmul(dst[:, P:3 * P], s_q[rows, x + P:x + T], s_k[rows, 0:T], start=True, stop=True,
                          skip_group_check=True).then_inc(S("s_scores"), 1)

            def turn_probs(e):
                pe.wait_ge(S("p_norm"), 2 * e + 2)
                if e >= 1:
                    pe.wait_ge(S("p_T"), e)
                for b in range(3):
                    last = pe.transpose(psum[7][:, b * P:b * P + P], s_p[e % 2][:, b * P:b * P + P], ident)
                last.then_inc(S("p_turned"), 1)

            def swa_values(e):
                g, q = e // 4, S_DH * (e % 2)
                pe.wait_ge(S("p_T"), e + 1)
                if e == 0:
                    pe.wait_ge(S("v2"), 1)
                if e >= 2:
                    pe.wait_ge(S("swa"), e - 1)
                pe.matmul(psum[4][q:q + S_DH, 0:T], s_v[:, S_DH * g:S_DH * g + S_DH], s_pT[e % 2][:, 0:T],
                          start=True, stop=False, skip_group_check=True)
                pe.matmul(psum[4][q:q + S_DH, P:T], s_v[:, P + S_DH * g:P + S_DH * g + S_DH], s_pT[e % 2][:, T:3 * P],
                          start=False, stop=True, skip_group_check=True).then_inc(S("pv"), 1)

            def ret_scores(r):
                dst = psum[5 + r % 2]
                if r == 0:
                    pe.wait_ge(S("s_biased"), S_HEADS)
                if r >= 2:
                    pe.wait_ge(S("r_sc"), r - 1)
                pe.matmul(dst[:, 0:T], r_k[:, r * T:r * T + P], r_q[:, r * T:(r + 1) * T], start=True, stop=True,
                          skip_group_check=True)
                pe.matmul(dst[:, T:3 * P], r_k[:, r * T + P:(r + 1) * T], r_q[:, r * T + P:(r + 1) * T], start=True,
                          stop=True, skip_group_check=True).then_inc(S("r_scores"), 1)

            def ret_values(r):
                pe.wait_ge(S("r_sc"), r + 1)
                if r == 0:
                    pe.wait_ge(S("swa"), S_HEADS)
                    pe.wait_ge(S("v_centred"), 1)
                else:
                    pe.wait_ge(S("r_gated"), r)
                    pe.wait_ge(S("r_squares"), r)
                for m in range(2):
                    x = r * R_DV + m * P
                    pe.matmul(psum[4][:, m * T:m * T + T], r_v[:, x:x + P], r_sc[r % 2][:, 0:T], start=True, stop=False,
                              skip_group_check=True)
                    last = pe.matmul(psum[4][:, m * T + P:m * T + T], r_v[:, 4 * T + x:4 * T + x + P],
                                     r_sc[r % 2][:, T:3 * P], start=False, stop=True, skip_group_check=True)
                last.then_inc(S("r_o"), 1)

            def ret_sum(r):
                pe.wait_ge(S("r_added"), r + 1)
                if r == 0:
                    pe.wait_ge(S("p_T"), S_HEADS)
                else:
                    pe.wait_ge(S("r_mean"), r)
                pe.matmul(psum[7][:, 0:T], ones, r_sq[:, 0:T], start=True, stop=True).then_inc(S("r_summed"), 1)

            for t in range(TILES_IN2):
                old = t - IN2_BANKS
                if 0 <= old < T_GR:
                    pe.wait_ge(S("in2_copied"), old + 1)
                elif T_GR <= old < T_GS:
                    pe.wait_ge(S("g_silu"), old - T_GR + 1)
                elif old >= T_GS:
                    pe.wait_ge(S("gate"), old - T_GS + 1)
                if t == 0:
                    first_columns(pe, [Chunk(N_IN2), Chunk(N_IN2, 1)], [psum[0][:, 0:T], psum[1][:, 0:T]], 3 * KT)
                elif t >= 2:
                    column_tile(pe, Chunk(N_IN2, t), psum[t % IN2_BANKS][:, 0:T], T, T)
                if t >= 1 and v_index(t - 1) is not None:
                    turn_values(t - 1)
                for after, step in ((0, swa_scores), (3, turn_probs), (4, swa_values)):
                    if swa_at(t, after) is not None:
                        step(swa_at(t, after))
                for after, step in ((0, ret_scores), (2, ret_values), (4, ret_sum)):
                    if ret_at(t, after) is not None:
                        step(ret_at(t, after))

            pe.wait_ge(S("swa_lo"), 1)
            pe.wait_ge(S("r_mean"), R_HEADS)
            pe.wait_ge(S("r_squares"), R_HEADS)
            for k in range(4):
                x = slice((8 + k) * T, (9 + k) * T)
                row_tile(pe, Chunk(N_SOUT, k), HIGH_BANKS, h_hi[:, x], h_lo[:, x], k == 0, k == 3)
            pe.wait_ge(S("gate"), TILES_IN2 - T_GS)
            for k in range(KT):
                x = slice(k * T, (k + 1) * T)
                pe.wait_ge(S("r_lo"), k // 2 + 1)
                row_tile(pe, Chunk(N_ROUT, k), LOW_BANKS, y_hi[:, x], y_lo[:, x], k == 0, k == KT - 1)
            for k in range(KT):
                x = slice(k * T, (k + 1) * T)
                pe.wait_ge(S("mg_lo"), k + 1)
                row_tile(pe, Chunk(N_MOUT, k), HIGH_BANKS, h_hi[:, x], h_lo[:, x], k == 0, k == KT - 1)
            norm_sum_banks(pe, 3, 0, bank=0)
            keep_clock(pe, LOW_BANKS[1], IDLE)
            norm_sum(pe, 4, bank=0)
            keep_clock(pe, LOW_BANKS[1], IDLE)

            def mlp_up(j, p, c, has_old):
                if has_old:
                    pe.wait_ge(S("m_relu"), j - 1)
                column_tile(pe, c, psum[4 + p][:, 0:T], T, T)

            def mlp_down(t, s, c, first, last):
                pe.wait_ge(S("m_lo"), t + 1)
                row_tile(pe, c, LOW_BANKS, y_hi[:, s * T:s * T + T], y_lo[:, s * T:s * T + T], first, last)

            first_columns(pe, [Chunk(mlp_first(j)) for j in range(2)], [psum[4][:, 0:T], psum[5][:, 0:T]], 4 * KT)
            for j in range(2, MLP_PEEL):
                mlp_up(j, j % 2, Chunk(mlp_first(j)), True)
                mlp_down(j - 2, (j - 2) % 4, Chunk(mlp_first(j), 1), j == 2, False)
            with pe.Fori(0, (JM - MLP_PEEL) // 4) as i:
                for u in range(4):
                    j = MLP_PEEL + u
                    mlp_up(i * 4 + j, j % 2, Chunk(mlp_first(MLP_PEEL), 2 * u, i, 8), True)
                    mlp_down(i * 4 + (j - 2), (j - 2) % 4, Chunk(mlp_first(MLP_PEEL), 2 * u + 1, i, 8), False, False)
            for t in range(JM - 2, JM):
                mlp_down(t, t % 4, Chunk(N_ALL - JM + t), False, t == JM - 1)
            norm_sum_banks(pe, 5, 1, bank=7)

        @block.gpsimd
        def _(pool):
            pool.wait_ge(S("tok_rstd"), 1)
            def norm_tokens(k):
                x = tok[:, k * TC:(k + 1) * TC]
                pool.tensor_tensor(x, x, rstd, ALU.mult).then_inc(S("tok_normed"), 1)

            def modulate(k):
                for half, (at, gain, shift) in enumerate(((k * TC, gain_l, mod), (k * TC + T, gain_c, mod_c))):
                    pool.wait_ge(S("h_hi"), 2 * k + half + 1)
                    x = tok[:, at:at + T]
                    pool.tensor_scalar(x, x, gain[:, k:k + 1], shift[:, k:k + 1], ALU.mult, ALU.add).then_inc(S("modulated"), 1)

            for k in range(KT - 2):
                norm_tokens(k)
            for k in POOL_TILES[:2]:
                modulate(k)
            for k in range(KT - 2, KT):
                norm_tokens(k)
            for k in POOL_TILES[2:]:
                modulate(k)
            for i in range(2):
                add_normed_pool(pool, i)

        @block.vector
        def _(dve):
            def mod_row(k, dst, src, first):
                c_k = cs[:, bass.ds(2 * k, 1)]
                if first:
                    return dve.tensor_scalar(dst, src, c_k, None, ALU.mult)
                return dve.scalar_tensor_tensor(dst, src, c_k, dst, ALU.mult, ALU.add)

            def mod_tiles(k):
                for g in range(GROUPS):
                    n = GROUPS * k + g
                    slot = n % (2 * GROUPS)
                    dve.wait_ge(S(f"mod_loaded{slot}"), 16 * (k // 2 + 1))
                    if k >= 1:
                        dve.wait_ge(S("mod_summed"), n - GROUPS + 1)
                    mod_row(k, mod_sum[g], mod_raw[slot], k == 0).then_inc(S("mod_summed"), 1)

            dve.memset(eps_sq, EPS * EPS)
            dve.memset(eps, EPS).then_inc(S("eps"), 1)
            dve.memset(sc_T, 0.0)
            dve.wait_ge(S("cs_hi"), 1)
            dve.tensor_tensor(cs_parts[:, :, 2:4], cs_pairs, cs_parts[:, :, 0:2].bitcast(F32),
                              ALU.subtract).then_inc(S("cs_lo"), 1)

            def quarter(q):
                at = KT - 4 * (q % 2) * 2 + 4 * (q // 2)
                x, tiles = slice(at, at + 4), slice(4 * (q // 2), 4 * (q // 2) + 4)
                turned = psum[TURN_BANKS[q]][:, 0:16].rearrange("p (m w) -> p m w", w=4)
                dve.wait_ge(S("mod_turned"), q + 1)
                for w, dst in ((0, mod), (1, mod_c)):
                    dve.tensor_tensor(dst[:, x], turned[:, :, w], p1("b_ada", at, 4), ALU.add).then_inc(S("quarter_part"), 1)
                for w, dst in ((0, mod), (1, mod_c)):
                    dve.wait_ge(S("quarter_part"), 2 * q + w + 1)
                    last = dve.tensor_tensor(dst[:, x], turned[:, :, w + 2], dst[:, x], ALU.add)
                    if q % 2 == 0:
                        last.then_inc(S("scale_first"), 1)
                if q % 2 == 1:
                    last.then_inc(S("mod_first"), 1)
                    return
                dve.wait_ge(S("scale_first"), q + 2)
                for gain, scale in ((gain_l, mod), (gain_c, mod_c)):
                    dve.scalar_tensor_tensor(gain[:, tiles], scale[:, x], 1.0, p1("norm1", 4 * (q // 2), 4), ALU.add, ALU.mult)

            def token_rest(k):
                for half, (at, gain, shift) in enumerate(((k * TC, gain_l, mod), (k * TC + T, gain_c, mod_c))):
                    dve.wait_ge(S("h_hi"), 2 * k + half + 1)
                    x = tok[:, at:at + T]
                    if k in OWN_TILES:
                        dve.tensor_scalar(x, x, gain[:, k:k + 1], shift[:, k:k + 1], ALU.mult, ALU.add).then_inc(S("first_modulated"), 1)
                if k in OWN_TILES:
                    dve.wait_ge(S("first_modulated"), 2 * OWN_TILES.index(k) + 2)
                else:
                    dve.wait_ge(S("modulated"), 2 * POOL_TILES.index(k) + 2)
                x = slice(k * TC, (k + 1) * TC)
                dve.tensor_tensor(h_lo[:, x], tok[:, x], h_hi[:, x].bitcast(F32), ALU.subtract).then_inc(S("h_lo"), 2)

            for n in range(KT):
                lo(dve, Chunk(n))
                if n == 3:
                    dve.wait_ge(S("par_in"), 16)
                    dve.tensor_tensor(lb_m, p1("lb0", 0, 16), p1("lb1", 0, 16), ALU.max).then_inc(S("lb_max"), 1)
                    dve.wait_ge(S("lb_max"), 1)
                    dve.tensor_tensor(lb_d[:, 0:16], p1("lb0", 0, 16), lb_m, ALU.subtract)
                    dve.tensor_tensor(lb_d[:, 16:32], p1("lb1", 0, 16), lb_m, ALU.subtract).then_inc(S("lb_diff"), 1)
            quarter(0)
            lo(dve, Chunk(KT))
            quarter(1)
            dve.wait_ge(S("mod_first"), 1)
            lo(dve, Chunk(KT + 1))
            token_rest(0)
            lo(dve, Chunk(V_FIRST))
            token_rest(1)
            lo(dve, Chunk(V_FIRST + 1))
            token_rest(2)
            token_rest(3)
            for n in range(V_FIRST + 2, EARLY):
                lo(dve, Chunk(n))
            lo(dve, Chunk(EARLY))
            quarter(2)
            lo(dve, Chunk(EARLY + 1))
            quarter(3)
            dve.wait_ge(S("mod_first"), 2)
            for k in range(4, KT):
                token_rest(k)
                if k == 5:
                    lo(dve, Chunk(EARLY + AHEAD))
            dve.wait_ge(S("lb_exp"), 1)
            dve.tensor_tensor(lb_m, lb_d[:, 0:16], lb_d[:, 16:32], ALU.add).then_inc(S("lb_sum"), 1)
            dve.wait_ge(S("lb_sum"), 1)
            dve.reciprocal(lb_m, lb_m).then_inc(S("lb_r"), 1)
            dve.wait_ge(S("lb_r"), 1)
            dve.tensor_tensor(lb, lb_d[:, 0:16], lb_m, ALU.mult).then_inc(S("lb"), 1)
            dve.wait_ge(S("lb"), 1)
            dve.tensor_scalar(lb_om, lb, -1.0, 1.0, ALU.mult, ALU.add).then_inc(S("lb_om"), 1)

            def move_odd(first):
                for i in (first, first + 2):
                    if i % 4 < 3:
                        dve.wait_ge(S("v_bank"), i // 4 * 3 + i % 4 + 1)
                    else:
                        dve.wait_ge(S("multiplied"), value_number(4 * (i // 4) + 3) + 1)
                    move_values(dve.tensor_copy, i).then_inc(S("v_odd"), 1)

            for k in range(4):
                lo(dve, Chunk(EARLY + AHEAD + 1 + k))
                mod_tiles(k)
            move_odd(1)
            for k in range(4, KT):
                if k < 6:
                    lo(dve, Chunk(N_HEAD, k - 4))
                mod_tiles(k)
            move_odd(5)
            dve.wait_ge(S("v_odd"), 3)
            dve.memset(psum[5][:, 0:T], 0.0).then_inc(S("scores_cleared"), 1)
            def split2(x):
                return x.rearrange("p (d t) -> p d t", d=2)

            def chunks(x):
                return x.rearrange("p (c t) -> p c t", c=NCH)

            def distances(h):
                dve.wait_ge(S("scanned"), h * 2 + 2)
                for d in range(2):
                    b = chunks(b_buf[:, d * TC:d * TC + T])
                    at = CH // 2 if d == 0 else CH - 1 - CH // 2
                    dve.tensor_tensor(chunks(d1[:, d * T:(d + 1) * T]), b, b[:, :, at:at + 1].broadcast_to([P, NCH, CH]),
                                      ALU.subtract).then_inc(S("d1"), 1)
                for d in range(2):
                    b = chunks(b_buf[:, d * TC:d * TC + T])
                    at = CH - 1 if d == 0 else 0
                    dve.tensor_tensor(chunks(e_kd[:, d * TC:d * TC + T]), b[:, :, at:at + 1].broadcast_to([P, NCH, CH]), b,
                                      ALU.subtract).then_inc(S("d3"), 1)

            def silu_qg(h, p):
                dve.wait_ge(S("qg_sigmoid"), h + 1)
                dve.tensor_tensor(qg[p], psum[2][:, :], qg_s, ALU.mult).then_inc(S("qg"), 1)

            def scale_qk(h, p):
                dve.wait_ge(S("qg"), h + 1)
                q = over_tiles(qg[p][:, 0:T], 2)
                dve.wait_ge(S("e_qd"), h + 1)
                dve.tensor_tensor(split2(q_d[p]), split2(e_qd), q, ALU.mult)
                dve.wait_ge(S("e_qe"), h + 1)
                dve.tensor_tensor(split2(q_e), split2(e_qe), q, ALU.mult)
                dve.wait_ge(S("e_ke"), h + 1)
                dve.wait_ge(S("k"), h + 1)
                dve.tensor_tensor(split2(k_e), split2(e_ke), split2(k_buf)[:, :, 0:T], ALU.mult)
                dve.wait_ge(S("e_kd"), h + 1)
                dve.tensor_tensor(k_d, e_kd, k_buf, ALU.mult).then_inc(S("k_d"), 1)

            def out_gated(h, p):
                dve.wait_ge(S("o_rstd"), h + 1)
                dve.tensor_tensor(o_n, psum[5][:, T:2 * T], o_rs, ALU.mult).then_inc(S("o_n"), 1)
                dve.wait_ge(S("o_n"), h + 1)
                dve.scalar_tensor_tensor(y_f, o_n, p1("gnorm"), qg[p][:, T:2 * T], ALU.mult, ALU.mult).then_inc(S("y_full"), 1)

            def out_lo(h):
                dve.wait_ge(S("y_hi"), h + 1)
                dve.tensor_tensor(y_lo[:, bass.ds(h * T, T)], y_f, y_hi[:, bass.ds(h * T, T)].bitcast(F32),
                                  ALU.subtract).then_inc(S("y_lo"), 1)

            def forget(h):
                for d in range(2):
                    dve.wait_ge(S("f_sigmoid"), h * 2 + (d + 1))
                    x = f_buf[:, d * TC:(d + 1) * TC]
                    dve.tensor_scalar(x, x, lb_om[:, bass.ds(h + d * HEADS, 1)], lb[:, bass.ds(h + d * HEADS, 1)],
                                      ALU.mult, ALU.add).then_inc(S("f"), 1)

            def values_and_mask(h, old):
                if old:
                    dve.wait_ge(S("o"), h)
                dve.wait_ge(S("scores"), h + 1)
                dve.tensor_copy(v_cur, v_all[:, bass.ds(h * 512, 512)]).then_inc(S("v_cur"), 1)
                for odd in range(2):
                    rows = slice(CH * odd, CH * odd + CH)
                    dst = sc_T.rearrange("p (n q t) -> p n q t", q=2, t=CH)[rows, :, odd, :]
                    dve.copy_predicated(dst, by_tile(msk[rows, :], 4), by_tile(psum[5][rows, 0:T], 4)).then_inc(S("masked"), 1)

            def states(h):
                dve.wait_ge(S("kv"), h + 1)
                for s in range(NCH):
                    for d in range(2):
                        dst = state[:, (4 * d + s) * P:(4 * d + s + 1) * P]
                        kv = kv_at(d, s)
                        if s == 0:
                            dve.tensor_copy(dst, kv).then_inc(S("state"), 1)
                            continue
                        c = s - 1 if d == 0 else NCH - s
                        end = d * T + c * CH + (CH - 1 if d == 0 else 0)
                        dve.wait_ge(S("state"), h * 8 + (2 * s + d - 1))
                        dve.scalar_tensor_tensor(dst, state[:, (4 * d + s - 1) * P:(4 * d + s) * P], e_qd[:, end:end + 1],
                                                 kv, ALU.mult, ALU.add).then_inc(S("state"), 1)

            def scan(h):
                dve.wait_ge(S("log_f"), h + 1)
                dve.tensor_tensor_scan(b_buf[:, 0:TC], scan_mask[0], f_buf[:, 0:TC], 0.0, ALU.mult, ALU.add).then_inc(S("scanned"), 1)
                dve.tensor_tensor_scan(b_buf[:, TC:2 * TC][:, ::-1], scan_mask[1], f_buf[:, TC:2 * TC][:, ::-1], 0.0,
                                       ALU.mult, ALU.add).then_inc(S("scanned"), 1)

            def head(h, u, at, prev, prev2):
                if prev:
                    silu_qg(h - 1, 1 - u)
                    scan(h - 1)
                    distances(h - 1)
                    scale_qk(h - 1, 1 - u)
                lo(dve, at(AHEAD))
                lo(dve, at(1 + AHEAD))
                if prev2:
                    out_gated(h - 2, u)
                forget(h)
                if prev:
                    values_and_mask(h - 1, prev2)
                if prev2:
                    out_lo(h - 2)
                lo(dve, at(2 + AHEAD))
                for g in range(LATE):
                    dve.wait_ge(S(f"late_in{g}"), h * 16 + 16)
                    if prev:
                        dve.wait_ge(S("late_summed"), h * LATE + (g + 1 - LATE))
                    mod_row(h, late_sum[g], late_raw[g], not prev).then_inc(S("late_summed"), 1)
                if prev:
                    states(h - 1)
                lo(dve, at(3 + AHEAD))

            head(0, 0, lambda m: Chunk(N_HEAD, m), False, False)
            dve.wait_ge(S("v_even"), 4)
            dve.wait_ge(S("small_in"), 32)
            dve.wait_ge(S("con_small_in"), 16)
            late = slice(ADA_FIRST, ADA_FIRST + GROUPS * KT)
            dve.wait_ge(S("mod_columns"), GROUPS)
            dve.tensor_tensor(mod[:, late], psum[7][:, 0:GROUPS * KT], p1("b_ada", ADA_FIRST, GROUPS * KT),
                              ALU.add).then_inc(S("mod_late"), 1)
            head(1, 1, lambda m: Chunk(N_HEAD, 4 + m), True, False)
            with dve.Fori(0, (HEADS - 2) // 2) as i:
                for u in range(2):
                    head(i * 2 + (2 + u), u, lambda m: Chunk(N_HEAD + 8, 4 * u + m, i, 8), True, True)
            silu_qg(HEADS - 1, 1)
            scan(HEADS - 1)
            distances(HEADS - 1)
            lo(dve, Chunk(N_HOUT, 2))
            scale_qk(HEADS - 1, 1)
            lo(dve, Chunk(N_HOUT, 3))
            out_gated(HEADS - 2, 0)
            lo(dve, Chunk(N_HOUT, 4))
            values_and_mask(HEADS - 1, True)
            dve.wait_ge(S("late_columns"), LATE)
            dve.tensor_tensor(mod[:, 4 * KT:ADA], psum[6][:, 0:LATE * KT], p1("b_ada", 4 * KT, LATE * KT),
                              ALU.add).then_inc(S("mod_all"), 1)
            dve.wait_ge(S("mod_all"), 1)
            dve.scalar_tensor_tensor(gain_2, mod[:, 4 * KT:5 * KT], 1.0, p1("norm2", 0, KT), ALU.add, ALU.mult)
            dve.tensor_tensor(final_pre, p1("final", 0, KT), p1("pre_mix", 0, KT), ALU.mult)
            dve.tensor_tensor(final_sq, p1("final", 0, KT), p1("final", 0, KT), ALU.mult).then_inc(S("final_weights"), 1)
            dve.wait_ge(S("final_weights"), 1)
            dve.tensor_scalar(final_sq, final_sq, EPS, None, ALU.add).then_inc(S("final_weights"), 1)
            lo(dve, Chunk(N_HOUT, 5))
            out_lo(HEADS - 2)
            lo(dve, Chunk(N_HOUT, 6))
            states(HEADS - 1)
            lo(dve, Chunk(N_HOUT, 7))
            out_gated(HEADS - 1, 1)
            lo(dve, Chunk(N_FFN))
            out_lo(HEADS - 1)
            lo(dve, Chunk(N_FFN, 1))
            dve.wait_ge(S("xres_in"), 16)
            add_product(dve, lambda m: mod[:, 2 * KT + m:2 * KT + m + 1], 0, N_FFN, HOUT_BANKS)
            dve.wait_ge(S("norm_rstd"), 1)
            norm_input(dve, 1, lambda m: gain_2[:, m:m + 1], lambda m: mod[:, 3 * KT + m:3 * KT + m + 1])

            def ffn_tile(t, p, s):
                for half in range(2):
                    z = psum[4 + 2 * half + p]
                    x = conv[p][half]
                    dve.wait_ge(S("conv_mid"), t * 2 + (1 + half))
                    dve.scalar_tensor_tensor(x[:, 1:T], z[:, 0:T - 1], p1("conv_w", t + half * JF), x[:, 1:T],
                                             ALU.mult, ALU.add).then_inc(S("conv_left"), 1)
                for half in range(2):
                    z = psum[4 + 2 * half + p]
                    x = conv[p][half]
                    dve.wait_ge(S("conv_left"), t * 2 + (1 + half))
                    dve.scalar_tensor_tensor(x[:, 0:T - 1], z[:, 1:T], p1("conv_w", t + (4 * JF + half * JF)), x[:, 0:T - 1],
                                             ALU.mult, ALU.add).then_inc(S("conv"), 1)
                dve.wait_ge(S("conv"), t * 2 + 2)
                dve.wait_ge(S("f_silu"), t + 1)
                dve.tensor_tensor(u_f[p], f_silu[p], conv[p][1], ALU.mult).then_inc(S("u_full"), 1)
                dve.wait_ge(S("u_hi"), t + 1)
                dve.tensor_tensor(y_lo[:, s * T:s * T + T], u_f[p], y_hi[:, s * T:s * T + T].bitcast(F32),
                                  ALU.subtract).then_inc(S("u_lo"), 1)

            for j in range(FFN_PEEL):
                c = ffn_first(j)
                lo(dve, Chunk(c, AHEAD))
                lo(dve, Chunk(c, 1 + AHEAD))
                if j >= 1:
                    ffn_tile(j - 1, (j - 1) % 2, (j - 1) % 4)
                if j >= 2:
                    lo(dve, Chunk(c, 2 + AHEAD))
            with dve.Fori(0, (JF - FFN_PEEL) // 4) as i:
                for u in range(4):
                    lo(dve, Chunk(ffn_first(FFN_PEEL), 3 * u + AHEAD, i, 12))
                    lo(dve, Chunk(ffn_first(FFN_PEEL), 3 * u + 1 + AHEAD, i, 12))
                    t = FFN_PEEL + u - 1
                    ffn_tile(i * 4 + t, t % 2, t % 4)
                    lo(dve, Chunk(ffn_first(FFN_PEEL), 3 * u + 2 + AHEAD, i, 12))
            ffn_tile(JF - 1, (JF - 1) % 2, (JF - 1) % 4)
            lo(dve, Chunk(N_IN2 - 2, AHEAD))
            lo(dve, Chunk(N_IN2 - 1, AHEAD))
            add_product(dve, lambda m: mod[:, 5 * KT + m:5 * KT + m + 1], 1, N_IN2, LOW_BANKS,
                        lambda m: add_weighted_squares(dve, m))
            add_weighted_squares(dve, KT - 2)
            add_weighted_squares(dve, KT - 1)
            dve.wait_ge(S("norm_rstd"), 3)
            norm_input(dve, 2, lambda m: final_pre[:, m:m + 1])

            def values2(t):
                v = v_index(t)
                dve.wait_ge(S("v2_turned"), v + 1)
                z = psum[V_BANK][:, 0:T]
                if v == 0:
                    dve.tensor_copy(s_v, z).then_inc(S("v2"), 1)
                else:
                    x = (v - 1) * P
                    dve.tensor_copy(split2(r_v)[:, :, x:x + P], split2(z)).then_inc(S("v2"), 1)

            def centre_values():
                x = r_v.rearrange("p (n e) -> p n e", e=R_DV)
                dve.wait_ge(S("v2"), 9)
                dve.tensor_reduce(v_mean, x, AX, ALU.add).then_inc(S("v_sum"), 1)
                dve.wait_ge(S("v_sum"), 1)
                dve.tensor_scalar(v_mean, v_mean, 1.0 / R_DV, None, ALU.mult).then_inc(S("v_mean"), 1)
                dve.wait_ge(S("v_mean"), 1)
                dve.tensor_tensor(x, x, v_mean.rearrange("p (n o) -> p n o", o=1).broadcast_to([P, 8, R_DV]),
                                  ALU.subtract).then_inc(S("v_centred"), 1)

            def silu(t):
                x = gate_dst(t)
                dve.wait_ge(S("g_sigmoid"), t - T_GR + 1)
                dve.tensor_tensor(x, psum[t % IN2_BANKS][:, 0:T], x, ALU.mult).then_inc(S("g_silu"), 1)

            def softmax_max(e):
                p = e % 2
                slope = 2.0 ** (-8.0 / S_HEADS * (e + 1))
                dve.wait_ge(S("s_scores"), e + 1)
                if e >= 2:
                    dve.wait_ge(S("s_exp"), 3 * (e - 1))
                dve.scalar_tensor_tensor(s_b[p], dist, -slope * S_DH ** 0.5, psum[5 + p][:, 0:3 * P], ALU.mult,
                                         ALU.add).then_inc(S("s_biased"), 1)
                dve.wait_ge(S("s_biased"), e + 1)
                dve.reduce_max(s_max[p][:, 0:1], s_b[p][:, 0:P], AX)
                dve.reduce_max(s_max[p][:, 1:2], s_b[p][:, P:3 * P], AX).then_inc(S("s_max"), 1)
                dve.wait_ge(S("s_max"), e + 1)
                dve.tensor_scalar(s_neg[p], s_max[p], -(S_DH ** -0.5), sink_neg[:, e:e + 1], ALU.mult,
                                  ALU.min).then_inc(S("s_neg"), 1)

            def softmax_norm(e):
                p = e % 2
                dve.wait_ge(S("s_exp"), 3 * e + 3)
                dve.tensor_tensor(s_den[p], s_sum[p], s_sink[p], ALU.add).then_inc(S("s_den"), 1)
                dve.wait_ge(S("s_den"), e + 1)
                dve.reciprocal(s_den[p], s_den[p]).then_inc(S("s_rden"), 1)
                dve.wait_ge(S("s_rden"), e + 1)
                for x, b in ((slice(0, P), 0), (slice(P, 3 * P), 1)):
                    dve.tensor_scalar(s_p[p][:, x], s_p[p][:, x], s_den[p][:, b:b + 1], None, ALU.mult).then_inc(S("p_norm"), 1)

            def swa_copy(e):
                q = S_DH * (e % 2)
                dve.wait_ge(S("pv"), e + 1)
                dve.tensor_copy(swa[q:q + S_DH, (e // 2) * T:(e // 2 + 1) * T], psum[4][q:q + S_DH, 0:T]).then_inc(S("swa"), 1)

            def ret_decay(r):
                dve.wait_ge(S("r_scores"), r + 1)
                if r >= 2:
                    dve.wait_ge(S("r_o"), r - 1)
                x = CON["decay"] + 3 * P * r
                dve.tensor_tensor(r_sc[r % 2], psum[5 + r % 2][:, 0:3 * P], con[:, x:x + 3 * P], ALU.mult).then_inc(S("r_sc"), 1)

            def ret_gate(r):
                dve.wait_ge(S("r_squares"), r + 1)
                x = slice(2 * r * T, 2 * (r + 1) * T)
                dve.wait_ge(S("g_silu"), 2 * r + 2)
                dve.tensor_tensor(r_t[:, x], psum[4][:, :], silu_g[:, x], ALU.mult).then_inc(S("r_gated"), 1)

            def ret_add(r):
                dve.wait_ge(S("r_squares"), r + 1)
                dve.tensor_tensor(r_sq[:, 0:T], r_sq[:, 0:T], r_sq[:, T:2 * T], ALU.add).then_inc(S("r_added"), 1)

            def ret_mean(r):
                dve.wait_ge(S("r_summed"), r + 1)
                dve.tensor_scalar(r_rs[:, r * T:r * T + T], psum[7][:, 0:T], 1.0 / R_DV, EPS, ALU.mult,
                                  ALU.add).then_inc(S("r_mean"), 1)

            def ret_norm(r):
                x = split2(r_t[:, 2 * r * T:2 * (r + 1) * T])
                dve.wait_ge(S("r_rstd"), 1)
                dve.wait_ge(S("r_gated"), r + 1)
                dve.tensor_tensor(x, x, over_tiles(r_rs[:, r * T:r * T + T], 2), ALU.mult).then_inc(S("r_full"), 1)

            def ret_lo(r):
                x = slice(2 * r * T, 2 * (r + 1) * T)
                dve.wait_ge(S("r_hi"), r + 1)
                dve.tensor_tensor(y_lo[:, x], r_t[:, x], y_hi[:, x].bitcast(F32), ALU.subtract).then_inc(S("r_lo"), 1)

            dve.tensor_scalar(sink_neg, sink[:, :], -1.0, None, ALU.mult).then_inc(S("sink_neg"), 1)
            dve.wait_ge(S("sink_neg"), 1)
            for t in range(TILES_IN2 + 1):
                if t < TILES_IN2:
                    lo(dve, Chunk(N_IN2, t + AHEAD))
                if t < KT:
                    scale_residual(dve, t)
                if t >= 2 and v_index(t - 2) is not None:
                    values2(t - 2)
                if t == T_GR + 2:
                    centre_values()
                if T_GR <= t - 1 < T_GS:
                    silu(t - 1)
                for after, step in ((1, softmax_max), (2, softmax_norm), (5, swa_copy)):
                    if swa_at(t, after) is not None:
                        step(swa_at(t, after))
                if swa_at(t, 7) == S_HEADS - 1:
                    dve.wait_ge(S("swa_hi"), 1)
                    dve.tensor_tensor(h_lo[:, 8 * T:12 * T], swa, h_hi[:, 8 * T:12 * T].bitcast(F32),
                                      ALU.subtract).then_inc(S("swa_lo"), 1)
                for after, step in ((1, ret_decay), (4, ret_add), (4, ret_gate), (5, ret_mean)):
                    if ret_at(t, after) is not None:
                        step(ret_at(t, after))
            lo(dve, Chunk(N_SOUT, AHEAD))
            ret_norm(0)
            for n in range(N_SOUT, N_MOUT):
                if n > N_SOUT:
                    lo(dve, Chunk(n, AHEAD))
                r = n - N_SOUT
                if r < R_HEADS:
                    if r + 1 < R_HEADS:
                        ret_norm(r + 1)
                    ret_lo(r)
                if n == N_ROUT:
                    dve.wait_ge(S("gate"), KT)
                    for b in range(4):
                        wait_bank(dve, 2, N_ROUT, b)
                        x = gate_s[:, b * 512:b * 512 + 512]
                        last = dve.tensor_tensor(x, psum[HIGH_BANKS[b]][:, :], x, ALU.mult)
                    last.then_inc(S("swa_gated"), 1)
            dve.wait_ge(S("swa_gated"), 1)
            dve.wait_ge(S("gate"), 2 * KT)
            for m in range(KT + 2):
                if m < KT:
                    if m % 2 == 0:
                        wait_bank(dve, 3, N_MOUT, m // 2)
                    x = gate_r[:, m * T:m * T + T]
                    dve.tensor_tensor(x, psum[m // 2][:, (m % 2) * T:(m % 2) * T + T], x, ALU.mult).then_inc(S("ret_gated"), 1)
                if 1 <= m <= KT:
                    x = gate_r[:, (m - 1) * T:m * T]
                    dve.wait_ge(S("ret_gated"), m)
                    dve.tensor_tensor(x, x, gate_s[:, (m - 1) * T:m * T], ALU.add).then_inc(S("mg_full"), 1)
                if m >= 2:
                    x = slice((m - 2) * T, (m - 1) * T)
                    dve.wait_ge(S("mg_hi"), m - 1)
                    dve.tensor_tensor(h_lo[:, x], gate_r[:, x], h_hi[:, x].bitcast(F32), ALU.subtract).then_inc(S("mg_lo"), 1)
                if 2 <= m < 6:
                    lo(dve, Chunk(N_MOUT, m - 2 + AHEAD))
            for n in range(N_MOUT + 4, N_MLP):
                lo(dve, Chunk(n, AHEAD))
            add_squares(dve, 3, 0)
            add_normed_product(dve, 3, 0, lambda m: p1("post_mix", m), HIGH_BANKS)
            dve.wait_ge(S("norm_rstd"), 5)
            norm_input(dve, 3, lambda m: p1("pre_mlp", m))

            def mlp_tile(t, p, s):
                dve.wait_ge(S("m_relu"), t + 1)
                dve.tensor_tensor(u_f[p], m_relu[p], m_relu[p], ALU.mult).then_inc(S("m_full"), 1)
                dve.wait_ge(S("m_hi"), t + 1)
                dve.tensor_tensor(y_lo[:, s * T:s * T + T], u_f[p], y_hi[:, s * T:s * T + T].bitcast(F32),
                                  ALU.subtract).then_inc(S("m_lo"), 1)

            for j in range(MLP_PEEL):
                lo(dve, Chunk(mlp_first(j), AHEAD))
                if j >= 1:
                    mlp_tile(j - 1, (j - 1) % 2, (j - 1) % 4)
                if j >= 2:
                    lo(dve, Chunk(mlp_first(j), 1 + AHEAD))
            with dve.Fori(0, (JM - MLP_PEEL) // 4 - 1) as i:
                for u in range(4):
                    lo(dve, Chunk(mlp_first(MLP_PEEL), 2 * u + AHEAD, i, 8))
                    t = MLP_PEEL + u - 1
                    mlp_tile(i * 4 + t, t % 2, t % 4)
                    lo(dve, Chunk(mlp_first(MLP_PEEL), 2 * u + 1 + AHEAD, i, 8))
            for j in range(JM - 4, JM):
                lo(dve, Chunk(mlp_first(j), AHEAD))
                mlp_tile(j - 1, (j - 1) % 2, (j - 1) % 4)
                lo(dve, Chunk(mlp_first(j), 1 + AHEAD))
            mlp_tile(JM - 1, (JM - 1) % 2, (JM - 1) % 4)
            add_squares(dve, 5, 1)
            add_normed_product(dve, 5, 1, lambda m: p1("post_mlp", m), LOW_BANKS)


def _columns(w):
    n = w.shape[1]
    return w.reshape(KT, P, n // P, P).transpose(2, 1, 0, 3).reshape(n // P, P, D)


def _rows(w):
    return w.reshape(-1, P, D)


def _quarter(w, half):
    return w[:, :, half * 512:half * 512 + 512].reshape(4, 2, P, 512).transpose(0, 2, 1, 3).reshape(4, P, D)


def _vec(v):
    return v.reshape(-1, P).T


def _tiles(x):
    return x.T.reshape(KT, P, -1).transpose(1, 0, 2)


def kernel(**inputs):
    import concourse.bacc as bacc
    from concourse.bass_utils import run_bass_kernel_spmd as run

    a = {k: np.asarray(v) for k, v in inputs.items()}
    x, ctx = _tiles(a["x"][0]), _tiles(a["ctx"][0])
    tok = np.concatenate([x, ctx], axis=2).reshape(P, KT * TC)
    cc = np.stack([_vec(a["c"][0]), _vec(a["c_ctx"])], axis=2).reshape(P, 2 * KT)
    w = a["w_ada"][0].reshape(KT, P, 6, D)
    ada = np.concatenate([w[:, :, g:g + 2].transpose(0, 2, 1, 3).reshape(2 * KT, P, D) for g in (2, 4)])

    hg = _columns(a["hg_w_in"][0]).reshape(5, HEADS, P, D)
    v = _rows(a["hg_w_in"][0][:, 3 * D:4 * D])
    v = np.concatenate([_quarter(v, 0), _quarter(v, 1)])
    heads = np.stack([hg[1], hg[2], hg[0], hg[4]], axis=1).reshape(4 * HEADS, P, D)
    up = _columns(a["ffn_w_up"][0]).reshape(2, JF, P, D)
    down = _rows(a["ffn_w_down"][0])
    ffn = []
    for j in range(JF + 2):
        ffn += [up[0, j], up[1, j]] if j < JF else []
        ffn += [down[j - 2]] if j >= 2 else []
    w2 = a["w_in_2"][0]
    edges = np.cumsum([0, 512, 512, 1024, 1024, 512, 128, 128, D, D])
    r_q, r_k, r_v, r_g, s_q, s_k, s_v, g_r, g_s = (w2[:, i:j] for i, j in zip(edges[:-1], edges[1:]))
    s_q = s_q.reshape(D, 2, 4, S_DH).transpose(0, 2, 1, 3).reshape(D, 512)
    in2 = _columns(np.concatenate([s_q, s_k, s_v, r_q, r_k, r_v, r_g, g_s, g_r], axis=1))
    up2, down2 = _columns(a["w_up_2"][0]), _rows(a["w_down_2"][0])
    mlp = []
    for j in range(JM + 2):
        mlp += [up2[j]] if j < JM else []
        mlp += [down2[j - 2]] if j >= 2 else []
    first = np.concatenate([_quarter(w[:, :, which], half) for half in range(2) for which in (1, 0)])
    stream = np.concatenate([first[:V_FIRST], v[:1], first[V_FIRST:], v[1:], heads, _rows(a["hg_w_out"][0]), np.stack(ffn), in2,
                             _rows(a["w_swa_out_2"][0]), _rows(a["w_ret_out_2"][0]), _rows(a["w_out_2"][0]), np.stack(mlp)])
    lb = a["hg_lb_logits"]
    par = np.concatenate([_vec(v) for v in (
        a["norm_g"][0, 0], a["norm_g"][0, 1], a["b_ada"][0], lb[0], lb[1], a["hg_gnorm"][0], a["ffn_conv_w"][0],
        a["ffn_conv_b"][0], a["final_g"], a["pre_mix_norm_2"][0], a["post_mix_norm_2"][0], a["pre_mlp_norm_2"][0],
        a["post_mlp_norm_2"][0])], axis=1)
    con, msk = constants()
    arrays = {"tok": tok, "cc": cc, "ada": ada.reshape((ADA - ADA_FIRST) * P, D), "stream": stream.reshape(N_ALL * P, D), "par": par,
              "con": con, "msk": msk, "sink": a["sinks_2"][0]}
    arrays = {"in_" + k: np.ascontiguousarray(v) for k, v in arrays.items()}

    nc = bacc.Bacc("TRN2", target_bir_lowering=False, num_devices=1)
    args = [nc.dram_tensor(k, v.shape, mybir.dt.from_np(v.dtype), kind="ExternalInput").ap() for k, v in arrays.items()]
    args.append(nc.dram_tensor("out", (P, KT * T), F32, kind="ExternalOutput").ap())
    build(nc, *args)
    y = run(nc, [arrays], core_ids=[0]).results[0]["out"]
    return np.ascontiguousarray(y.reshape(P, KT, T).transpose(2, 1, 0).reshape(1, T, D))
```
